# Optimizing a Trainium2 kernel written in Bass

```python
import math
import jax, jax.numpy as jnp
from jax import lax
import numpy as np

D_MODEL = 1024
BATCH = 1
SEQ = 256
DEPTH = 1

HEAD_DIM = 64
N_HEADS_A = 8
N_KV_A = 2
GQA_GROUP = N_HEADS_A // N_KV_A
N_HEADS_B = 8
WIDTH_A = N_HEADS_A * HEAD_DIM
WIDTH_B = N_HEADS_B * HEAD_DIM
KV_WIDTH_A = N_KV_A * HEAD_DIM
IN_WIDTH = WIDTH_A + 2 * KV_WIDTH_A + 3 * WIDTH_B
D_FF = 2816
CONV_WIDTH = 3
GRID_W = 64
ROPE_THETA = 10000.0
ROPE_AXIS_DIM = HEAD_DIM // 2
Q_BLOCK = 128
DIL_BLOCK = 64
DILATED_PATTERNS = ((128, 1), (512, 4), (2048, 16))
NORM_EPS = 1e-6
NEG_INF = -1e30


def rms_norm(x, g):
    xf = x.astype(jnp.float32)
    y = xf * lax.rsqrt(jnp.mean(xf * xf, axis=-1, keepdims=True) + NORM_EPS)
    return (y * g.astype(jnp.float32)).astype(x.dtype)

def axial_rope_tables(seq_len):
    rows = seq_len // GRID_W
    row = jnp.repeat(jnp.arange(rows, dtype=jnp.float32), GRID_W)
    col = jnp.tile(jnp.arange(GRID_W, dtype=jnp.float32), rows)
    inv = ROPE_THETA ** (-jnp.arange(0, ROPE_AXIS_DIM, 2, dtype=jnp.float32) / ROPE_AXIS_DIM)
    ang_r = row[:, None] * inv[None, :]
    ang_c = col[:, None] * inv[None, :]
    return jnp.cos(ang_r), jnp.sin(ang_r), jnp.cos(ang_c), jnp.sin(ang_c)

def _rotate(u, c, s):
    half = u.shape[-1] // 2
    u1, u2 = u[..., :half], u[..., half:]
    c = c[:, None, :]
    s = s[:, None, :]
    return jnp.concatenate([u1 * c - u2 * s, u2 * c + u1 * s], axis=-1)

def apply_axial_rope(x, tables):
    cos_r, sin_r, cos_c, sin_c = tables
    xf = x.astype(jnp.float32)
    out = jnp.concatenate([_rotate(xf[..., :ROPE_AXIS_DIM], cos_r, sin_r),
                           _rotate(xf[..., ROPE_AXIS_DIM:], cos_c, sin_c)], axis=-1)
    return out.astype(x.dtype)

def global_gqa_attention(q, k, v):
    b, s = q.shape[0], q.shape[1]
    nb = s // Q_BLOCK
    qg = q.reshape(b, nb, Q_BLOCK, N_KV_A, GQA_GROUP, HEAD_DIM).transpose(1, 0, 2, 3, 4, 5)
    scale = HEAD_DIM ** -0.5

    def block(qb):
        sc = jnp.einsum('bqkgd,bskd->bkgqs', qb, k, preferred_element_type=jnp.float32) * scale
        p = jax.nn.softmax(sc, axis=-1)
        return jnp.einsum('bkgqs,bskd->bqkgd', p.astype(v.dtype), v)

    o = lax.map(block, qg)
    return o.transpose(1, 0, 2, 3, 4, 5).reshape(b, s, WIDTH_A)

def alibi_slopes(n_heads):
    return 2.0 ** (-8.0 * jnp.arange(1, n_heads + 1, dtype=jnp.float32) / n_heads)

def dilated_window_attention(q, k, v, window, dilation, slopes):
    b, s, h, hd = q.shape
    d = dilation
    n_side = (window // 2) // d
    L = s // d
    nb = -(-L // DIL_BLOCK)
    Lp = nb * DIL_BLOCK

    def strided(a):
        return a.reshape(b, L, d, h, hd).transpose(0, 2, 1, 3, 4)

    qs = jnp.pad(strided(q), ((0, 0), (0, 0), (0, Lp - L), (0, 0), (0, 0)))
    qb = qs.reshape(b, d, nb, DIL_BLOCK, h, hd)

    def banded(a):
        ap = jnp.pad(strided(a), ((0, 0), (0, 0), (DIL_BLOCK, Lp - L + DIL_BLOCK), (0, 0), (0, 0)))
        ap = ap.reshape(b, d, nb + 2, DIL_BLOCK, h, hd)
        return jnp.concatenate([ap[:, :, :-2], ap[:, :, 1:-1], ap[:, :, 2:]], axis=3)

    kw = banded(k)
    vw = banded(v)

    qi = jnp.arange(DIL_BLOCK)[:, None]
    kj = jnp.arange(3 * DIL_BLOCK)[None, :]
    off = kj - DIL_BLOCK - qi
    key_idx = jnp.arange(nb)[:, None, None] * DIL_BLOCK - DIL_BLOCK + kj[None]
    valid = (jnp.abs(off) <= n_side)[None] & (key_idx >= 0) & (key_idx < L)
    dist = (jnp.abs(off) * d).astype(jnp.float32)
    bias = jnp.where(valid[:, None], -slopes[None, :, None, None] * dist[None, None],
                     NEG_INF)

    sc = jnp.einsum('brnqhd,brnkhd->brnhqk', qb, kw, preferred_element_type=jnp.float32)
    sc = sc * (hd ** -0.5) + bias[None, None]
    lse = jax.nn.logsumexp(sc, axis=-1)
    p = jnp.exp(sc - lse[..., None])
    o = jnp.einsum('brnhqk,brnkhd->brnqhd', p.astype(v.dtype), vw)

    o = o.reshape(b, d, Lp, h, hd)[:, :, :L].transpose(0, 2, 1, 3, 4).reshape(b, s, h, hd)
    lse = lse.transpose(0, 1, 2, 4, 3).reshape(b, d, Lp, h)[:, :, :L]
    lse = lse.transpose(0, 2, 1, 3).reshape(b, s, h)
    return o, lse

def dilated_mixture_attention(q, k, v):
    slopes = alibi_slopes(N_HEADS_B)
    outs, lses = [], []
    for window, dilation in DILATED_PATTERNS:
        o, lse = dilated_window_attention(q, k, v, window, dilation, slopes)
        outs.append(o)
        lses.append(lse)
    w = jax.nn.softmax(jnp.stack(lses, axis=0), axis=0)
    o = jnp.sum(w[..., None].astype(q.dtype) * jnp.stack(outs, axis=0), axis=0)
    return o.reshape(q.shape[0], q.shape[1], WIDTH_B)

def conv_ffn(h, w_up, conv_w, conv_b, w_down):
    u = h @ w_up
    c = u.shape[-1]
    u = lax.conv_general_dilated(u, conv_w[:, None, :].astype(u.dtype), window_strides=(1,),
                                 padding=((CONV_WIDTH // 2, CONV_WIDTH // 2),),
                                 dimension_numbers=('NWC', 'WIO', 'NWC'),
                                 feature_group_count=c) + conv_b
    gate, val = u[..., :D_FF], u[..., D_FF:]
    return (jax.nn.gelu(gate) * val) @ w_down

def first_inputs(seed: int = 0) -> dict:
    key = jax.random.key(seed)
    ks = jax.random.split(key, 16)
    f32 = jnp.float32

    def gain(k, n):
        return 1.0 + 0.05 * jax.random.normal(k, (n,), f32)

    return {
        "x": jax.random.normal(ks[0], (BATCH, SEQ, D_MODEL), f32),
        "norm1_g": gain(ks[1], D_MODEL),
        "w_in": jax.random.normal(ks[2], (D_MODEL, IN_WIDTH), f32) * D_MODEL ** -0.5,
        "qa_norm_g": gain(ks[3], HEAD_DIM),
        "ka_norm_g": gain(ks[4], HEAD_DIM),
        "qb_norm_g": gain(ks[5], HEAD_DIM),
        "kb_norm_g": gain(ks[6], HEAD_DIM),
        "outa_norm_g": gain(ks[7], WIDTH_A),
        "outb_norm_g": gain(ks[8], WIDTH_B),
        "w_out": jax.random.normal(ks[9], (WIDTH_A + WIDTH_B, D_MODEL), f32) * (WIDTH_A + WIDTH_B) ** -0.5,
        "norm2_g": gain(ks[10], D_MODEL),
        "w_up": jax.random.normal(ks[11], (D_MODEL, 2 * D_FF), f32) * D_MODEL ** -0.5,
        "conv_w": jax.random.normal(ks[12], (CONV_WIDTH, 2 * D_FF), f32) * CONV_WIDTH ** -0.5,
        "conv_b": 0.02 * jax.random.normal(ks[13], (2 * D_FF,), f32),
        "w_down": jax.random.normal(ks[14], (D_FF, D_MODEL), f32) * D_FF ** -0.5,
    }

def first_block(x, norm1_g, w_in, qa_norm_g, ka_norm_g, qb_norm_g, kb_norm_g,
              outa_norm_g, outb_norm_g, w_out, norm2_g, w_up, conv_w, conv_b, w_down):
    b, s, _ = x.shape
    tables = axial_rope_tables(s)
    for _layer in range(DEPTH):
        hn = rms_norm(x, norm1_g)
        proj = hn @ w_in
        o1 = WIDTH_A
        o2 = o1 + KV_WIDTH_A
        o3 = o2 + KV_WIDTH_A
        o4 = o3 + WIDTH_B
        o5 = o4 + WIDTH_B
        qa = proj[..., :o1].reshape(b, s, N_HEADS_A, HEAD_DIM)
        ka = proj[..., o1:o2].reshape(b, s, N_KV_A, HEAD_DIM)
        va = proj[..., o2:o3].reshape(b, s, N_KV_A, HEAD_DIM)
        qb = proj[..., o3:o4].reshape(b, s, N_HEADS_B, HEAD_DIM)
        kb = proj[..., o4:o5].reshape(b, s, N_HEADS_B, HEAD_DIM)
        vb = proj[..., o5:].reshape(b, s, N_HEADS_B, HEAD_DIM)

        qa = apply_axial_rope(rms_norm(qa, qa_norm_g), tables)
        ka = apply_axial_rope(rms_norm(ka, ka_norm_g), tables)
        out_a = global_gqa_attention(qa, ka, va)

        out_b = dilated_mixture_attention(rms_norm(qb, qb_norm_g), rms_norm(kb, kb_norm_g), vb)

        mixed = jnp.concatenate([rms_norm(out_a, outa_norm_g), rms_norm(out_b, outb_norm_g)], axis=-1)
        x = x + mixed @ w_out

        x = x + conv_ffn(rms_norm(x, norm2_g), w_up, conv_w, conv_b, w_down)
    return x


DEPTH_2 = 2

CTX_LEN = 256

ATT_HEADS = 8
ATT_HEAD_DIM = 64
ATT_QK_DIM = ATT_HEADS * 2 * ATT_HEAD_DIM
ATT_V_DIM = ATT_HEADS * 2 * ATT_HEAD_DIM
ROPE_BASE = 10000.0
ROPE_PAIRS = ATT_HEAD_DIM // 4

SSD_D_INNER = 2 * D_MODEL
SSD_HEAD_DIM = 64
SSD_HEADS = SSD_D_INNER // SSD_HEAD_DIM
SSD_GROUPS = 8
SSD_STATE = 128
SSD_CONV = 5
SSD_CHUNK = 128
SSD_CONV_DIM = SSD_D_INNER + 2 * SSD_GROUPS * SSD_STATE

D_FF_2 = 4 * D_MODEL

N_BRANCH = 2
N_MOD = 6
IN_DIM = 2 * ATT_QK_DIM + ATT_V_DIM + SSD_D_INNER + SSD_CONV_DIM + 2 * SSD_HEADS + N_BRANCH * D_MODEL


def rmsnorm(x, g, eps=1e-6):
    xf = x.astype(jnp.float32)
    y = xf * lax.rsqrt(jnp.mean(xf * xf, axis=-1, keepdims=True) + eps)
    return (y * g.astype(jnp.float32)).astype(x.dtype)

def modulate(x, g, shift, scale):
    return rmsnorm(x, g) * (1 + scale) + shift

def in_proj_split(t):
    sizes = (ATT_QK_DIM, ATT_QK_DIM, ATT_V_DIM, SSD_D_INNER, SSD_CONV_DIM,
             SSD_HEADS, SSD_HEADS, D_MODEL, D_MODEL)
    idx, acc = [], 0
    for s in sizes[:-1]:
        acc += s
        idx.append(acc)
    return jnp.split(t, idx, axis=-1)

def axial_rope(n_tok):
    rows = n_tok // GRID_W
    row = jnp.broadcast_to(jnp.arange(rows)[:, None], (rows, GRID_W)).reshape(-1).astype(jnp.float32)
    col = jnp.broadcast_to(jnp.arange(GRID_W)[None, :], (rows, GRID_W)).reshape(-1).astype(jnp.float32)
    inv = jnp.float32(ROPE_BASE) ** (-jnp.arange(ROPE_PAIRS, dtype=jnp.float32) / ROPE_PAIRS)
    ang = jnp.concatenate([row[:, None] * inv, col[:, None] * inv], axis=-1)
    return jnp.cos(ang), jnp.sin(ang)

def apply_rope(x, cos, sin):
    half = x.shape[-1] // 2
    x1 = x[..., :half].astype(jnp.float32)
    x2 = x[..., half:].astype(jnp.float32)
    c = cos[:, None, None, :]
    s = sin[:, None, None, :]
    return jnp.concatenate([x1 * c - x2 * s, x1 * s + x2 * c], axis=-1).astype(x.dtype)

def diff_attend(q, k, v, lam):
    s = jnp.einsum('bqhcd,bkhcd->bchqk', q, k).astype(jnp.float32) * (ATT_HEAD_DIM ** -0.5)
    p = jax.nn.softmax(s, axis=-1)
    a = p[:, 0] - lam * p[:, 1]
    return jnp.einsum('bhqk,bkhe->bqhe', a.astype(v.dtype), v)

def diff_attention(q_l, k_l, v_l, q_c, k_c, v_c, lam, lam_init, subln_g, with_ctx_out):
    b, n, h = q_l.shape[:3]
    k_all = jnp.concatenate([k_l, k_c], axis=1)
    v_all = jnp.concatenate([v_l, v_c], axis=1)
    nb = n // Q_BLOCK
    qb = jnp.moveaxis(q_l.reshape(b, nb, Q_BLOCK, h, 2, ATT_HEAD_DIM), 1, 0)
    o_l = lax.map(lambda qq: diff_attend(qq, k_all, v_all, lam), qb)
    o_l = jnp.moveaxis(o_l, 0, 1).reshape(b, n, h, 2 * ATT_HEAD_DIM)

    def post(o):
        return (rmsnorm(o, subln_g) * (1.0 - lam_init)).reshape(o.shape[0], o.shape[1], ATT_V_DIM)

    o_c = post(diff_attend(q_c, k_c, v_c, lam)) if with_ctx_out else None
    return post(o_l), o_c

def dwconv_silu(x, w, bias):
    kw = w.shape[0]
    y = lax.conv_general_dilated(x, w.astype(x.dtype)[:, None, :], window_strides=(1,),
                                 padding=[(kw // 2, kw // 2)],
                                 dimension_numbers=('NWC', 'WIO', 'NWC'),
                                 feature_group_count=x.shape[-1])
    return jax.nn.silu(y + bias)

def ssd_chunked(x, dt, a, bm, cm, h0, need_y):
    f32 = jnp.float32
    out_dtype = x.dtype
    b, n, h, p = x.shape
    g, ns = bm.shape[2], bm.shape[3]
    r = h // g
    nc = n // SSD_CHUNK
    dt = dt.astype(f32)
    xc = (x.astype(f32) * dt[..., None]).reshape(b, nc, SSD_CHUNK, g, r, p)
    cs = jnp.cumsum((dt * a.astype(f32)).reshape(b, nc, SSD_CHUNK, g, r), axis=2)
    bc = bm.astype(f32).reshape(b, nc, SSD_CHUNK, g, ns)
    cc = cm.astype(f32).reshape(b, nc, SSD_CHUNK, g, ns)
    decay_to_end = jnp.exp(cs[:, :, -1:] - cs)
    chunk_states = jnp.einsum('bclgn,bclgr,bclgrp->bcgrpn', bc, decay_to_end, xc)
    chunk_decay = jnp.exp(cs[:, :, -1])

    def step(hc, inp):
        st, dec = inp
        return hc * dec[..., None, None] + st, hc

    h_last, h_in = lax.scan(step, h0.astype(f32),
                            (jnp.moveaxis(chunk_states, 1, 0), jnp.moveaxis(chunk_decay, 1, 0)))
    if not need_y:
        return None, h_last
    h_in = jnp.moveaxis(h_in, 0, 1)
    seg = cs[:, :, :, None] - cs[:, :, None, :]
    lower = jnp.tril(jnp.ones((SSD_CHUNK, SSD_CHUNK), dtype=bool))[:, :, None, None]
    lmat = jnp.exp(jnp.where(lower, seg, -jnp.inf))
    cb = jnp.einsum('bclgn,bcsgn->bclsg', cc, bc)
    y = (jnp.einsum('bclsg,bclsgr,bcsgrp->bclgrp', cb, lmat, xc)
         + jnp.einsum('bclgn,bcgrpn,bclgr->bclgrp', cc, h_in, jnp.exp(cs)))
    return y.reshape(b, n, h, p).astype(out_dtype), h_last

def ssd_inputs(xbc_raw, dtf_raw, dtb_raw, conv_w, conv_b, dt_bias_f, dt_bias_b):
    xbc = dwconv_silu(xbc_raw, conv_w, conv_b)
    xs, bm, cm = jnp.split(xbc, [SSD_D_INNER, SSD_D_INNER + SSD_GROUPS * SSD_STATE], axis=-1)
    b, n = xs.shape[:2]
    xs = xs.reshape(b, n, SSD_HEADS, SSD_HEAD_DIM)
    bm = bm.reshape(b, n, SSD_GROUPS, SSD_STATE)
    cm = cm.reshape(b, n, SSD_GROUPS, SSD_STATE)
    dt_f = jax.nn.softplus((dtf_raw + dt_bias_f).astype(jnp.float32))
    dt_b = jax.nn.softplus((dtb_raw + dt_bias_b).astype(jnp.float32))
    return xs, bm, cm, dt_f, dt_b

def ssd_output(yf, yb, xs, z, ssd_d, ssd_norm_g, w_ssd_o):
    b, n = xs.shape[:2]
    y = (yf + yb + ssd_d[:, None] * xs).reshape(b, n, SSD_D_INNER)
    return rmsnorm(y * jax.nn.silu(z), ssd_norm_g) @ w_ssd_o

def hybrid_mixer(h_l, h_c, cos, sin, w_in, conv_w, conv_b, dt_bias_f, dt_bias_b, a_log_f, a_log_b,
                 ssd_d, ssd_norm_g, lam, lam_init, subln_g, w_attn_o, w_ssd_o, w_out, with_ctx_out):
    ql, kl, vl, zl, xbcl, dtfl, dtbl, gal, gsl = in_proj_split(h_l @ w_in)
    qc, kc, vc, zc, xbcc, dtfc, dtbc, gac, gsc = in_proj_split(h_c @ w_in)

    def qk(t):
        return t.reshape(t.shape[0], t.shape[1], ATT_HEADS, 2, ATT_HEAD_DIM)

    def vv(t):
        return t.reshape(t.shape[0], t.shape[1], ATT_HEADS, 2 * ATT_HEAD_DIM)

    att_l, att_c = diff_attention(apply_rope(qk(ql), cos, sin), apply_rope(qk(kl), cos, sin), vv(vl),
                                  qk(qc), qk(kc), vv(vc), lam, lam_init, subln_g, with_ctx_out)

    a_f = -jnp.exp(a_log_f.astype(jnp.float32))
    a_b = -jnp.exp(a_log_b.astype(jnp.float32))
    rev = lambda t: jnp.flip(t, axis=1)
    xs_c, bm_c, cm_c, dtf_c, dtb_c = ssd_inputs(xbcc, dtfc, dtbc, conv_w, conv_b, dt_bias_f, dt_bias_b)
    xs_l, bm_l, cm_l, dtf_l, dtb_l = ssd_inputs(xbcl, dtfl, dtbl, conv_w, conv_b, dt_bias_f, dt_bias_b)
    b = h_l.shape[0]
    h0 = jnp.zeros((b, SSD_GROUPS, SSD_HEADS // SSD_GROUPS, SSD_HEAD_DIM, SSD_STATE), jnp.float32)
    yc_f, st_f = ssd_chunked(xs_c, dtf_c, a_f, bm_c, cm_c, h0, with_ctx_out)
    yc_b, st_b = ssd_chunked(rev(xs_c), rev(dtb_c), a_b, rev(bm_c), rev(cm_c), h0, with_ctx_out)
    yl_f, _ = ssd_chunked(xs_l, dtf_l, a_f, bm_l, cm_l, st_f, True)
    yl_b, _ = ssd_chunked(rev(xs_l), rev(dtb_l), a_b, rev(bm_l), rev(cm_l), st_b, True)
    ssd_l = ssd_output(yl_f, rev(yl_b), xs_l, zl, ssd_d, ssd_norm_g, w_ssd_o)

    def merge(att, ssd, ga, gs):
        return (jax.nn.sigmoid(ga) * (att @ w_attn_o) + jax.nn.sigmoid(gs) * ssd) @ w_out

    o_l = merge(att_l, ssd_l, gal, gsl)
    o_c = None
    if with_ctx_out:
        ssd_c = ssd_output(yc_f, rev(yc_b), xs_c, zc, ssd_d, ssd_norm_g, w_ssd_o)
        o_c = merge(att_c, ssd_c, gac, gsc)
    return o_l, o_c

def sq_relu_mlp(h, w1, w2):
    return jnp.square(jax.nn.relu(h @ w1)) @ w2

def second_inputs(seed: int = 0) -> dict:
    key = jax.random.key(seed)
    ks = jax.random.split(key, 32)
    f32 = jnp.float32

    def nrm(k, shape, scale):
        return jax.random.normal(k, shape, f32) * scale

    def gain(k, shape):
        return 1.0 + 0.05 * jax.random.normal(k, shape, f32)

    dt = jnp.exp(jax.random.uniform(ks[10], (DEPTH_2, 2, SSD_HEADS), f32,
                                    math.log(1e-3), math.log(1e-1)))
    dt_bias = dt + jnp.log(-jnp.expm1(-dt))
    a_log = jnp.log(jax.random.uniform(ks[11], (DEPTH_2, 2, SSD_HEADS), f32, 1.0, 16.0))
    return {
        'x': nrm(ks[0], (BATCH, SEQ, D_MODEL), 1.0),
        'c': nrm(ks[1], (BATCH, D_MODEL), 1.0),
        'ctx': nrm(ks[2], (BATCH, CTX_LEN, D_MODEL), 1.0),
        'c_ctx': nrm(ks[3], (D_MODEL,), 1.0),
        'ada_w': nrm(ks[4], (DEPTH_2, D_MODEL, N_MOD * D_MODEL), 0.5 * D_MODEL ** -0.5),
        'ada_b': nrm(ks[5], (DEPTH_2, N_MOD * D_MODEL), 0.02),
        'norm_mix_g': gain(ks[6], (DEPTH_2, D_MODEL)),
        'w_in': nrm(ks[7], (DEPTH_2, D_MODEL, IN_DIM), D_MODEL ** -0.5),
        'conv_w': nrm(ks[8], (DEPTH_2, SSD_CONV, SSD_CONV_DIM), SSD_CONV ** -0.5),
        'conv_b': nrm(ks[9], (DEPTH_2, SSD_CONV_DIM), 0.02),
        'dt_bias_f': dt_bias[:, 0],
        'dt_bias_b': dt_bias[:, 1],
        'a_log_f': a_log[:, 0],
        'a_log_b': a_log[:, 1],
        'ssd_d': gain(ks[12], (DEPTH_2, SSD_HEADS)),
        'ssd_norm_g': gain(ks[13], (DEPTH_2, SSD_D_INNER)),
        'lambda_q1': nrm(ks[14], (DEPTH_2, ATT_HEAD_DIM), 0.1),
        'lambda_k1': nrm(ks[15], (DEPTH_2, ATT_HEAD_DIM), 0.1),
        'lambda_q2': nrm(ks[16], (DEPTH_2, ATT_HEAD_DIM), 0.1),
        'lambda_k2': nrm(ks[17], (DEPTH_2, ATT_HEAD_DIM), 0.1),
        'attn_subln_g': gain(ks[18], (DEPTH_2, 2 * ATT_HEAD_DIM)),
        'w_attn_o': nrm(ks[19], (DEPTH_2, ATT_V_DIM, D_MODEL), ATT_V_DIM ** -0.5),
        'w_ssd_o': nrm(ks[20], (DEPTH_2, SSD_D_INNER, D_MODEL), SSD_D_INNER ** -0.5),
        'w_out': nrm(ks[21], (DEPTH_2, D_MODEL, D_MODEL), D_MODEL ** -0.5),
        'norm_mlp_g': gain(ks[22], (DEPTH_2, D_MODEL)),
        'w_mlp1': nrm(ks[23], (DEPTH_2, D_MODEL, D_FF_2), D_MODEL ** -0.5),
        'w_mlp2': nrm(ks[24], (DEPTH_2, D_FF_2, D_MODEL), D_FF_2 ** -0.5),
        'final_norm_g': gain(ks[25], (D_MODEL,)),
    }

def second_block(x, c, ctx, c_ctx, ada_w, ada_b, norm_mix_g, w_in, conv_w, conv_b, dt_bias_f, dt_bias_b,
              a_log_f, a_log_b, ssd_d, ssd_norm_g, lambda_q1, lambda_k1, lambda_q2, lambda_k2,
              attn_subln_g, w_attn_o, w_ssd_o, w_out, norm_mlp_g, w_mlp1, w_mlp2, final_norm_g):
    n_lat = x.shape[1]
    cos, sin = axial_rope(n_lat)
    c_act = jax.nn.silu(c)
    cc_act = jax.nn.silu(c_ctx)
    xl, xc = x, ctx
    for l in range(DEPTH_2):
        last = l == DEPTH_2 - 1
        mod_l = [m[:, None, :] for m in jnp.split(c_act @ ada_w[l] + ada_b[l], N_MOD, axis=-1)]
        mod_c = jnp.split(cc_act @ ada_w[l] + ada_b[l], N_MOD, axis=-1)
        lam_init = 0.8 - 0.6 * math.exp(-0.3 * l)
        lam = (jnp.exp(jnp.sum(lambda_q1[l].astype(jnp.float32) * lambda_k1[l].astype(jnp.float32)))
               - jnp.exp(jnp.sum(lambda_q2[l].astype(jnp.float32) * lambda_k2[l].astype(jnp.float32)))
               + lam_init)
        h_l = modulate(xl, norm_mix_g[l], mod_l[0], mod_l[1])
        h_c = modulate(xc, norm_mix_g[l], mod_c[0], mod_c[1])
        o_l, o_c = hybrid_mixer(h_l, h_c, cos, sin, w_in[l], conv_w[l], conv_b[l], dt_bias_f[l], dt_bias_b[l],
                                a_log_f[l], a_log_b[l], ssd_d[l], ssd_norm_g[l], lam, lam_init,
                                attn_subln_g[l], w_attn_o[l], w_ssd_o[l], w_out[l], not last)
        xl = xl + mod_l[2] * o_l
        xl = xl + mod_l[5] * sq_relu_mlp(modulate(xl, norm_mlp_g[l], mod_l[3], mod_l[4]), w_mlp1[l], w_mlp2[l])
        if not last:
            xc = xc + mod_c[2] * o_c
            xc = xc + mod_c[5] * sq_relu_mlp(modulate(xc, norm_mlp_g[l], mod_c[3], mod_c[4]), w_mlp1[l], w_mlp2[l])
    return rmsnorm(xl, final_norm_g)


def setup_inputs(seed=0):
    out = dict(first_inputs(seed))
    for name, value in second_inputs(seed + 1).items():
        if name != "x":
            out[name + "_2"] = value
    return out


def reference(
    x, norm1_g, w_in, qa_norm_g, ka_norm_g, qb_norm_g, kb_norm_g, outa_norm_g, outb_norm_g,
    w_out, norm2_g, w_up, conv_w, conv_b, w_down, c_2, ctx_2, c_ctx_2, ada_w_2, ada_b_2,
    norm_mix_g_2, w_in_2, conv_w_2, conv_b_2, dt_bias_f_2, dt_bias_b_2, a_log_f_2, a_log_b_2,
    ssd_d_2, ssd_norm_g_2, lambda_q1_2, lambda_k1_2, lambda_q2_2, lambda_k2_2, attn_subln_g_2,
    w_attn_o_2, w_ssd_o_2, w_out_2, norm_mlp_g_2, w_mlp1_2, w_mlp2_2, final_norm_g_2,
):
    x = first_block(
        x, norm1_g, w_in, qa_norm_g, ka_norm_g, qb_norm_g, kb_norm_g, outa_norm_g, outb_norm_g,
        w_out, norm2_g, w_up, conv_w, conv_b, w_down,
    )
    return second_block(
        x, c_2, ctx_2, c_ctx_2, ada_w_2, ada_b_2, norm_mix_g_2, w_in_2, conv_w_2, conv_b_2,
        dt_bias_f_2, dt_bias_b_2, a_log_f_2, a_log_b_2, ssd_d_2, ssd_norm_g_2, lambda_q1_2,
        lambda_k1_2, lambda_q2_2, lambda_k2_2, attn_subln_g_2, w_attn_o_2, w_ssd_o_2, w_out_2,
        norm_mlp_g_2, w_mlp1_2, w_mlp2_2, final_norm_g_2,
    )


_drawn_inputs = setup_inputs


def setup_inputs(seed=0):
    import zlib

    import numpy as np

    out = dict(_drawn_inputs(seed))
    spreads = {}
    factors = {'conv_b': 4.52,
     'norm_mix_g_2': 4.553,
     'conv_b_2': 8.0,
     'ssd_d_2': 8.0,
     'ssd_norm_g_2': 7.683,
     'lambda_q1_2': 4.79,
     'lambda_k1_2': 8.0,
     'lambda_q2_2': 8.0,
     'lambda_k2_2': 8.0,
     'attn_subln_g_2': 8.0}
    for name, (base, spread) in spreads.items():
        noise = np.random.default_rng([zlib.crc32(name.encode()), seed]).standard_normal(out[name].shape)
        drawn = base * np.exp(spread * noise) if base else spread * noise
        out[name] = __import__('jax').numpy.asarray(drawn.astype(out[name].dtype))
    for name, factor in factors.items():
        out[name] = (out[name] * factor).astype(out[name].dtype)
    return out
```

```python
from contextlib import ExitStack, contextmanager

import numpy as np

import concourse.bass as bass
from concourse import mybir

F32 = mybir.dt.float32
ALU = mybir.AluOpType
ACT = mybir.ActivationFunctionType
AX = mybir.AxisListType

P = 128
SEQ = 256
T = 2 * SEQ
D = 1024
KT = D // P
LT = SEQ // P
TT = T // P
HD = 64
HEADS = 8
D_FF = 2816
FFT = D_FF // P
EPS = 1e-6
LAYERS = 2
SSD_IN = 2048
GROUPS = 8
GH = 4
GW = GH * HD
SSD_HEADS = 32
HID = 4096
HIDT = HID // P
YT = SSD_IN // P
N_MOD = 48
SLOTS = 4
SLAB = 2048
C_Z, C_X, C_B, C_C, C_DT, C_GA, C_GS = 3072, 5120, 7168, 8192, 9216, 9280, 10304


def shape_constants():
    i, j = np.arange(P)[:, None], np.arange(P)[None, :]
    ident = (i == j).astype(np.float32)
    heads = (i // HD == j // HD).astype(np.float32)
    ones = np.ones((P, P), np.float32)

    def turn(half):
        m = np.zeros((P, P), np.float32)
        for p in range(P):
            if p % (2 * half) < half:
                m[p + half, p] = -1.0
            else:
                m[p - half, p] = 1.0
        return m

    row = np.repeat(np.arange(4, dtype=np.float32), 64)
    col = np.tile(np.arange(64, dtype=np.float32), 4)
    inv = np.float32(10000.0) ** (-np.arange(16, dtype=np.float32) / np.float32(16))
    ang1 = np.zeros((P, SEQ), np.float32)
    ang2 = np.zeros((P, SEQ), np.float32)
    for p in range(P):
        d = p % HD
        ang1[p] = (row if d < 32 else col) * inv[d % 16]
        e = p % 32
        ang2[p] = (row if e < 16 else col) * inv[e % 16]
    cols = [ident, heads, ones, turn(16), turn(32),
            (i > j), (i < j), (i <= j), (i >= j),
            np.cos(ang1), np.sin(ang1), np.cos(ang2), np.sin(ang2)]
    for q in range(LT):
        dist = np.abs(np.arange(SEQ)[None, :] - (q * P + np.arange(P))[:, None])
        count = (dist <= 64).astype(np.float32) + (dist % 4 == 0) + (dist % 16 == 0)
        cols += [np.where(count > 0, -dist, -1e30), count]
    return np.ascontiguousarray(np.concatenate([np.asarray(c, np.float32) for c in cols], axis=1))


class Counts:

    def __init__(self, eng):
        self.eng, self.n, self.i, self.per = eng, {}, None, {}

    def skip(self, sem, k=1):
        self.n[sem.name] = self.n.get(sem.name, 0) + k

    def value(self, sem):
        n = self.n.get(sem.name, 0)
        if self.i is not None and self.per.get(sem.name):
            return self.i * self.per[sem.name] + n
        return n

    def made(self, sem, k=1):
        self.skip(sem, k)
        return sem, k

    def need(self, sem, k=1):
        self.skip(sem, k)
        return sem, self.value(sem)

    def sofar(self, sem):
        return sem, self.value(sem)

    @contextmanager
    def loop(self, times, per):
        with self.eng.Fori(0, times) as i:
            start = dict(self.n)
            self.i, self.per = i, {s.name: k for s, k in per}
            yield i
            for name, n in self.n.items():
                moved = n - start.get(name, 0)
                assert moved == self.per.get(name, 0), (name, moved)
            for name, k in self.per.items():
                self.n[name] = start.get(name, 0) + k * times
            self.i, self.per = None, {}


def two_blocks(nc, a, const, out, upto=99):
    with ExitStack() as ctx:
        def sb(name, shape):
            return ctx.enter_context(nc.sbuf_tensor(name, shape, F32))

        def sem(name):
            return ctx.enter_context(nc.semaphore(name))

        PS = ctx.enter_context(nc.psum_tensor("PS", [P, 8, 512], F32))
        n_const = const.shape[1]
        K = sb("constants", [P, n_const])
        xT = sb("xT", [P, KT, T])
        hT = sb("hT", [P, KT, T])
        ring = sb("ring", [P, SLOTS, SLAB])
        big1 = sb("big1", [P, 8192])
        big2 = sb("big2", [P, 8192])
        mid_v = sb("mid_v", [P, 4096])
        mid_o = sb("mid_o", [P, 4096])
        mid_a = sb("mid_a", [P, 4096])

        def view(buf, at, *dims):
            n = int(np.prod(dims))
            flat = buf[:, at:at + n]
            if len(dims) == 1:
                return flat
            if len(dims) == 2:
                return flat.rearrange("p (a b) -> p a b", a=dims[0])
            return flat.rearrange("p (a b c) -> p a b c", a=dims[0], b=dims[1])

        ident, heads, ones, turn1, turn2, t_gt, t_lt, t_le, t_ge = (
            K[:, n * P:(n + 1) * P] for n in range(9))
        at = 9 * P
        cos1, sin1, cos2, sin2 = (K[:, at + n * SEQ:at + (n + 1) * SEQ] for n in range(4))
        at += 4 * SEQ
        far = [K[:, at + 2 * q * SEQ:at + (2 * q + 1) * SEQ] for q in range(LT)]
        times_seen = [K[:, at + (2 * q + 1) * SEQ:at + (2 * q + 2) * SEQ] for q in range(LT)]

        rows, pieces = {}, []
        n_rows = 0

        def vector(name, src):
            nonlocal n_rows
            rows[name] = n_rows
            n, k = src.shape[0], 0
            while k < n:
                m = min(n - k, P - n_rows % P)
                pieces.append((n_rows // P, n_rows % P, m, src[k:k + m, :]))
                n_rows += m
                k += m

        flat1 = "(a b) -> a b"
        flat2 = "l (a b) -> (l a) b"
        for name in ("norm1_g", "norm2_g", "conv_b", "c_ctx_2", "final_norm_g_2", "outa_norm_g", "outb_norm_g"):
            vector(name, a[name].rearrange(flat1, b=P))
        vector("conv_w", a["conv_w"].rearrange(flat2, b=P))
        for name in ("c_2", "ada_b_2", "norm_mix_g_2", "norm_mlp_g_2", "ssd_norm_g_2", "attn_subln_g_2"):
            vector(name, a[name].rearrange(flat2, b=P))
        vector("conv_w_2", a["conv_w_2"].rearrange("l t (a b) -> (l t a) b", b=P))
        vector("conv_b_2", a["conv_b_2"].rearrange(flat2, b=P))
        n_head_rows = n_rows
        for name in ("qa_norm_g", "qb_norm_g", "ka_norm_g", "kb_norm_g"):
            rows[name] = n_rows
            n_rows += 1
        n_stage = -(-n_rows // P)
        vstage = view(big2, 0, n_stage, P)
        V = sb("V", [P, n_rows])

        def col(name, j=0):
            return V[:, rows[name] + j:rows[name] + j + 1]

        def dcol(name, j, i):
            return V[:, bass.ds(i + (rows[name] + j), 1)]

        lam_in = sb("lam_in", [P, LAYERS, 4, HD])
        lam_s = sb("lam_s", [P, 3 * LAYERS * 2])
        neg_lam = sb("neg_lam", [P, LAYERS])
        head_in = sb("head_in", [P, LAYERS, 5 * SSD_HEADS])
        neg_a = sb("neg_a", [P, LAYERS, 2 * SSD_HEADS])
        cact = sb("cact", [P, KT, 2])
        ctan = sb("ctan", [P, KT, 2])
        craw = sb("craw", [P, KT, 2])
        mod = sb("mod", [P, N_MOD, 2])
        amix = sb("amix", [P, KT, 2])
        amlp = sb("amlp", [P, KT, 2])
        hgate = sb("hgate", [P, KT, 2])
        eps = sb("eps", [P, 1])
        stat = sb("stat", [P, 256])
        by_head = sb("by_head", [P, TT, 7 * SSD_HEADS])
        dt, dta, wst = (by_head[:, :, n * 64:(n + 1) * 64] for n in range(3))
        of_group = sb("of_group", [P, TT, 7, GH])
        edec = sb("edec", [P, TT, 192])

        rms = view(mid_a, 0, T)
        rstd = view(mid_a, T, T)
        xin = view(mid_o, 0, TT, D)

        const_loaded, x_loaded, vec_loaded, small_loaded = map(
            sem, ("const_loaded", "x_loaded", "vec_loaded", "small_loaded"))
        slot_loaded = [sem(f"slot_loaded{s}") for s in range(SLOTS)]
        tile_ready = sem("tile_ready")
        act_freed = sem("act_freed")
        dve_freed = sem("dve_freed")
        turned = sem("turned")
        turned_freed = sem("turned_freed")
        fence = sem("fence")
        act_step = sem("act_step")
        dve_step = sem("dve_step")
        pool_step = sem("pool_step")
        squares, mean_sq, rms_ready, scaled, shifted = map(
            sem, ("squares", "mean_sq", "rms_ready", "scaled", "shifted"))
        vec_ready, lam_sum, lam_exp, cond_tanh, cond_ready, mods_ready = map(
            sem, ("vec_ready", "lam_sum", "lam_exp", "cond_tanh", "cond_ready", "mods_ready"))
        head_sq, head_ms, head_rms, head_normed, rot_ready, rot_done, q_raw = map(
            sem, ("head_sq", "head_ms", "head_rms", "head_normed", "rot_ready", "rot_done", "q_raw"))
        s_ready, max_ready, p_ready, a_ready, t_ready, at_ready, o_ready, o_done = map(
            sem, ("s_ready", "max_ready", "p_ready", "a_ready", "t_ready", "at_ready", "o_ready", "o_done"))
        sum_sq, tok_rms, tok_scaled = map(sem, ("sum_sq", "tok_rms", "tok_scaled"))
        conv_mid, conv_done, gate_act, hid_mid = map(sem, ("conv_mid", "conv_done", "gate_act", "hid_mid"))
        dt_abs, dt_exp, dt_one, dt_ln, dta_ready, dec_ready, dec_exp = map(
            sem, ("dt_abs", "dt_exp", "dt_one", "dt_ln", "dta_ready", "dec_ready", "dec_exp"))
        conv_tanh, chan_ready, z_tanh = map(sem, ("conv_tanh", "chan_ready", "z_tanh"))
        tok_turned, tok_ready, cb_ready, cb_masked, seg_in, seg_ready, e_ready, dtu_ready, m_ready = map(
            sem, ("tok_turned", "tok_ready", "cb_ready", "cb_masked", "seg_in", "seg_ready", "e_ready",
                  "dtu_ready", "m_ready"))
        xw_ready, xd_ready, st_ready, hin_ready, y_ready, y_done = map(
            sem, ("xw_ready", "xd_ready", "st_ready", "hin_ready", "y_ready", "y_done"))
        gated, out_ready, stored = map(sem, ("gated", "out_ready", "stored"))

        block = ctx.enter_context(nc.Block())

        def tiles(w):
            return w.rearrange("(k p) n -> p k n", p=P)

        w_in, w_out, w_up, w_down = (tiles(a[n]) for n in ("w_in", "w_out", "w_up", "w_down"))

        def of_layer(name, l):
            return tiles(a[name][l])

        def slot(s, kt, width):
            return ring[:, s, 0:kt * width].rearrange("p (k n) -> p k n", k=kt)

        raw1 = view(big1, 0, 14, SEQ)
        sq1 = view(big2, 0, 14, SEQ)
        v1 = view(mid_v, 0, LT, 640)
        rot1 = view(big1, 14 * SEQ, 3, 2 * SEQ)
        o1 = view(mid_o, 0, LT, D)
        mix1 = view(mid_a, 0, KT, SEQ)
        gate1 = view(big1, 0, FFT, SEQ)
        cv1 = view(big2, 0, 4, 2, SEQ)
        qT = view(big1, 0, KT, T)
        kT = view(big1, KT * T, KT, T)
        v2 = view(mid_v, 0, TT, D)
        rot2 = view(big2, 0, 2, SEQ)
        o2 = view(mid_o, 0, TT, D)
        attT = view(mid_a, 0, KT, T)
        prob = view(big2, 0, 2, 2 * T)
        amat = view(big2, 4 * T, 2, T)
        amatT = view(big2, 6 * T, 2, T)
        atmp = view(big2, 8 * T, 2, T)
        yg = view(big2, 0, TT, SSD_IN)
        yT = view(big1, 0, YT, T)
        junk = view(mid_v, 0, SSD_IN)
        merged = view(mid_v, 0, KT, T)
        gs = view(mid_o, 0, KT, T)

        def hidden(n):
            return big1[:, n * T:(n + 1) * T] if n < YT else big2[:, (n - YT) * T:(n - YT + 1) * T]

        chan = view(mid_o, 0, 4, T)
        ctanh = view(mid_o, 4 * T, 2, T)
        sz = view(mid_o, 6 * T, TT, GW)
        xtok = view(big1, 0, TT, GW)
        btok = view(big1, 1024, TT, P)
        cb_lo = view(big1, 1536, TT, P)
        cb_up = view(big1, 2048, TT, P)
        seg_f = view(big1, 2560, 2, GH, P)
        seg_b = view(big1, 3584, 2, GH, P)
        ex = view(big1, 4608, 2, GH * P)
        dt_lo = view(big1, 5632, GH, P)
        dt_up = view(big1, 6144, 2, GH * P)
        mt = view(big1, 7168, 2, GH * P)
        xw = view(mid_v, 0, 6, GW)
        hin = view(mid_v, 1536, 6, GW)
        ys = view(mid_v, 3072, GW)
        yi = view(mid_v, 3328, GW)
        xd = view(mid_v, 3584, 2, GW)
        dtx = [view(big1, n * 256, TT, 2 * SSD_HEADS) for n in range(6)]

        def y_chunks(l):
            return range(TT) if l == 0 else range(LT)

        F_STATES = [2, 3, 0]
        B_STATES = [3, 2, 1]
        HF = {3: 0, 0: 1, 1: 2}
        HB = {2: 3, 1: 4, 0: 5}

        def units2(l):
            return [(h, q) for h in range(HEADS) for q in range(TT if l == 0 else LT)]

        UNITS1 = [(kind, hp, q) for kind in "AB" for hp in range(4) for q in range(LT)]

        @block.sync
        def _(sp):
            c = Counts(sp)
            done = []
            total = [0]

            sp.dma_start(K[:, :], const).then_inc(const_loaded, 16)
            sp.dma_start(xin[:, 0:LT, :], a["x"][0].rearrange("(t p) d -> p t d", p=P)).then_inc(x_loaded, 16)
            sp.dma_start(xin[:, LT:TT, :], a["ctx_2"][0].rearrange("(t p) d -> p t d", p=P)).then_inc(x_loaded, 16)

            def load(parts, tiles_after):
                s = len(done) % SLOTS
                if len(done) >= SLOTS:
                    sp.wait_ge(tile_ready, done[len(done) - SLOTS])
                for dst, src in parts(s):
                    sp.dma_start(dst, src).then_inc(slot_loaded[s], 16)
                done.append(total[0] + tiles_after)

            def slabs(n, kt, width, src, tiles_done, body=SLOTS, parts=None):
                parts = parts or (lambda s, j: [(slot(s, kt, width), src(j))])
                turns = n // body
                first = body if turns >= 3 else n
                for j in range(first):
                    load(lambda s: parts(s, j), tiles_done(j + 1))
                if turns >= 3:
                    slope = tiles_done(2 * body) - tiles_done(body)
                    s0 = len(done) - body
                    with sp.Fori(1, turns) as i:
                        for q in range(body):
                            s = (s0 + q) % SLOTS
                            sp.wait_ge(tile_ready, i * slope + (total[0] + tiles_done(body + q - SLOTS + 1) - slope))
                            for dst, part in parts(s, i * body + q):
                                sp.dma_start(dst, part).then_inc(slot_loaded[s], 16)
                    for j in range(body, body * turns):
                        done.append(total[0] + tiles_done(j + 1))
                    for j in range(body * turns, n):
                        load(lambda s: parts(s, j), tiles_done(j + 1))
                total[0] += tiles_done(n)

            def wide(w, c0, n, per=2):
                slabs(n, KT, 256, lambda j: w[:, :, bass.ds(j * 256 + c0, 256)], lambda j: per * j)

            wide(w_in, 0, 2)
            slabs(1, KT, 256, None, lambda j: 2 * j, parts=lambda s, j: [
                (slot(s, KT, 256)[:, :, n * HD:(n + 1) * HD], w_in[:, :, 512 + HD * (n // 2):576 + HD * (n // 2)])
                for n in range(4)])
            slabs(1, KT, 128, lambda j: w_in[:, :, 640:768], lambda j: 2 * j)
            wide(w_in, 768, 6)
            wide(w_out, 0, 4)
            slabs(FFT, KT, 256, None, lambda j: 2 * j, parts=lambda s, j: [
                (slot(s, KT, 256)[:, :, 0:P], w_up[:, :, bass.ds(j * P, P)]),
                (slot(s, KT, 256)[:, :, P:2 * P], w_up[:, :, bass.ds(j * P + D_FF, P)])])
            halves = FFT // 2
            for n in range(KT):
                slabs(2, halves, P, lambda j: w_down[:, halves * j:halves * (j + 1), n * P:(n + 1) * P],
                      lambda j: (j + 1) // 2)

            for l in range(LAYERS):
                ada, wi = of_layer("ada_w_2", l), of_layer("w_in_2", l)
                wide(ada, 0, N_MOD // 2)
                wide(wi, 0, 4)
                wide(wi, 1024, 4)
                wide(wi, 2048, 4, per=TT)
                slabs(1, KT, 64, lambda j: wi[:, :, C_DT:C_DT + 64], lambda j: TT * j)
                nz = len(y_chunks(l)) // 2
                per_group = 4 + nz
                after = [1, 2, 4, per_group]

                def group_parts(s, q, g):
                    half = slot(s, KT, P)
                    full = slot(s, KT, 256)
                    if q < 2:
                        return [(half, wi[:, :, bass.ds(g * GW + (C_X + q * P), P)])]
                    if q == 2:
                        return [(full[:, :, 0:P], wi[:, :, bass.ds(g * P + C_B, P)]),
                                (full[:, :, P:2 * P], wi[:, :, bass.ds(g * P + C_C, P)])]
                    return [(full, wi[:, :, bass.ds(g * GW + C_Z, GW)])]

                s0 = len(done)
                for q in range(4):
                    load(lambda s: group_parts(s, q, 0), after[q])
                with sp.Fori(1, GROUPS) as g:
                    for q in range(4):
                        s = (s0 + q) % SLOTS
                        sp.wait_ge(tile_ready, g * per_group + (total[0] + after[q] - per_group))
                        for dst, src in group_parts(s, q, g):
                            sp.dma_start(dst, src).then_inc(slot_loaded[s], 16)
                for g in range(1, GROUPS):
                    done.extend(total[0] + per_group * g + n for n in after)
                total[0] += per_group * GROUPS
                wide(wi, C_GA, 4)
                wide(of_layer("w_attn_o_2", l), 0, 4)
                wide(wi, C_GS, 4)
                wo = of_layer("w_ssd_o_2", l)
                slabs(KT, YT, P, lambda j: wo[:, :, bass.ds(j * P, P)], lambda j: j)
                wide(of_layer("w_out_2", l), 0, 4)
                wide(of_layer("w_mlp1_2", l), 0, HIDT // 2)
                w2 = of_layer("w_mlp2_2", l)
                for n in range(KT):
                    slabs(2, YT, P, lambda j: w2[:, YT * j:YT * (j + 1), n * P:(n + 1) * P], lambda j: (j + 1) // 2)

            sp.wait_ge(out_ready, 4)
            sp.dma_start(out[0].rearrange("(t p) d -> p t d", p=P), view(big2, 0, LT, D)).then_inc(stored, 16)
            sp.wait_ge(stored, 16)

        @block.tensor
        def _(pe):
            c = Counts(pe)
            slab, tile, bank4, fences = [0], [0], [0], [0]

            def stage():
                pe.drain().then_inc(*c.made(fence))
                fences[0] += 1
                pe.wait_ge(fence, 4 * fences[0])

            def ring_wait(sem):
                _, v = c.need(sem)
                if c.i is not None or v > 0:
                    pe.wait_ge(sem, v)

            def ring_begin(sem):
                c.skip(sem, -4)

            def ring_end(sem):
                pe.wait_ge(*c.need(sem, 4))

            def bodies(n, body, work, per):
                turns = n // body
                if turns >= 2:
                    with c.loop(turns, per) as i:
                        for j in range(body):
                            work(j, i)
                    for j in range(n % body):
                        work(j, turns)
                else:
                    for j in range(n):
                        work(j, 0)

            def weights(k=16):
                s = slab[0] % SLOTS
                slab[0] += 1
                pe.wait_ge(*c.need(slot_loaded[s], k))
                return s

            def to_features(n, rhs, cols, freed, kt=KT, width=256, halves=1, loads=1):
                ring_begin(freed)
                per_slab = width // P
                body = SLOTS * halves

                def work(j, i):
                    s = weights(16 * loads)
                    w = slot(s, kt, width)
                    half = j % halves
                    for m in range(per_slab):
                        b = tile[0] % 4
                        if half == 0:
                            ring_wait(freed)
                        for k in range(kt):
                            mm = pe.matmul(PS[:, b, 0:cols], w[:, k, m * P:(m + 1) * P], rhs(half * kt + k),
                                           start=(half == 0 and k == 0), stop=(half == halves - 1 and k == kt - 1))
                        if half == halves - 1:
                            mm.then_inc(*c.made(tile_ready))
                            tile[0] += 1

                moved = body * per_slab // halves
                bodies(n, body, work, [(tile_ready, moved), (freed, moved)]
                       + [(q, 16 * loads * body // SLOTS) for q in slot_loaded])
                ring_end(freed)

            def to_tokens(n, width, n_tok, freed, pairs=False):
                ring_begin(freed)

                def work(j, i):
                    w = slot(weights(), KT, width)
                    for t in range(n_tok):
                        b = tile[0] % 4
                        ring_wait(freed)
                        for k in range(KT):
                            mm = pe.matmul(PS[:, b, 0:width], hT[:, k, t * P:(t + 1) * P], w[:, k, :],
                                           start=(k == 0), stop=(k == KT - 1))
                        mm.then_inc(*c.made(tile_ready))
                        tile[0] += 1

                bodies(n, SLOTS, work, [(tile_ready, SLOTS * n_tok), (freed, SLOTS * n_tok)]
                       + [(q, 16) for q in slot_loaded])
                ring_end(freed)

            def norm(cols):
                for k in range(KT):
                    pe.wait_ge(*c.need(squares))
                    mm = pe.matmul(PS[:, 4, 0:cols], ones, hT[:, k, 0:cols], start=(k == 0), stop=(k == KT - 1))
                mm.then_inc(*c.made(mean_sq))

            def turn_begin():
                c.skip(turned_freed, -4)

            def turn_end():
                pe.wait_ge(*c.need(turned_freed, 4))

            def turn(parts):
                b = 4 + bank4[0] % 4
                bank4[0] += 1
                ring_wait(turned_freed)
                for n, src in enumerate(parts):
                    mm = pe.transpose(PS[0:src.shape[1], b, n * P:n * P + src.shape[0]], src,
                                      ident[0:src.shape[0], 0:src.shape[0]])
                mm.then_inc(*c.made(turned))

            pe.wait_ge(const_loaded, 16)
            pe.wait_ge(x_loaded, 32)
            turn_begin()
            for k in range(KT):
                turn([xin[:, t, k * P:(k + 1) * P] for t in range(TT)])
            pe.wait_ge(vec_loaded, 16 * (len(pieces) + 8))
            n_left = [min(P, n_rows - n * P) for n in range(n_stage)]
            for b in range(-(-n_stage // 4)):
                turn([vstage[0:n_left[n], n, :] for n in range(4 * b, min(4 * b + 4, n_stage))])
            turn_end()
            stage()

            norm(SEQ)
            pe.wait_ge(*c.need(scaled, KT))
            lat = lambda k: hT[:, k, 0:SEQ]
            to_features(2, lat, SEQ, act_freed)
            to_features(1, lat, SEQ, act_freed, loads=4)
            to_tokens(1, 128, LT, act_freed)
            to_features(4, lat, SEQ, act_freed)
            to_tokens(2, 256, LT, act_freed)
            for n in range(7):
                pe.wait_ge(*c.need(head_sq, 2))
                pe.matmul(PS[:, n, :], heads, sq1[:, 2 * n:2 * n + 2, :], start=True, stop=True).then_inc(*c.made(head_ms))
            pe.wait_ge(*c.need(head_normed, 14))
            for n in range(3):
                pe.matmul(PS[:, n, :], turn1, raw1[:, 2 * n:2 * n + 2, :], start=True, stop=True).then_inc(*c.made(rot_ready))
            pe.wait_ge(*c.need(rot_done, 3))

            def scores1(u):
                kind, hp, q = UNITS1[u]
                if u >= 2:
                    pe.wait_ge(*c.need(p_ready))
                for e in range(2):
                    r = slice(e * HD, (e + 1) * HD)
                    tq = hp if kind == "A" else 6 + hp
                    tk = 4 + hp // 2 if kind == "A" else 10 + hp
                    mm = pe.matmul(PS[:, 2 * (u % 2) + e, 0:SEQ], raw1[r, tq, q * P:(q + 1) * P], raw1[r, tk, :],
                                   start=True, stop=True)
                mm.then_inc(*c.made(s_ready))

            scores1(0)
            for u in range(len(UNITS1)):
                kind, hp, q = UNITS1[u]
                if u + 1 < len(UNITS1):
                    scores1(u + 1)
                pe.wait_ge(*c.need(a_ready))
                for n in range(4):
                    mm = pe.transpose(PS[:, 4 + u % 2, n * P:(n + 1) * P], amat[:, u % 2, n * P:(n + 1) * P], ident)
                mm.then_inc(*c.made(t_ready))
                pe.wait_ge(*c.need(at_ready))
                if u >= 2:
                    pe.wait_ge(*c.need(o_done))
                for e in range(2):
                    h = 2 * hp + e
                    v0 = HD * (h // 4) if kind == "A" else P + HD * h
                    for t in range(LT):
                        mm = pe.matmul(PS[:, 6 + u % 2, e * HD:(e + 1) * HD],
                                       amatT[:, u % 2, (e * LT + t) * P:(e * LT + t + 1) * P],
                                       v1[:, t, v0:v0 + HD], start=(t == 0), stop=(t == LT - 1))
                mm.then_inc(*c.made(o_ready))
            c.skip(p_ready, 2)
            pe.wait_ge(*c.need(o_done, 2))
            pe.wait_ge(*c.need(tok_scaled, 2 * LT))
            turn_begin()
            for f in range(KT):
                turn([o1[:, t, f * P:(f + 1) * P] for t in range(LT)])
            turn_end()
            to_features(4, lambda k: mix1[:, k, :], SEQ, dve_freed)
            stage()
            norm(SEQ)
            pe.wait_ge(*c.need(scaled, KT))
            to_features(FFT, lat, SEQ, dve_freed, loads=2)
            pe.wait_ge(*c.need(conv_done, FFT))
            to_features(2 * KT, lambda k: gate1[:, k, :], SEQ, dve_freed, kt=FFT // 2, width=P, halves=2)
            stage()

            for l in range(LAYERS):
                if l == 0:
                    pe.wait_ge(*c.need(cond_ready))

                def ada(j, i):
                    w = slot(weights(), KT, 256)
                    for m in range(2):
                        for k in range(KT):
                            mm = pe.matmul(PS[:, 5, bass.ds(i * 16 + (4 * j + 2 * m), 2)], w[:, k, m * P:(m + 1) * P],
                                           cact[:, k, :], start=(k == 0), stop=(k == KT - 1))
                        mm.then_inc(*c.made(tile_ready))
                        tile[0] += 1

                bodies(N_MOD // 2, SLOTS, ada, [(tile_ready, 2 * SLOTS)] + [(q, 16) for q in slot_loaded])
                norm(T)
                pe.wait_ge(*c.need(shifted, 2 * KT))
                c.skip(scaled, 2 * KT)
                both = lambda k: hT[:, k, :]
                q_cols = T if l == 0 else SEQ
                some = lambda k: hT[:, k, 0:q_cols]

                to_features(4, some, q_cols, act_freed)
                to_features(4, both, T, act_freed)
                for n in range(2 * KT):
                    src = qT if n < KT else kT
                    if n >= 4:
                        pe.wait_ge(*c.need(rot_done))
                    pe.matmul(PS[:, 4 + n % 4, 0:SEQ], turn2, src[:, n % KT, 0:SEQ], start=True, stop=True)\
                        .then_inc(*c.made(rot_ready))
                to_tokens(4, 256, TT, act_freed)
                pe.wait_ge(*c.need(rot_done, 4))

                units = units2(l)

                def scores2(u):
                    h, q = units[u]
                    k0, nk = (0, T) if q < LT else (SEQ, SEQ)
                    if u >= 2:
                        pe.wait_ge(*c.need(p_ready, 2))
                    for e in range(2):
                        r = slice(e * HD, (e + 1) * HD)
                        mm = pe.matmul(PS[:, 2 * (u % 2) + e, 0:nk], qT[r, h, q * P:(q + 1) * P], kT[r, h, k0:k0 + nk],
                                       start=True, stop=True)
                    mm.then_inc(*c.made(s_ready))

                scores2(0)
                for u, (h, q) in enumerate(units):
                    k0, nt = (0, TT) if q < LT else (LT, LT)
                    if u + 1 < len(units):
                        scores2(u + 1)
                    pe.wait_ge(*c.need(a_ready))
                    for n in range(nt):
                        mm = pe.transpose(PS[:, 4 + u % 2, n * P:(n + 1) * P], amat[:, u % 2, n * P:(n + 1) * P], ident)
                    mm.then_inc(*c.made(t_ready))
                    pe.wait_ge(*c.need(at_ready))
                    if u >= 2:
                        pe.wait_ge(*c.need(o_done))
                    for n in range(nt):
                        mm = pe.matmul(PS[:, 6 + u % 2, 0:P], amatT[:, u % 2, n * P:(n + 1) * P],
                                       v2[:, k0 + n, h * P:(h + 1) * P], start=(n == 0), stop=(n == nt - 1))
                    mm.then_inc(*c.made(o_ready))
                c.skip(p_ready, 4)
                pe.wait_ge(*c.need(o_done, 2))
                n_tok = len(y_chunks(l))
                pe.wait_ge(*c.need(tok_scaled, n_tok))
                turn_begin()
                for f in range(KT):
                    turn([o2[:, t, f * P:(f + 1) * P] for t in range(n_tok)])
                turn_end()
                stage()

                to_tokens(1, 64, TT, dve_freed)
                pe.wait_ge(*c.need(dta_ready))
                for t in range(TT):
                    bank, o = t, 0
                    for m, lhs, r0, n in ((0, t_gt, 0, 32), (32, t_le, 0, 32), (64, t_lt, 32, 32), (96, t_ge, 32, 32),
                                          (128, ones, 0, 64)):
                        mm = pe.matmul(PS[:, bank, o + m:o + m + n], lhs, dta[:, t, r0:r0 + n], start=True, stop=True)
                    mm.then_inc(*c.made(dec_ready))
                stage()

                ny = len(y_chunks(l))
                nz = ny // 2
                s0 = slab[0]

                def group(g):
                    def w_of(q):
                        s = (s0 + q) % SLOTS
                        pe.wait_ge(*c.need(slot_loaded[s], 32 if q == 2 else 16))
                        return s

                    for j in range(4):
                        if j < 3:
                            s = w_of(j)
                            w = slot(s, KT, P if j < 2 else 256)
                        m = P if j == 3 else 0
                        for k in range(KT):
                            mm = pe.matmul(PS[:, j, :], w[:, k, m:m + P], hT[:, k, :], start=(k == 0), stop=(k == KT - 1))
                        mm.then_inc(*c.made(tile_ready))
                    w = slot(w_of(3), KT, 256)
                    for b in range(nz):
                        pe.wait_ge(*c.need(dve_freed))
                        for t in range(2):
                            for k in range(KT):
                                mm = pe.matmul(PS[:, b, t * GW:(t + 1) * GW], hT[:, k, (2 * b + t) * P:(2 * b + t + 1) * P],
                                               w[:, k, :], start=(k == 0), stop=(k == KT - 1))
                        mm.then_inc(*c.made(tile_ready))
                    for n in range(2):
                        if n == 0:
                            pe.wait_ge(*c.need(chan_ready, 4))
                        for t in range(4):
                            mm = pe.transpose(PS[:, 4 + n, t * P:(t + 1) * P],
                                              chan[:, t % 2, (2 * n + t // 2) * P:(2 * n + t // 2 + 1) * P], ident)
                        mm.then_inc(*c.made(tok_turned))
                    for t in range(TT):
                        mm = pe.transpose(PS[:, 6, t * P:(t + 1) * P], chan[:, 2, t * P:(t + 1) * P], ident)
                    mm.then_inc(*c.made(tok_turned))
                    for t in range(ny):
                        mm = pe.matmul(PS[:, 7, t * P:(t + 1) * P], chan[:, 2, t * P:(t + 1) * P], chan[:, 3, t * P:(t + 1) * P],
                                       start=True, stop=True)
                    mm.then_inc(*c.made(cb_ready))

                    pe.wait_ge(*c.need(dve_freed, 4))

                    def seg(t):
                        pe.wait_ge(*c.need(seg_in, 2))
                        if t == 1:
                            pe.wait_ge(*c.need(cb_masked))
                        pe.matmul(PS[:, (3, 7)[t % 2], :], t_gt, seg_f[:, t % 2, :, :].rearrange("p r l -> p (r l)"),
                                  start=True, stop=False)
                        pe.matmul(PS[:, (3, 7)[t % 2], :], t_lt, seg_b[:, t % 2, :, :].rearrange("p r l -> p (r l)"),
                                  start=False, stop=True).then_inc(*c.made(seg_ready))

                    seg(0)
                    seg(1)
                    pe.wait_ge(*c.need(tok_ready, 3))
                    pe.wait_ge(*c.need(xw_ready, 6))
                    for n, t in enumerate(F_STATES + B_STATES):
                        mm = pe.matmul(PS[:, 4 + n // 2, (n % 2) * GW:(n % 2 + 1) * GW], btok[:, t, :], xw[:, n, :],
                                       start=True, stop=True)
                    mm.then_inc(*c.made(st_ready))
                    for t in range(ny):
                        pe.wait_ge(*c.need(m_ready))
                        if t == 0:
                            pe.wait_ge(*c.need(hin_ready))
                        if t >= 2:
                            pe.wait_ge(*c.need(y_done))
                        b = t % 2
                        for r in range(GH):
                            pe.matmul(PS[:, b, r * HD:(r + 1) * HD], mt[:, b, r * P:(r + 1) * P],
                                      xtok[:, t, r * HD:(r + 1) * HD], start=True, stop=True)
                        for d, hs in enumerate((HF, HB)):
                            if t in hs:
                                mm = pe.matmul(PS[:, 4 + b, d * GW:(d + 1) * GW], chan[:, 3, t * P:(t + 1) * P],
                                               hin[:, hs[t], :], start=True, stop=True)
                        mm.then_inc(*c.made(y_ready))
                        if t + 2 < ny:
                            pe.wait_ge(*c.need(e_ready))
                            seg(t + 2)
                    c.skip(e_ready, 2)
                    pe.wait_ge(*c.need(y_done, 2))

                with c.loop(GROUPS, [(tile_ready, 4 + nz), (dve_freed, 4 + nz), (chan_ready, 4), (tok_turned, 3),
                                     (cb_ready, 1), (seg_in, 2 * ny), (cb_masked, 1), (seg_ready, ny), (tok_ready, 3),
                                     (xw_ready, 6), (st_ready, 1), (m_ready, ny), (hin_ready, 1), (y_done, ny),
                                     (y_ready, ny), (e_ready, ny)]
                            + [(slot_loaded[(s0 + q) % SLOTS], 32 if q == 2 else 16) for q in range(4)]) as g:
                    group(g)
                slab[0] += 4 * GROUPS
                tile[0] += (4 + nz) * GROUPS
                stage()
                pe.wait_ge(*c.need(tok_scaled, ny))
                turn_begin()
                for f in range(YT):
                    turn([yg[:, t, f * P:(f + 1) * P] for t in range(ny)])
                turn_end()
                stage()
                to_features(4, some, q_cols, act_freed)
                to_features(4, lambda k: attT[:, k, 0:q_cols], q_cols, dve_freed)
                to_features(4, some, q_cols, act_freed)
                to_features(KT, lambda k: yT[:, k, 0:q_cols], q_cols, dve_freed, kt=YT, width=P)
                pe.wait_ge(*c.need(gated, KT))
                to_features(4, lambda k: merged[:, k, 0:q_cols], q_cols, dve_freed)
                stage()
                norm(q_cols)
                pe.wait_ge(*c.need(shifted, 2 * KT if l == 0 else KT))
                c.skip(scaled, 2 * KT if l == 0 else KT)
                to_features(HIDT // 2, some, q_cols, dve_freed)
                pe.wait_ge(*c.need(hid_mid, HIDT))
                to_features(2 * KT, lambda k: hidden(k)[:, 0:q_cols], q_cols, dve_freed, kt=YT, width=P, halves=2)
                stage()

            norm(SEQ)
            pe.wait_ge(*c.need(scaled, KT))
            turn_begin()
            for t in range(LT):
                for b in range(2):
                    turn([hT[:, 4 * b + k, t * P:(t + 1) * P] for k in range(4)])

        @block.scalar
        def _(act):
            c = Counts(act)
            tile, bank4, fences = [0], [0], [0]

            for n, p0, m, src in pieces:
                act.dma_start(vstage[p0:p0 + m, n, :], src).then_inc(vec_loaded, 16)
            for name in ("qa_norm_g", "qb_norm_g", "ka_norm_g", "kb_norm_g"):
                r = rows[name]
                for e in range(2):
                    act.dma_start(vstage[r % P:r % P + 1, r // P, e * HD:(e + 1) * HD],
                                  a[name].rearrange("(a b) -> a b", a=1)).then_inc(vec_loaded, 16)
            n_small = 0
            for l in range(LAYERS):
                for n, name in enumerate(("lambda_q1_2", "lambda_k1_2", "lambda_q2_2", "lambda_k2_2")):
                    act.dma_start(lam_in[:, l, n, :], a[name][l:l + 1, :].broadcast_to([P, HD])).then_inc(small_loaded, 16)
                for n, name in enumerate(("dt_bias_f_2", "dt_bias_b_2", "a_log_f_2", "a_log_b_2", "ssd_d_2")):
                    act.dma_start(head_in[:, l, n * 32:(n + 1) * 32], a[name][l:l + 1, :].broadcast_to([P, 32]))\
                        .then_inc(small_loaded, 16)
                n_small += 9

            def stage():
                act.drain().then_inc(*c.made(fence))
                fences[0] += 1
                act.wait_ge(fence, 4 * fences[0])

            def norm(cols):
                for k in range(KT):
                    act.activation(hT[:, k, 0:cols], xT[:, k, 0:cols], ACT.Square).then_inc(*c.made(squares))
                act.wait_ge(*c.need(mean_sq))
                act.activation(rms[:, 0:cols], PS[:, 4, 0:cols], ACT.Sqrt, scale=1.0 / D, bias=eps[:, 0:1])\
                    .then_inc(*c.made(rms_ready))

            def shift(l, m0, halves):
                for k in range(KT):
                    for e in range(halves):
                        act.wait_ge(*c.need(scaled))
                        h = hT[:, k, e * SEQ:(e + 1) * SEQ]
                        act.activation(h, h, ACT.Identity, bias=mod[:, m0 + k, e:e + 1]).then_inc(*c.made(shifted))

            def unload(dst, cols, func=ACT.Copy, scale=1.0):
                b = tile[0] % 4
                tile[0] += 1
                act.wait_ge(*c.need(tile_ready))
                act.activation(dst, PS[:, b:b + 1, 0:cols], func, scale=scale).then_inc(*c.made(act_freed))

            def unloads(n, dst, cols, func=ACT.Copy, scale=1.0):
                with c.loop(n // 4, [(tile_ready, 4), (act_freed, 4)]) as i:
                    for j in range(4):
                        unload(dst(i * 4 + j), cols, func, scale)

            def passed(n):
                c.skip(tile_ready, n)
                tile[0] += n

            def turned_to(dst, n, gain=None):
                b = 4 + bank4[0] % 4
                bank4[0] += 1
                act.wait_ge(*c.need(turned))
                if gain is None:
                    act.activation(dst, PS[:, b, 0:n], ACT.Copy).then_inc(*c.made(turned_freed))
                else:
                    act.activation(dst, PS[:, b, 0:n], ACT.Copy, scale=gain).then_inc(*c.made(turned_freed))

            act.wait_ge(*c.need(vec_ready))
            for k in range(KT):
                turned_to(xT[:, k, :], T)
            for b in range(-(-n_stage // 4)):
                turned_to(V[:, 512 * b:min(512 * (b + 1), n_rows)], min(512, n_rows - 512 * b))
            act.wait_ge(*c.sofar(turned_freed))
            act.wait_ge(*c.need(lam_sum))
            act.activation(lam_s[:, 4:8], lam_s[:, 0:4], ACT.Exp).then_inc(*c.made(lam_exp))
            act.wait_ge(small_loaded, 16 * n_small)
            act.activation(neg_a[:, :, :], head_in[:, :, 64:128], ACT.Exp).then_inc(*c.made(lam_exp))
            for e, name in enumerate(("c_2", "c_ctx_2")):
                act.activation(craw[:, :, e], V[:, rows[name]:rows[name] + KT], ACT.Copy).then_inc(*c.made(act_step))
            act.wait_ge(*c.sofar(act_step))
            act.activation(ctan[:, :, :], craw[:, :, :], ACT.Tanh, scale=0.5).then_inc(*c.made(cond_tanh))
            stage()

            norm(SEQ)
            c.skip(scaled, KT)
            for j in range(4):
                unload(raw1[:, j:j + 1, :], SEQ)
            for j in range(4, 6):
                unload(raw1[:, j:j + 1, :], SEQ)
            for t in range(LT):
                unload(v1[:, t:t + 1, 0:P], P)
            for j in range(6, 14):
                unload(raw1[:, j:j + 1, :], SEQ)
            for n in range(2):
                for t in range(LT):
                    unload(v1[:, t:t + 1, P + n * 256:P + (n + 1) * 256], 256)
            act.wait_ge(*c.sofar(act_freed))
            for j in range(14):
                act.activation(sq1[:, j, :], raw1[:, j, :], ACT.Square).then_inc(*c.made(head_sq))
            for n in range(7):
                act.wait_ge(*c.need(head_ms))
                act.activation(sq1[:, 2 * n:2 * n + 2, :], PS[:, n, :].rearrange("p (a b) -> p a b", a=2), ACT.Sqrt,
                               scale=1.0 / HD, bias=eps[:, 0:1]).then_inc(*c.made(head_rms))

            def exp1(u):
                act.wait_ge(*c.need(max_ready))
                if u >= 2:
                    act.wait_ge(*c.need(a_ready))
                for e in range(2):
                    src = PS[:, 2 * (u % 2) + e, 0:SEQ] if UNITS1[u][0] == "A" else atmp[:, u % 2, e * SEQ:(e + 1) * SEQ]
                    ins = act.activation(prob[:, u % 2, e * SEQ:(e + 1) * SEQ], src, ACT.Exp,
                                         bias=stat[:, 2 * u + e:2 * u + e + 1], accum_out=stat[:, 64 + 2 * u + e:65 + 2 * u + e])
                    if e:
                        ins.then_inc(*c.made(p_ready))

            def weightsT(u, n):
                act.wait_ge(*c.need(t_ready))
                if u >= 2:
                    act.wait_ge(*c.need(o_ready))
                act.activation(amatT[:, u % 2, 0:n], PS[:, 4 + u % 2, 0:n], ACT.Copy).then_inc(*c.made(at_ready))

            n_u = len(UNITS1)
            for u in range(n_u + 1):
                if u < n_u:
                    exp1(u)
                if u >= 1:
                    weightsT(u - 1, 512)
            c.skip(a_ready, 2)
            c.skip(o_ready, 2)
            act.wait_ge(*c.need(o_done, n_u))
            for t in range(LT):
                for e in range(2):
                    act.activation(junk[:, 0:512], o1[:, t, e * 512:(e + 1) * 512], ACT.Square,
                                   accum_out=stat[:, 128 + 2 * t + e:129 + 2 * t + e]).then_inc(*c.made(act_step))
                    act.wait_ge(*c.sofar(act_step))
            act.activation(stat[:, 136:140], stat[:, 128:132], ACT.Sqrt, scale=1.0 / 512, bias=eps[:, 0:1])\
                .then_inc(*c.made(tok_rms))
            c.skip(tok_scaled, 2 * LT)
            for f in range(KT):
                turned_to(mix1[:, f, :], SEQ, col("outa_norm_g", f) if f < 4 else col("outb_norm_g", f - 4))
            passed(KT)
            stage()
            norm(SEQ)
            c.skip(scaled, KT)

            def ffn(j):
                for e in range(2):
                    b = (tile0 + 2 * (j % 2) + e) % 4
                    act.wait_ge(*c.need(tile_ready))
                    if e == 0:
                        act.wait_ge(*c.need(conv_done))
                    jj = j if c.i is None else c.i * 2 + j
                    act.activation(cv1[:, j % 2, e, :], PS[:, b, 0:SEQ], ACT.Identity, scale=dcol("conv_w", 44 + 22 * e, jj),
                                   bias=dcol("conv_b", 22 * e, jj)).then_inc(*c.made(conv_mid))
                act.wait_ge(*c.need(dve_freed, 2))
                act.activation(cv1[:, 2 + j % 2, 0, :], cv1[:, j % 2, 0, :], ACT.Gelu_apprx_tanh).then_inc(*c.made(gate_act))

            c.skip(dve_freed, KT)
            tile0 = tile[0]
            c.skip(conv_done, -2)
            for j in range(2):
                jj = j
                for e in range(2):
                    b = (tile0 + 2 * (j % 2) + e) % 4
                    act.wait_ge(*c.need(tile_ready))
                    act.activation(cv1[:, j % 2, e, :], PS[:, b, 0:SEQ], ACT.Identity, scale=col("conv_w", 44 + 22 * e + j),
                                   bias=col("conv_b", 22 * e + j)).then_inc(*c.made(conv_mid))
                c.skip(conv_done)
                act.wait_ge(*c.need(dve_freed, 2))
                act.activation(cv1[:, 2 + j % 2, 0, :], cv1[:, j % 2, 0, :], ACT.Gelu_apprx_tanh).then_inc(*c.made(gate_act))
            with c.loop(FFT // 2 - 1, [(tile_ready, 4), (conv_mid, 4), (dve_freed, 4), (gate_act, 2), (conv_done, 2)]) as i:
                c.i = i
                for j in range(2):
                    for e in range(2):
                        b = (tile0 + 2 * j + e) % 4
                        act.wait_ge(*c.need(tile_ready))
                        if e == 0:
                            act.wait_ge(*c.need(conv_done))
                        act.activation(cv1[:, j, e, :], PS[:, b, 0:SEQ], ACT.Identity,
                                       scale=dcol("conv_w", 44 + 22 * e + 2 + j, i * 2),
                                       bias=dcol("conv_b", 22 * e + 2 + j, i * 2)).then_inc(*c.made(conv_mid))
                    act.wait_ge(*c.need(dve_freed, 2))
                    act.activation(cv1[:, 2 + j, 0, :], cv1[:, j, 0, :], ACT.Gelu_apprx_tanh).then_inc(*c.made(gate_act))
            c.skip(conv_done, 2)
            tile[0] += 2 * FFT
            passed(KT)
            c.skip(dve_freed, KT)
            stage()

            for l in range(LAYERS):
                halves = 2 if l == 0 else 1
                q_cols = halves * SEQ
                ny = len(y_chunks(l))
                passed(N_MOD)
                norm(T)
                act.wait_ge(*c.need(mods_ready))
                shift(l, 0, 2)
                unloads(KT, lambda j: qT[:, bass.ds(j, 1), 0:q_cols], q_cols, scale=HD ** -0.5)
                unloads(KT, lambda j: kT[:, bass.ds(j, 1), :], T)
                with c.loop(4, [(tile_ready, 4), (act_freed, 4)]) as i:
                    for t in range(TT):
                        unload(v2[:, t:t + 1, bass.ds(i * 256, 256)], 256)

                units = units2(l)

                def exp2(u):
                    h, q = units[u]
                    nk = T if q < LT else SEQ
                    act.wait_ge(*c.need(max_ready))
                    if u >= 2:
                        act.wait_ge(*c.need(a_ready))
                    for e in range(2):
                        act.activation(prob[:, u % 2, e * T:e * T + nk], PS[:, 2 * (u % 2) + e, 0:nk], ACT.Exp,
                                       bias=stat[:, 2 * u + e:2 * u + e + 1],
                                       accum_out=stat[:, 64 + 2 * u + e:65 + 2 * u + e]).then_inc(*c.made(p_ready))

                n_u = len(units)
                for u in range(n_u + 1):
                    if u < n_u:
                        exp2(u)
                    if u >= 1:
                        weightsT(u - 1, T if units[u - 1][1] < LT else SEQ)
                c.skip(a_ready, 2)
                c.skip(o_ready, 2)
                act.wait_ge(*c.need(o_done, n_u))
                for h in range(HEADS):
                    for t in range(ny):
                        act.activation(junk[:, 0:P], o2[:, t, h * P:(h + 1) * P], ACT.Square,
                                       accum_out=stat[:, 128 + t * HEADS + h:129 + t * HEADS + h]).then_inc(*c.made(act_step))
                        act.wait_ge(*c.sofar(act_step))
                act.activation(stat[:, 160:160 + ny * HEADS], stat[:, 128:128 + ny * HEADS], ACT.Sqrt, scale=1.0 / P,
                               bias=eps[:, 0:1]).then_inc(*c.made(tok_rms))
                c.skip(tok_scaled, ny)
                for f in range(KT):
                    turned_to(attT[:, f, 0:ny * P], ny * P, col("attn_subln_g_2", l))
                stage()

                passed(TT)
                c.skip(dve_freed, TT)
                act.wait_ge(*c.need(dt_abs))
                act.activation(dtx[1][:, :, :], dtx[0][:, :, :], ACT.Abs).then_inc(*c.made(act_step))
                act.wait_ge(*c.sofar(act_step))
                act.activation(dtx[2][:, :, :], dtx[1][:, :, :], ACT.Exp, scale=-1.0).then_inc(*c.made(dt_exp))
                act.wait_ge(*c.need(dt_one))
                act.activation(dtx[4][:, :, :], dtx[3][:, :, :], ACT.Ln).then_inc(*c.made(dt_ln))
                for t in range(TT):
                    act.wait_ge(*c.need(dec_ready))
                    act.activation(edec[:, t, :], PS[:, t, 0:192], ACT.Exp)\
                        .then_inc(*c.made(dec_exp))
                stage()

                nz = ny // 2
                cw = rows["conv_w_2"] + l * 160
                cb = rows["conv_b_2"] + l * 32

                def group(g):
                    for j in range(4):
                        act.wait_ge(*c.need(tile_ready))
                        step, off = (2, j) if j < 2 else (1, 16 + 8 * (j - 2))
                        act.activation(chan[:, j, :], PS[:, j, :], ACT.Identity, scale=V[:, bass.ds(g * step + (cw + 64 + off), 1)],
                                       bias=V[:, bass.ds(g * step + (cb + off), 1)]).then_inc(*c.made(conv_mid))
                        act.wait_ge(*c.need(dve_freed))
                        if j >= 2:
                            act.wait_ge(*c.need(chan_ready))
                        act.activation(ctanh[:, j % 2, :], chan[:, j, :], ACT.Tanh).then_inc(*c.made(conv_tanh))
                    c.skip(chan_ready, 2)
                    for b in range(nz):
                        act.wait_ge(*c.need(tile_ready))
                        act.activation(sz[:, 2 * b:2 * b + 2, :], PS[:, b, :].rearrange("p (t n) -> p t n", t=2), ACT.Tanh,
                                       scale=0.5).then_inc(*c.made(z_tanh))
                    c.skip(dve_freed, nz)
                    for n in range(2):
                        act.wait_ge(*c.need(tok_turned))
                        act.activation(xtok[:, 2 * n:2 * n + 2, :], PS[:, 4 + n, :].rearrange("p (t n) -> p t n", t=2), ACT.Copy)\
                            .then_inc(*c.made(tok_ready))
                    act.wait_ge(*c.need(tok_turned))
                    act.activation(btok[:, :, :], PS[:, 6, :].rearrange("p (t n) -> p t n", t=TT), ACT.Copy)\
                        .then_inc(*c.made(tok_ready))
                    for t in range(ny):
                        act.wait_ge(*c.need(seg_ready))
                        if t >= 2:
                            act.wait_ge(*c.need(m_ready))
                        act.activation(ex[:, t % 2, :], PS[:, (3, 7)[t % 2], :], ACT.Exp).then_inc(*c.made(e_ready))
                    c.skip(m_ready, 2)

                with c.loop(GROUPS, [(tile_ready, 4 + nz), (conv_mid, 4), (dve_freed, 4 + nz), (chan_ready, 4), (conv_tanh, 4),
                                     (z_tanh, nz), (tok_turned, 3), (tok_ready, 3), (seg_ready, ny), (m_ready, ny),
                                     (e_ready, ny)]) as g:
                    act.wait_ge(*c.need(y_done, 0)) if False else None
                    group(g)
                tile[0] += (4 + nz) * GROUPS
                stage()
                for t in range(ny):
                    act.activation(junk, yg[:, t, :], ACT.Square, accum_out=stat[:, 128 + t:129 + t]).then_inc(*c.made(act_step))
                    act.wait_ge(*c.sofar(act_step))
                act.activation(stat[:, 160:160 + ny], stat[:, 128:128 + ny], ACT.Sqrt, scale=1.0 / SSD_IN, bias=eps[:, 0:1])\
                    .then_inc(*c.made(tok_rms))
                c.skip(tok_scaled, ny)
                for f in range(YT):
                    turned_to(yT[:, f, 0:ny * P], ny * P, col("ssd_norm_g_2", l * YT + f))
                stage()
                unloads(KT, lambda j: merged[:, bass.ds(j, 1), 0:q_cols], q_cols, ACT.Tanh, 0.5)
                passed(KT)
                unloads(KT, lambda j: gs[:, bass.ds(j, 1), 0:q_cols], q_cols, ACT.Tanh, 0.5)
                passed(2 * KT)
                c.skip(gated, KT)
                stage()
                norm(q_cols)
                shift(l, 24, halves)
                c.skip(dve_freed, 3 * KT)
                for n in range(HIDT):
                    act.wait_ge(*c.need(dve_freed))
                    h = hidden(n)[:, 0:q_cols]
                    act.activation(h, h, ACT.Square).then_inc(*c.made(hid_mid))
                passed(HIDT + KT)
                c.skip(dve_freed, KT)
                stage()

            norm(SEQ)
            c.skip(scaled, KT)
            res = view(big2, 0, LT, D)
            for t in range(LT):
                for b in range(2):
                    bk = 4 + bank4[0] % 4
                    bank4[0] += 1
                    act.wait_ge(*c.need(turned))
                    act.activation(res[:, t, 512 * b:512 * (b + 1)], PS[:, bk, :], ACT.Copy).then_inc(*c.made(out_ready))

        def act_total(l, n):
            return 20 + l * (8 + 8 + 16 + 16) + 32 + 8 * n

        @block.vector
        def _(dve):
            c = Counts(dve)
            tile, fences = [0], [0]

            def stage():
                dve.drain().then_inc(*c.made(fence))
                fences[0] += 1
                dve.wait_ge(fence, 4 * fences[0])

            def settle(sem=None):
                dve.wait_ge(*c.sofar(sem or dve_step))

            def step(ins):
                return ins.then_inc(*c.made(dve_step))

            def bc(ap, n, axis=2):
                return ap.unsqueeze(2).broadcast_to([P, ap.shape[1], n])

            def bc_mid(ap, n):
                return ap.unsqueeze(1).broadcast_to([P, n, ap.shape[1]])

            def norm(gain, cols):
                dve.wait_ge(*c.need(rms_ready))
                step(dve.reciprocal(rstd[:, 0:cols], rms[:, 0:cols]))
                settle()
                for k in range(KT):
                    for e in range(-(-cols // SEQ)):
                        r = slice(e * SEQ, (e + 1) * SEQ)
                        dve.scalar_tensor_tensor(out=hT[:, k, r], in0=xT[:, k, r], scalar=gain(k, e), in1=rstd[:, r],
                                                 op0=ALU.mult, op1=ALU.mult).then_inc(*c.made(scaled))

            def passed(n):
                c.skip(tile_ready, n)
                tile[0] += n

            def next_tile():
                b = tile[0] % 4
                tile[0] += 1
                dve.wait_ge(*c.need(tile_ready))
                return b

            dve.memset(eps[:, :], EPS).then_inc(*c.made(vec_ready))
            dve.wait_ge(small_loaded, 16 * 9 * LAYERS)
            for l in range(LAYERS):
                for n in range(2):
                    pr = view(big1, (2 * l + n) * HD, HD)
                    step(dve.tensor_tensor(pr, lam_in[:, l, 2 * n, :], lam_in[:, l, 2 * n + 1, :], ALU.mult))
                    settle()
                    ins = dve.reduce_sum(lam_s[:, 2 * l + n:2 * l + n + 1], pr, AX.X)
                    if l == LAYERS - 1 and n == 1:
                        ins.then_inc(*c.made(lam_sum))
                    else:
                        step(ins)
            dve.wait_ge(*c.need(lam_exp))
            step(dve.tensor_tensor(lam_s[:, 8:10], lam_s[:, 5:8:2], lam_s[:, 4:8:2], ALU.subtract))
            settle()
            for l in range(LAYERS):
                lam_init = 0.8 - 0.6 * float(np.exp(-0.3 * l))
                step(dve.tensor_scalar(neg_lam[:, l:l + 1], lam_s[:, 8 + l:9 + l], -lam_init, None, ALU.add))
            dve.wait_ge(*c.need(lam_exp))
            step(dve.tensor_scalar(neg_a[:, :, :], neg_a[:, :, :], -1.0, None, ALU.mult))
            dve.wait_ge(*c.need(cond_tanh))
            step(dve.scalar_tensor_tensor(out=craw[:, :, :], in0=ctan[:, :, :], scalar=1.0, in1=craw[:, :, :],
                                          op0=ALU.add, op1=ALU.mult))
            settle()
            dve.tensor_scalar(cact[:, :, :], craw[:, :, :], 0.5, None, ALU.mult).then_inc(*c.made(cond_ready))
            n_c2 = LAYERS * 6 * 32
            half_conv = V[:, rows["conv_w_2"]:rows["conv_w_2"] + n_c2]
            step(dve.tensor_scalar(half_conv, half_conv, 0.5, None, ALU.mult))
            q_gain = V[:, rows["qa_norm_g"]:rows["qa_norm_g"] + 2]
            step(dve.tensor_scalar(q_gain, q_gain, HD ** -0.5, None, ALU.mult))
            stage()

            norm(lambda k, e: col("norm1_g", k), SEQ)
            passed(20)
            gains = ["qa_norm_g"] * 4 + ["ka_norm_g"] * 2 + ["qb_norm_g"] * 4 + ["kb_norm_g"] * 4
            for n in range(7):
                dve.wait_ge(*c.need(head_rms))
                step(dve.reciprocal(sq1[:, 2 * n:2 * n + 2, :], sq1[:, 2 * n:2 * n + 2, :]))
                settle()
                for j in (2 * n, 2 * n + 1):
                    dve.scalar_tensor_tensor(out=raw1[:, j, :], in0=raw1[:, j, :], scalar=col(gains[j]), in1=sq1[:, j, :],
                                             op0=ALU.mult, op1=ALU.mult).then_inc(*c.made(head_normed))
            settle(head_normed)
            for n in range(3):
                dve.wait_ge(*c.need(rot_ready))
                t2 = rot1[:, n, :].rearrange("p (a b) -> p a b", a=2)
                src = raw1[:, 2 * n:2 * n + 2, :]
                step(dve.tensor_tensor(t2, PS[:, n, :].rearrange("p (a b) -> p a b", a=2), bc_mid(sin1, 2), ALU.mult))
                step(dve.tensor_tensor(src, src, bc_mid(cos1, 2), ALU.mult))
                settle()
                dve.tensor_tensor(src, src, t2, ALU.add).then_inc(*c.made(rot_done))

            n_u = len(UNITS1)

            def max1(u):
                kind, hp, q = UNITS1[u]
                dve.wait_ge(*c.need(s_ready))
                if kind == "A":
                    src = PS[:, 2 * (u % 2):2 * (u % 2) + 2, 0:SEQ]
                else:
                    for e in range(2):
                        slope = 2.0 ** -(2 * hp + e + 1)
                        if u - 2 >= 8 and e == 0:
                            dve.wait_ge(p_ready, u - 1)
                        step(dve.scalar_tensor_tensor(out=atmp[:, u % 2, e * SEQ:(e + 1) * SEQ], in0=far[q], scalar=slope,
                                                      in1=PS[:, 2 * (u % 2) + e, 0:SEQ], op0=ALU.mult, op1=ALU.add))
                    settle()
                    src = atmp[:, u % 2, :].rearrange("p (a b) -> p a b", a=2)
                dve.tensor_reduce(stat[:, 2 * u:2 * u + 2], src, AX.X, ALU.max, negate=True).then_inc(*c.made(max_ready))

            def weights1(u):
                kind, hp, q = UNITS1[u]
                dve.wait_ge(*c.need(p_ready))
                if u >= 2:
                    dve.wait_ge(*c.need(t_ready))
                src = prob[:, u % 2, 0:T]
                dst = amat[:, u % 2, :]
                rs = stat[:, 64 + 2 * u:66 + 2 * u]
                if kind == "A":
                    step(dve.reciprocal(stat[:, 160 + 2 * u:162 + 2 * u], rs))
                    dve.tensor_copy(dst, src).then_inc(*c.made(a_ready))
                else:
                    for e in range(2):
                        r = slice(e * SEQ, (e + 1) * SEQ)
                        ins = dve.scalar_tensor_tensor(out=dst[:, r], in0=src[:, r], scalar=1.0, in1=times_seen[q],
                                                       op0=ALU.mult, op1=ALU.mult, accum_out=rs[:, e:e + 1])
                        if e:
                            ins.then_inc(*c.made(a_ready))
                    settle(a_ready)
                    step(dve.reciprocal(stat[:, 160 + 2 * u:162 + 2 * u], rs))

            def out1(u):
                kind, hp, q = UNITS1[u]
                dve.wait_ge(*c.need(o_ready))
                c0 = (0 if kind == "A" else 512) + 2 * hp * HD
                dve.tensor_tensor(o1[:, q, c0:c0 + 2 * HD].rearrange("p (a b) -> p a b", a=2),
                                  PS[:, 6 + u % 2, 0:2 * HD].rearrange("p (a b) -> p a b", a=2),
                                  bc(stat[:, 160 + 2 * u:162 + 2 * u], HD), ALU.mult).then_inc(*c.made(o_done))

            for u in range(n_u + 2):
                if u < n_u:
                    max1(u)
                if 1 <= u <= n_u:
                    weights1(u - 1)
                if u >= 2:
                    settle()
                    out1(u - 2)
            c.skip(t_ready, 2)
            dve.wait_ge(*c.need(tok_rms))
            step(dve.reciprocal(stat[:, 144:148], stat[:, 136:140]))
            settle()
            settle(o_done)
            for t in range(LT):
                for e in range(2):
                    h = o1[:, t, e * 512:(e + 1) * 512]
                    dve.tensor_scalar(h, h, stat[:, 144 + 2 * t + e:145 + 2 * t + e], None, ALU.mult).then_inc(*c.made(tok_scaled))
            for k in range(KT):
                b = next_tile()
                dve.tensor_tensor(xT[:, k, 0:SEQ], xT[:, k, 0:SEQ], PS[:, b, 0:SEQ], ALU.add).then_inc(*c.made(dve_freed))
            stage()
            norm(lambda k, e: col("norm2_g", k), SEQ)

            tile0 = tile[0]
            with c.loop(FFT // 2, [(tile_ready, 4), (conv_mid, 4), (dve_step, 4), (dve_freed, 4), (gate_act, 2), (conv_done, 2)]) as i:
                for j in range(2):
                    for e in range(2):
                        b = (tile0 + 2 * j + e) % 4
                        dve.wait_ge(*c.need(conv_mid))
                        c.skip(tile_ready)
                        cv = cv1[:, j, e, :]
                        step(dve.scalar_tensor_tensor(out=cv[:, 1:SEQ], in0=PS[:, b, 0:SEQ - 1],
                                                      scalar=dcol("conv_w", 22 * e + j, i * 2), in1=cv[:, 1:SEQ],
                                                      op0=ALU.mult, op1=ALU.add))
                        settle()
                        dve.scalar_tensor_tensor(out=cv[:, 0:SEQ - 1], in0=PS[:, b, 1:SEQ],
                                                 scalar=dcol("conv_w", 88 + 22 * e + j, i * 2), in1=cv[:, 0:SEQ - 1],
                                                 op0=ALU.mult, op1=ALU.add).then_inc(*c.made(dve_freed))
                    dve.wait_ge(*c.need(gate_act))
                    settle(dve_freed)
                    dve.tensor_tensor(gate1[:, bass.ds(i * 2 + j, 1), :], cv1[:, 2 + j, 0:1, :], cv1[:, j, 1:2, :], ALU.mult)\
                        .then_inc(*c.made(conv_done))
            tile[0] += 2 * FFT
            for k in range(KT):
                b = next_tile()
                dve.tensor_tensor(xT[:, k, 0:SEQ], xT[:, k, 0:SEQ], PS[:, b, 0:SEQ], ALU.add).then_inc(*c.made(dve_freed))
            stage()

            for l in range(LAYERS):
                halves = 2 if l == 0 else 1
                q_cols = halves * SEQ
                ny = len(y_chunks(l))
                dve.wait_ge(*c.need(tile_ready, N_MOD))
                tile[0] += N_MOD
                ab = V[:, rows["ada_b_2"] + l * N_MOD:rows["ada_b_2"] + (l + 1) * N_MOD]
                step(dve.tensor_tensor(mod[:, :, :], PS[:, 5, 0:2 * N_MOD].rearrange("p (m e) -> p m e", e=2), bc(ab, 2), ALU.add))
                settle()
                for dst, m0, name in ((amix, 8, "norm_mix_g_2"), (amlp, 32, "norm_mlp_g_2")):
                    g0 = rows[name] + l * KT
                    step(dve.scalar_tensor_tensor(out=dst[:, :, :], in0=mod[:, m0:m0 + KT, :], scalar=1.0, in1=bc(V[:, g0:g0 + KT], 2),
                                                  op0=ALU.add, op1=ALU.mult))
                dve.tensor_scalar(hgate[:, :, :], mod[:, 16:24, :], 0.5, None, ALU.mult).then_inc(*c.made(mods_ready))
                settle(mods_ready)
                norm(lambda k, e: amix[:, k, e:e + 1], T)

                passed(8 + 8)
                for n in range(2 * KT):
                    h = (qT if n < KT else kT)[:, n % KT, 0:SEQ]
                    dve.wait_ge(*c.need(rot_ready))
                    if n >= 2:
                        settle(rot_done)
                    step(dve.tensor_tensor(rot2[:, n % 2, :], PS[:, 4 + n % 4, 0:SEQ], sin2, ALU.mult))
                    step(dve.tensor_tensor(h, h, cos2, ALU.mult))
                    settle()
                    dve.tensor_tensor(h, h, rot2[:, n % 2, :], ALU.add).then_inc(*c.made(rot_done))
                passed(16)

                units = units2(l)
                n_u = len(units)

                def max2(u):
                    nk = T if units[u][1] < LT else SEQ
                    b = 2 * (u % 2)
                    dve.wait_ge(*c.need(s_ready))
                    dve.tensor_reduce(stat[:, 2 * u:2 * u + 2], PS[:, b:b + 2, 0:nk], AX.X, ALU.max, negate=True)\
                        .then_inc(*c.made(max_ready))

                def weights2(u):
                    nk = T if units[u][1] < LT else SEQ
                    dve.wait_ge(*c.need(p_ready, 2))
                    s0, s1 = (stat[:, 64 + 2 * u + e:65 + 2 * u + e] for e in range(2))
                    r0, r1 = (stat[:, 128 + 2 * u + e:129 + 2 * u + e] for e in range(2))
                    step(dve.reciprocal(stat[:, 128 + 2 * u:130 + 2 * u], stat[:, 64 + 2 * u:66 + 2 * u]))
                    settle()
                    step(dve.scalar_tensor_tensor(out=r1, in0=r1, scalar=neg_lam[:, l:l + 1], in1=s0, op0=ALU.mult, op1=ALU.mult))
                    settle()
                    if u >= 2:
                        dve.wait_ge(*c.need(t_ready))
                    dve.scalar_tensor_tensor(out=amat[:, u % 2, 0:nk], in0=prob[:, u % 2, T:T + nk], scalar=r1,
                                             in1=prob[:, u % 2, 0:nk], op0=ALU.mult, op1=ALU.add).then_inc(*c.made(a_ready))

                def out2(u):
                    h, q = units[u]
                    dve.wait_ge(*c.need(o_ready))
                    dve.tensor_scalar(o2[:, q, h * P:(h + 1) * P], PS[:, 6 + u % 2, 0:P], stat[:, 128 + 2 * u:129 + 2 * u], None,
                                      ALU.mult).then_inc(*c.made(o_done))

                for u in range(n_u + 2):
                    if u < n_u:
                        max2(u)
                    if 1 <= u <= n_u:
                        weights2(u - 1)
                    if u >= 2:
                        out2(u - 2)
                c.skip(t_ready, 2)
                dve.wait_ge(*c.need(tok_rms))
                lam_init = 0.8 - 0.6 * float(np.exp(-0.3 * l))
                n_st = ny * HEADS
                step(dve.reciprocal(stat[:, 192:192 + n_st], stat[:, 160:160 + n_st]))
                settle()
                step(dve.tensor_scalar(stat[:, 192:192 + n_st], stat[:, 192:192 + n_st], 1.0 - lam_init, None, ALU.mult))
                settle()
                settle(o_done)
                for t in range(ny):
                    h = o2[:, t, :].rearrange("p (h e) -> p h e", h=HEADS)
                    dve.tensor_tensor(h, h, bc(stat[:, 192 + t * HEADS:192 + (t + 1) * HEADS], P), ALU.mult)\
                        .then_inc(*c.made(tok_scaled))
                stage()

                for t in range(TT):
                    b = next_tile()
                    dve.tensor_tensor(dtx[0][:, t, :], PS[:, b, 0:64], head_in[:, l, 0:64], ALU.add).then_inc(*c.made(dve_freed))
                settle(dve_freed)
                step(dve.tensor_scalar(dt[:, :, :], dtx[0][:, :, :], 0.0, None, ALU.max).then_inc(*c.made(dt_abs))) if False else \
                    dve.tensor_scalar(dt[:, :, :], dtx[0][:, :, :], 0.0, None, ALU.max).then_inc(*c.made(dt_abs))
                dve.wait_ge(*c.need(dt_exp))
                dve.tensor_scalar(dtx[3][:, :, :], dtx[2][:, :, :], 1.0, None, ALU.add).then_inc(*c.made(dt_one))
                settle(dt_one)
                step(dve.scalar_tensor_tensor(out=dtx[5][:, :, :], in0=dtx[3][:, :, :], scalar=-1.0, in1=dtx[2][:, :, :],
                                              op0=ALU.add, op1=ALU.subtract))
                step(dve.reciprocal(dtx[1][:, :, :], dtx[3][:, :, :]))
                settle()
                step(dve.tensor_tensor(dtx[5][:, :, :], dtx[5][:, :, :], dtx[1][:, :, :], ALU.mult))
                dve.wait_ge(*c.need(dt_ln))
                settle()
                step(dve.tensor_tensor(dtx[4][:, :, :], dtx[4][:, :, :], dtx[5][:, :, :], ALU.subtract))
                settle()
                step(dve.tensor_tensor(dt[:, :, :], dt[:, :, :], dtx[4][:, :, :], ALU.add))
                settle()
                dve.tensor_tensor(dta[:, :, :], dt[:, :, :], bc_mid(neg_a[:, l, :], TT), ALU.mult).then_inc(*c.made(dta_ready))
                for t in range(TT):
                    step(dve.tensor_copy(by_head[:, t, 192:224], head_in[:, l, 128:160]))
                dve.wait_ge(*c.need(dec_exp, TT))
                for e in range(2):
                    step(dve.tensor_tensor(wst[:, :, 32 * e:32 * e + 32], dt[:, :, 32 * e:32 * e + 32],
                                           edec[:, :, 64 * e:64 * e + 32], ALU.mult))
                stage()

                nz = ny // 2
                cw = rows["conv_w_2"] + l * 160

                def heads_of(buf, t, c0, g, n=HD):
                    return buf[:, t, bass.ds(g * GH + c0, GH)].unsqueeze(2).broadcast_to([P, GH, n])

                def per_head(ap):
                    return ap.rearrange("p (r n) -> p r n", r=GH)

                def group(g):
                    for j in range(4):
                        st, off = (2, j) if j < 2 else (1, 16 + 8 * (j - 2))
                        u = PS[:, j, :].rearrange("p (s t) -> p s t", s=2)
                        cv = chan[:, j, :].rearrange("p (s t) -> p s t", s=2)
                        dve.wait_ge(*c.need(conv_mid))
                        c.skip(tile_ready)
                        for n, d in enumerate((-2, -1, 1, 2)):
                            to, fr = slice(max(0, -d), SEQ - max(0, d)), slice(max(0, d), SEQ - max(0, -d))
                            ins = dve.scalar_tensor_tensor(out=cv[:, :, to], in0=u[:, :, fr],
                                                           scalar=V[:, bass.ds(g * st + (cw + 32 * (d + 2) + off), 1)],
                                                           in1=cv[:, :, to], op0=ALU.mult, op1=ALU.add)
                            if n < 3:
                                step(ins)
                                settle()
                            else:
                                ins.then_inc(*c.made(dve_freed))
                        settle(dve_freed)
                        dve.wait_ge(*c.need(conv_tanh))
                        dve.scalar_tensor_tensor(out=chan[:, j, :], in0=ctanh[:, j % 2, :], scalar=1.0, in1=chan[:, j, :],
                                                 op0=ALU.add, op1=ALU.mult).then_inc(*c.made(chan_ready))
                    for b in range(nz):
                        dve.wait_ge(*c.need(z_tanh))
                        c.skip(tile_ready)
                        h = sz[:, 2 * b:2 * b + 2, :]
                        dve.scalar_tensor_tensor(out=h, in0=h, scalar=1.0, in1=PS[:, b, :].rearrange("p (t n) -> p t n", t=2),
                                                 op0=ALU.add, op1=ALU.mult).then_inc(*c.made(dve_freed))
                    dve.wait_ge(*c.need(cb_ready))
                    cbp = PS[:, 7, 0:ny * P].rearrange("p (t l) -> p t l", t=ny)
                    step(dve.tensor_tensor(cb_lo[:, 0:ny, :], cbp, bc_mid(t_le, ny), ALU.mult))
                    dve.tensor_tensor(cb_up[:, 0:ny, :], cbp, bc_mid(t_ge, ny), ALU.mult).then_inc(*c.made(cb_masked))
                    settle(cb_masked)

                    def weights(t):
                        lo = dt_lo[:, :, :]
                        step(dve.tensor_tensor(lo, bc_mid(cb_lo[:, t, :], GH), heads_of(dt, t, 0, g, P), ALU.mult))
                        dve.wait_ge(*c.need(dtu_ready))
                        settle()
                        step(dve.tensor_tensor(per_head(dt_up[:, t % 2, :]), lo, per_head(dt_up[:, t % 2, :]), ALU.add))
                        dve.wait_ge(*c.need(e_ready))
                        settle()
                        if t >= 2:
                            dve.wait_ge(*c.need(y_ready, 0))
                        dve.tensor_tensor(mt[:, t % 2, :], dt_up[:, t % 2, :], ex[:, t % 2, :], ALU.mult).then_inc(*c.made(m_ready))

                    weights(0)
                    weights(1)
                    dve.wait_ge(*c.need(st_ready))
                    st = [PS[:, 4 + n // 2, (n % 2) * GW:(n % 2 + 1) * GW] for n in range(6)]
                    for d in range(2):
                        step(dve.tensor_copy(hin[:, 3 * d, :], st[3 * d]))
                    for n in range(1, 3):
                        for d, order in enumerate((F_STATES, B_STATES)):
                            settle()
                            h = hin[:, 3 * d + n, :]
                            step(dve.tensor_tensor(per_head(h), per_head(hin[:, 3 * d + n - 1, :]),
                                                   heads_of(edec, order[n], 128 + 32 * d, g), ALU.mult))
                            settle()
                            ins = dve.tensor_tensor(h, h, st[3 * d + n], ALU.add)
                            if n == 2 and d == 1:
                                ins.then_inc(*c.made(hin_ready))
                            else:
                                step(ins)
                    for t in range(ny):
                        b = t % 2
                        dve.wait_ge(*c.need(y_ready))
                        dve.wait_ge(*c.need(xd_ready))
                        if t:
                            settle(y_done)
                        step(dve.tensor_tensor(ys, PS[:, b, 0:GW], xd[:, b, :], ALU.add))
                        for d, hs in enumerate((HF, HB)):
                            if t in hs:
                                settle()
                                step(dve.tensor_tensor(per_head(yi), per_head(PS[:, 4 + b, d * GW:(d + 1) * GW]),
                                                       heads_of(edec, t, 32 + 64 * d, g), ALU.mult))
                                settle()
                                step(dve.tensor_tensor(ys, ys, yi, ALU.add))
                        settle()
                        dve.scalar_tensor_tensor(out=yg[:, t, bass.ds(g * GW, GW)], in0=ys, scalar=0.5, in1=sz[:, t, :],
                                                 op0=ALU.mult, op1=ALU.mult).then_inc(*c.made(y_done))
                        if t + 2 < ny:
                            weights(t + 2)

                n_steps = 4 * 3 + 1 + 2 * ny + 2 + 7 + sum(1 + 2 * ((t in HF) + (t in HB)) for t in range(ny))
                with c.loop(GROUPS, [(tile_ready, 4 + nz), (conv_mid, 4), (dve_step, n_steps), (dve_freed, 4 + nz),
                                     (conv_tanh, 4), (chan_ready, 4), (z_tanh, nz), (cb_ready, 1), (cb_masked, 1),
                                     (dtu_ready, ny), (e_ready, ny), (m_ready, ny), (st_ready, 1), (hin_ready, 1),
                                     (y_ready, ny), (xd_ready, ny), (y_done, ny)]) as g:
                    group(g)
                tile[0] += (4 + nz) * GROUPS
                stage()
                dve.wait_ge(*c.need(tok_rms))
                step(dve.reciprocal(stat[:, 192:192 + ny], stat[:, 160:160 + ny]))
                settle()
                for t in range(ny):
                    dve.tensor_scalar(yg[:, t, :], yg[:, t, :], stat[:, 192 + t:193 + t], None, ALU.mult).then_inc(*c.made(tok_scaled))
                stage()

                def gate(dst):
                    with c.loop(2, [(tile_ready, 4), (dve_freed, 4)]) as i:
                        for j in range(4):
                            b = next_tile()
                            h = dst[:, bass.ds(i * 4 + j, 1), 0:q_cols]
                            dve.scalar_tensor_tensor(out=h, in0=h, scalar=1.0, in1=PS[:, b:b + 1, 0:q_cols], op0=ALU.add,
                                                     op1=ALU.mult).then_inc(*c.made(dve_freed))

                passed(KT)
                dve.wait_ge(act_freed, act_total(l, 1))
                gate(merged)
                passed(KT)
                dve.wait_ge(act_freed, act_total(l, 2))
                gate(gs)
                settle(dve_freed)
                for k in range(KT):
                    dve.tensor_tensor(merged[:, k, 0:q_cols], merged[:, k, 0:q_cols], gs[:, k, 0:q_cols], ALU.add)\
                        .then_inc(*c.made(gated))

                def add_gated(gate_of):
                    for k in range(KT):
                        b = next_tile()
                        for e in range(halves):
                            r = slice(e * SEQ, (e + 1) * SEQ)
                            ins = dve.scalar_tensor_tensor(out=xT[:, k, r], in0=PS[:, b, r], scalar=gate_of(k, e), in1=xT[:, k, r],
                                                           op0=ALU.mult, op1=ALU.add)
                            if e == halves - 1:
                                ins.then_inc(*c.made(dve_freed))

                add_gated(lambda k, e: hgate[:, k, e:e + 1])
                stage()
                norm(lambda k, e: amlp[:, k, e:e + 1], q_cols)
                for n in range(HIDT):
                    b = next_tile()
                    dve.tensor_scalar(hidden(n)[:, 0:q_cols], PS[:, b, 0:q_cols], 0.0, None, ALU.max).then_inc(*c.made(dve_freed))
                add_gated(lambda k, e: mod[:, 40 + k, e:e + 1])
                stage()

            norm(lambda k, e: col("final_norm_g_2", k), SEQ)

        @block.gpsimd
        def _(pool):
            c = Counts(pool)
            fences = [0]

            def stage():
                pool.drain().then_inc(*c.made(fence))
                fences[0] += 1
                pool.wait_ge(fence, 4 * fences[0])

            def bc_mid(ap, n):
                return ap.unsqueeze(1).broadcast_to([P, n, ap.shape[1]])

            def heads_of(t, kind, n):
                return of_group[:, t, kind, :].unsqueeze(2).broadcast_to([P, GH, n])

            def per_head(ap):
                return ap.rearrange("p (r n) -> p r n", r=GH)

            stage()
            stage()
            stage()
            for l in range(LAYERS):
                ny = len(y_chunks(l))
                stage()
                stage()

                def group(g):
                    pool.tensor_copy(of_group[:, :, :, :].rearrange("p t k r -> p (t k) r"),
                                     by_head[:, :, :].rearrange("p t (k n) -> p (t k) n", k=7)[:, :, bass.ds(g * GH, GH)])\
                        .then_inc(*c.made(pool_step))
                    pool.wait_ge(*c.sofar(pool_step))

                    def seg(t):
                        if t >= 2:
                            pool.wait_ge(*c.need(seg_ready))
                        pool.tensor_tensor(seg_f[:, t % 2, :, :], bc_mid(t_le, GH), heads_of(t, 2, P), ALU.mult)\
                            .then_inc(*c.made(seg_in))
                        pool.tensor_tensor(seg_b[:, t % 2, :, :], bc_mid(t_ge, GH), heads_of(t, 3, P), ALU.mult)\
                            .then_inc(*c.made(seg_in))

                    def dtu(t):
                        if t >= 2:
                            pool.wait_ge(*c.need(m_ready))
                        pool.tensor_tensor(per_head(dt_up[:, t % 2, :]), bc_mid(cb_up[:, t, :], GH), heads_of(t, 1, P),
                                           ALU.mult).then_inc(*c.made(dtu_ready))

                    def skip_of(t):
                        if t >= 2:
                            pool.wait_ge(*c.need(y_done))
                        pool.tensor_tensor(per_head(xd[:, t % 2, :]), per_head(xtok[:, t, :]),
                                           heads_of(t, 6, HD),
                                           ALU.mult).then_inc(*c.made(xd_ready))

                    seg(0)
                    seg(1)
                    pool.wait_ge(*c.need(tok_ready, 3))
                    for n, t in enumerate(F_STATES + B_STATES):
                        pool.tensor_tensor(per_head(xw[:, n, :]), per_head(xtok[:, t, :]), heads_of(t, 4 + n // 3, HD),
                                           ALU.mult).then_inc(*c.made(xw_ready))
                    pool.wait_ge(*c.need(cb_masked))
                    for t in range(2):
                        dtu(t)
                        skip_of(t)
                    for t in range(2, ny):
                        seg(t)
                        dtu(t)
                        skip_of(t)
                    c.skip(seg_ready, 2)
                    c.skip(m_ready, 2)
                    pool.wait_ge(*c.need(y_done, 2))

                with c.loop(GROUPS, [(pool_step, 1), (seg_in, 2 * ny), (tok_ready, 3), (xw_ready, 6), (cb_masked, 1), (dtu_ready, ny), (xd_ready, ny),
                                     (seg_ready, ny), (m_ready, ny), (y_done, ny)]) as g:
                    group(g)
                for _ in range(4):
                    stage()


_INS = [
    "x", "norm1_g", "w_in", "qa_norm_g", "ka_norm_g", "qb_norm_g", "kb_norm_g", "outa_norm_g", "outb_norm_g",
    "w_out", "norm2_g", "w_up", "conv_w", "conv_b", "w_down", "c_2", "ctx_2", "c_ctx_2", "ada_w_2", "ada_b_2",
    "norm_mix_g_2", "w_in_2", "conv_w_2", "conv_b_2", "dt_bias_f_2", "dt_bias_b_2", "a_log_f_2", "a_log_b_2",
    "ssd_d_2", "ssd_norm_g_2", "lambda_q1_2", "lambda_k1_2", "lambda_q2_2", "lambda_k2_2", "attn_subln_g_2",
    "w_attn_o_2", "w_ssd_o_2", "w_out_2", "norm_mlp_g_2", "w_mlp1_2", "w_mlp2_2", "final_norm_g_2",
]
_OUT = (1, SEQ, D)


def kernel(**inputs):
    import concourse.bacc as _bacc
    from concourse.bass_utils import run_bass_kernel_spmd as _run

    nc = _bacc.Bacc("TRN2", target_bir_lowering=False, num_devices=1)
    arrays, aps = {}, {}
    for name in _INS:
        arr = np.ascontiguousarray(inputs[name])
        arrays[f"in_{name}_dram"] = arr
        aps[name] = nc.dram_tensor(f"in_{name}_dram", arr.shape, mybir.dt.from_np(arr.dtype), kind="ExternalInput").ap()
    table = shape_constants()
    arrays["in_shape_constants_dram"] = table
    const = nc.dram_tensor("in_shape_constants_dram", table.shape, F32, kind="ExternalInput").ap()
    out = nc.dram_tensor("out_0_dram", _OUT, F32, kind="ExternalOutput").ap()
    two_blocks(nc, aps, const, out)
    r = _run(nc, [arrays], core_ids=[0])
    return r.results[0]["out_0_dram"]
```

```python
from contextlib import ExitStack, contextmanager

import numpy as np

import concourse.bass as bass
from concourse import mybir

F32 = mybir.dt.float32
ALU = mybir.AluOpType
ACT = mybir.ActivationFunctionType
AX = mybir.AxisListType

P = 128
SEQ = 256
T = 2 * SEQ
D = 1024
KT = D // P
LT = SEQ // P
TT = T // P
HD = 64
HEADS = 8
D_FF = 2816
FFT = D_FF // P
EPS = 1e-6
LAYERS = 2
SSD_IN = 2048
GROUPS = 8
GH = 4
GW = GH * HD
SSD_HEADS = 32
HID = 4096
HIDT = HID // P
YT = SSD_IN // P
N_MOD = 48
SLOTS = 4
SLAB = 2048
C_Z, C_X, C_B, C_C, C_DT, C_GA, C_GS = 3072, 5120, 7168, 8192, 9216, 9280, 10304


def shape_constants():
    i, j = np.arange(P)[:, None], np.arange(P)[None, :]
    ident = (i == j).astype(np.float32)
    heads = (i // HD == j // HD).astype(np.float32)
    ones = np.ones((P, P), np.float32)

    def turn(half):
        m = np.zeros((P, P), np.float32)
        for p in range(P):
            if p % (2 * half) < half:
                m[p + half, p] = -1.0
            else:
                m[p - half, p] = 1.0
        return m

    row = np.repeat(np.arange(4, dtype=np.float32), 64)
    col = np.tile(np.arange(64, dtype=np.float32), 4)
    inv = np.float32(10000.0) ** (-np.arange(16, dtype=np.float32) / np.float32(16))
    ang1 = np.zeros((P, SEQ), np.float32)
    ang2 = np.zeros((P, SEQ), np.float32)
    for p in range(P):
        d = p % HD
        ang1[p] = (row if d < 32 else col) * inv[d % 16]
        e = p % 32
        ang2[p] = (row if e < 16 else col) * inv[e % 16]
    cols = [ident, heads, ones, turn(16), turn(32),
            (i > j), (i < j), (i <= j), (i >= j),
            np.cos(ang1), np.sin(ang1), np.cos(ang2), np.sin(ang2)]
    for q in range(LT):
        dist = np.abs(np.arange(SEQ)[None, :] - (q * P + np.arange(P))[:, None])
        count = (dist <= 64).astype(np.float32) + (dist % 4 == 0) + (dist % 16 == 0)
        cols += [np.where(count > 0, -dist, -1e30), count]
    return np.ascontiguousarray(np.concatenate([np.asarray(c, np.float32) for c in cols], axis=1))


class Counts:

    def __init__(self, eng):
        self.eng, self.n, self.i, self.per = eng, {}, None, {}

    def skip(self, sem, k=1):
        self.n[sem.name] = self.n.get(sem.name, 0) + k

    def value(self, sem):
        n = self.n.get(sem.name, 0)
        if self.i is not None and self.per.get(sem.name):
            return self.i * self.per[sem.name] + n
        return n

    def made(self, sem, k=1):
        self.skip(sem, k)
        return sem, k

    def need(self, sem, k=1):
        self.skip(sem, k)
        return sem, self.value(sem)

    def sofar(self, sem):
        return sem, self.value(sem)

    @contextmanager
    def loop(self, times, per):
        with self.eng.Fori(0, times) as i:
            start = dict(self.n)
            self.i, self.per = i, {s.name: k for s, k in per}
            yield i
            for name, n in self.n.items():
                moved = n - start.get(name, 0)
                assert moved == self.per.get(name, 0), (name, moved)
            for name, k in self.per.items():
                self.n[name] = start.get(name, 0) + k * times
            self.i, self.per = None, {}


def two_blocks(nc, a, const, out, upto=99):
    with ExitStack() as ctx:
        def sb(name, shape):
            return ctx.enter_context(nc.sbuf_tensor(name, shape, F32))

        def sem(name):
            return ctx.enter_context(nc.semaphore(name))

        PS = ctx.enter_context(nc.psum_tensor("PS", [P, 8, 512], F32))
        n_const = const.shape[1]
        K = sb("constants", [P, n_const])
        xT = sb("xT", [P, KT, T])
        hT = sb("hT", [P, KT, T])
        ring = sb("ring", [P, SLOTS, SLAB])
        big1 = sb("big1", [P, 8192])
        big2 = sb("big2", [P, 8192])
        mid_v = sb("mid_v", [P, 4096])
        mid_o = sb("mid_o", [P, 4096])
        mid_a = sb("mid_a", [P, 4096])

        def view(buf, at, *dims):
            n = int(np.prod(dims))
            flat = buf[:, at:at + n]
            if len(dims) == 1:
                return flat
            if len(dims) == 2:
                return flat.rearrange("p (a b) -> p a b", a=dims[0])
            return flat.rearrange("p (a b c) -> p a b c", a=dims[0], b=dims[1])

        ident, heads, ones, turn1, turn2, t_gt, t_lt, t_le, t_ge = (
            K[:, n * P:(n + 1) * P] for n in range(9))
        at = 9 * P
        cos1, sin1, cos2, sin2 = (K[:, at + n * SEQ:at + (n + 1) * SEQ] for n in range(4))
        at += 4 * SEQ
        far = [K[:, at + 2 * q * SEQ:at + (2 * q + 1) * SEQ] for q in range(LT)]
        times_seen = [K[:, at + (2 * q + 1) * SEQ:at + (2 * q + 2) * SEQ] for q in range(LT)]

        rows, pieces = {}, []
        n_rows = 0

        def vector(name, src):
            nonlocal n_rows
            rows[name] = n_rows
            n, k = src.shape[0], 0
            while k < n:
                m = min(n - k, P - n_rows % P)
                pieces.append((n_rows // P, n_rows % P, m, src[k:k + m, :]))
                n_rows += m
                k += m

        flat1 = "(a b) -> a b"
        flat2 = "l (a b) -> (l a) b"
        for name in ("norm1_g", "norm2_g", "conv_b", "c_ctx_2", "final_norm_g_2", "outa_norm_g", "outb_norm_g"):
            vector(name, a[name].rearrange(flat1, b=P))
        vector("conv_w", a["conv_w"].rearrange(flat2, b=P))
        for name in ("c_2", "ada_b_2", "norm_mix_g_2", "norm_mlp_g_2", "ssd_norm_g_2", "attn_subln_g_2"):
            vector(name, a[name].rearrange(flat2, b=P))
        vector("conv_w_2", a["conv_w_2"].rearrange("l t (a b) -> (l t a) b", b=P))
        vector("conv_b_2", a["conv_b_2"].rearrange(flat2, b=P))
        n_head_rows = n_rows
        for name in ("qa_norm_g", "qb_norm_g", "ka_norm_g", "kb_norm_g"):
            rows[name] = n_rows
            n_rows += 1
        n_stage = -(-n_rows // P)
        vstage = view(big2, 0, n_stage, P)
        V = sb("V", [P, n_rows])

        def col(name, j=0):
            return V[:, rows[name] + j:rows[name] + j + 1]

        def dcol(name, j, i):
            return V[:, bass.ds(i + (rows[name] + j), 1)]

        lam_in = sb("lam_in", [P, LAYERS, 4, HD])
        lam_s = sb("lam_s", [P, 3 * LAYERS * 2])
        neg_lam = sb("neg_lam", [P, LAYERS])
        head_in = sb("head_in", [P, LAYERS, 5 * SSD_HEADS])
        neg_a = sb("neg_a", [P, LAYERS, 2 * SSD_HEADS])
        cact = sb("cact", [P, KT, 2])
        ctan = sb("ctan", [P, KT, 2])
        craw = sb("craw", [P, KT, 2])
        mod = sb("mod", [P, N_MOD, 2])
        mod_in = sb("mod_in", [P, N_MOD, 2])
        ctanh_b = sb("ctanh_b", [P, T])
        amix = sb("amix", [P, KT, 2])
        amlp = sb("amlp", [P, KT, 2])
        hgate = sb("hgate", [P, KT, 2])
        eps = sb("eps", [P, 1])
        stat = sb("stat", [P, 256])
        by_head = sb("by_head", [P, TT, 7 * SSD_HEADS])
        dt, dta, wst = (by_head[:, :, n * 64:(n + 1) * 64] for n in range(3))
        of_group = sb("of_group", [P, TT, 7, GH])
        edec = sb("edec", [P, TT, 192])

        rms = view(mid_a, 0, T)
        rstd = view(mid_a, T, T)
        xin = view(mid_o, 0, TT, D)

        const_loaded, x_loaded, vec_loaded, small_loaded = map(
            sem, ("const_loaded", "x_loaded", "vec_loaded", "small_loaded"))
        slot_loaded = [sem(f"slot_loaded{s}") for s in range(SLOTS)]
        mod_ready = sem("mod_ready")
        mod_read = sem("mod_read")
        tile_ready = sem("tile_ready")
        act_freed = sem("act_freed")
        dve_freed = sem("dve_freed")
        turned = sem("turned")
        turned_freed = sem("turned_freed")
        fence = sem("fence")
        act_step = sem("act_step")
        dve_step = sem("dve_step")
        pool_step = sem("pool_step")
        squares, mean_sq, rms_ready, scaled, shifted = map(
            sem, ("squares", "mean_sq", "rms_ready", "scaled", "shifted"))
        vec_ready, lam_sum, lam_exp, cond_tanh, cond_ready, mods_ready = map(
            sem, ("vec_ready", "lam_sum", "lam_exp", "cond_tanh", "cond_ready", "mods_ready"))
        head_sq, head_ms, head_rms, head_normed, rot_ready, rot_done, q_raw = map(
            sem, ("head_sq", "head_ms", "head_rms", "head_normed", "rot_ready", "rot_done", "q_raw"))
        s_ready, max_ready, p_ready, a_ready, t_ready, at_ready, o_ready, o_done = map(
            sem, ("s_ready", "max_ready", "p_ready", "a_ready", "t_ready", "at_ready", "o_ready", "o_done"))
        sum_sq, tok_rms, tok_scaled = map(sem, ("sum_sq", "tok_rms", "tok_scaled"))
        conv_mid, conv_done, gate_act, hid_mid = map(sem, ("conv_mid", "conv_done", "gate_act", "hid_mid"))
        dt_abs, dt_exp, dt_one, dt_ln, dta_ready, dec_ready, dec_exp = map(
            sem, ("dt_abs", "dt_exp", "dt_one", "dt_ln", "dta_ready", "dec_ready", "dec_exp"))
        conv_tanh, chan_ready, z_tanh = map(sem, ("conv_tanh", "chan_ready", "z_tanh"))
        tok_turned, tok_ready, cb_ready, cb_masked, seg_in, seg_ready, e_ready, dtu_ready, m_ready = map(
            sem, ("tok_turned", "tok_ready", "cb_ready", "cb_masked", "seg_in", "seg_ready", "e_ready",
                  "dtu_ready", "m_ready"))
        xw_ready, xd_ready, st_ready, hin_ready, y_ready, y_done = map(
            sem, ("xw_ready", "xd_ready", "st_ready", "hin_ready", "y_ready", "y_done"))
        gated, out_ready, stored = map(sem, ("gated", "out_ready", "stored"))

        block = ctx.enter_context(nc.Block())

        def tiles(w):
            return w.rearrange("(k p) n -> p k n", p=P)

        w_in, w_out, w_up, w_down = (tiles(a[n]) for n in ("w_in", "w_out", "w_up", "w_down"))

        def of_layer(name, l):
            return tiles(a[name][l])

        def slot(s, kt, width):
            return ring[:, s, 0:kt * width].rearrange("p (k n) -> p k n", k=kt)

        raw1 = view(big1, 0, 14, SEQ)
        sq1 = view(big2, 0, 14, SEQ)
        v1 = view(mid_v, 0, LT, 640)
        rot1 = view(big1, 14 * SEQ, 3, 2 * SEQ)
        o1 = view(mid_o, 0, LT, D)
        mix1 = view(mid_a, 0, KT, SEQ)
        gate1 = view(big1, 0, FFT, SEQ)
        cv1 = view(big2, 0, 4, 2, SEQ)
        qT = view(big1, 0, KT, T)
        kT = view(big1, KT * T, KT, T)
        v2 = view(mid_v, 0, TT, D)
        rot2 = view(big2, 0, 2, SEQ)
        o2 = view(mid_o, 0, TT, D)
        attT = view(mid_a, 0, KT, T)
        prob = view(big2, 0, 2, 2 * T)
        amat = view(big2, 4 * T, 2, T)
        amatT = view(big2, 6 * T, 2, T)
        atmp = view(big2, 8 * T, 2, T)
        yg = view(big2, 0, TT, SSD_IN)
        yT = view(big1, 0, YT, T)
        junk = view(mid_v, 0, SSD_IN)
        merged = view(mid_v, 0, KT, T)
        gs = view(mid_o, 0, KT, T)

        def hidden(n):
            return big1[:, n * T:(n + 1) * T] if n < YT else big2[:, (n - YT) * T:(n - YT + 1) * T]

        chan = [view(mid_o, 4 * T * n, 4, T) for n in range(2)]
        at = 9 * P
        ctanh = [K[:, at:at + T], ctanh_b[:, :]]
        sz = [view(big1, 7168, TT, GW), view(K, at + 4 * SEQ, TT, GW)]
        xtok = view(big1, 0, TT, GW)
        btok = view(big1, 1024, TT, P)
        cb_lo = view(big1, 1536, TT, P)
        cb_up = view(big1, 2048, TT, P)
        seg_f = view(big1, 2560, 2, GH, P)
        seg_b = view(big1, 3584, 2, GH, P)
        ex = view(big1, 4608, 2, GH * P)
        dt_lo = view(big1, 5632, GH, P)
        dt_up = view(big1, 6144, 2, GH * P)
        xw = view(mid_v, 0, 6, GW)
        hin = view(mid_v, 1536, 6, GW)
        ys = view(mid_v, 3072, GW)
        yi = view(mid_v, 3328, GW)
        xd = view(mid_v, 3584, 2, GW)
        dtx = [view(big1, n * 256, TT, 2 * SSD_HEADS) for n in range(6)]

        def y_chunks(l):
            return range(TT) if l == 0 else range(LT)

        F_STATES = [2, 3, 0]
        B_STATES = [3, 2, 1]
        HF = {3: 0, 0: 1, 1: 2}
        HB = {2: 3, 1: 4, 0: 5}

        def units2(l):
            return [(h, q) for h in range(HEADS) for q in range(TT if l == 0 else LT)]

        UNITS1 = [(kind, hp, q) for kind in "AB" for hp in range(4) for q in range(LT)]

        @block.sync
        def _(sp):
            c = Counts(sp)
            done = []
            total = [0]

            sp.dma_start(K[:, :], const).then_inc(const_loaded, 16)
            sp.dma_start(xin[:, 0:LT, :], a["x"][0].rearrange("(t p) d -> p t d", p=P)).then_inc(x_loaded, 16)
            sp.dma_start(xin[:, LT:TT, :], a["ctx_2"][0].rearrange("(t p) d -> p t d", p=P)).then_inc(x_loaded, 16)

            mods = [0]

            def freed(slab):
                if slab >= SLOTS:
                    sp.wait_ge(*done[slab - SLOTS])

            def load(parts, tiles_after):
                s = len(done) % SLOTS
                freed(len(done))
                for dst, src in parts(s):
                    sp.dma_start(dst, src).then_inc(slot_loaded[s], 16)
                done.append((tile_ready, total[0] + tiles_after))

            def load_mods(ada):
                s = len(done) % SLOTS
                freed(len(done))
                j = mods[0] % (N_MOD // 2)
                sp.dma_start(slot(s, KT, 256), ada[:, :, j * 256:(j + 1) * 256]).then_inc(slot_loaded[s], 16)
                mods[0] += 1
                done.append((mod_ready, mods[0]))

            def slabs(n, kt, width, src, tiles_done, body=SLOTS, parts=None):
                parts = parts or (lambda s, j: [(slot(s, kt, width), src(j))])
                turns = n // body
                first = body if turns >= 3 else n
                for j in range(first):
                    load(lambda s: parts(s, j), tiles_done(j + 1))
                if turns >= 3:
                    slope = tiles_done(2 * body) - tiles_done(body)
                    s0 = len(done) - body
                    with sp.Fori(1, turns) as i:
                        for q in range(body):
                            s = (s0 + q) % SLOTS
                            sp.wait_ge(tile_ready, i * slope + (total[0] + tiles_done(body + q - SLOTS + 1) - slope))
                            for dst, part in parts(s, i * body + q):
                                sp.dma_start(dst, part).then_inc(slot_loaded[s], 16)
                    for j in range(body, body * turns):
                        done.append((tile_ready, total[0] + tiles_done(j + 1)))
                    for j in range(body * turns, n):
                        load(lambda s: parts(s, j), tiles_done(j + 1))
                total[0] += tiles_done(n)

            def slabs_and_mods(n, parts, ada):
                def turn(j, i, wait):
                    for q in range(2):
                        for m in range(2):
                            s = (s0 + 2 * q + m) % SLOTS
                            wait(q, m)
                            if m == 0:
                                for dst, src in parts(s, j + q):
                                    sp.dma_start(dst, src).then_inc(slot_loaded[s], 16)
                            else:
                                sp.dma_start(slot(s, KT, 256), ada[:, :, bass.ds(j * 256 + (m0 + q) * 256, 256)])\
                                    .then_inc(slot_loaded[s], 16)

                s0, m0 = len(done), mods[0] % (N_MOD // 2)
                turn(0, 0, lambda q, m: freed(s0 + 2 * q + m))
                with sp.Fori(1, n // 2) as i:
                    turn(i * 2, i, lambda q, m:
                         sp.wait_ge(tile_ready, i * 4 + (total[0] + 2 * q - 2)) if m == 0 else
                         sp.wait_ge(mod_ready, i * 2 + (mods[0] + q - 1)))
                for j in range(n):
                    done.append((tile_ready, total[0] + 2 * (j + 1)))
                    mods[0] += 1
                    done.append((mod_ready, mods[0]))
                total[0] += 2 * n

            def wide(w, c0, n, per=2):
                slabs(n, KT, 256, lambda j: w[:, :, bass.ds(j * 256 + c0, 256)], lambda j: per * j)

            wide(w_in, 0, 2)
            slabs(1, KT, 256, None, lambda j: 2 * j, parts=lambda s, j: [
                (slot(s, KT, 256)[:, :, n * HD:(n + 1) * HD], w_in[:, :, 512 + HD * (n // 2):576 + HD * (n // 2)])
                for n in range(4)])
            slabs(1, KT, 128, lambda j: w_in[:, :, 640:768], lambda j: 2 * j)
            wide(w_in, 768, 6)
            wide(w_out, 0, 4)
            ada = of_layer("ada_w_2", 0)
            for _ in range(2):
                load_mods(ada)
            slabs_and_mods(FFT, lambda s, j: [
                (slot(s, KT, 256)[:, :, 0:P], w_up[:, :, bass.ds(j * P, P)]),
                (slot(s, KT, 256)[:, :, P:2 * P], w_up[:, :, bass.ds(j * P + D_FF, P)])], ada)
            halves = FFT // 2
            for n in range(KT):
                slabs(2, halves, P, lambda j: w_down[:, halves * j:halves * (j + 1), n * P:(n + 1) * P],
                      lambda j: (j + 1) // 2)

            for l in range(LAYERS):
                wi = of_layer("w_in_2", l)
                wide(wi, 0, 4)
                wide(wi, 1024, 4)
                wide(wi, 2048, 4, per=TT)
                slabs(1, KT, 64, lambda j: wi[:, :, C_DT:C_DT + 64], lambda j: TT * j)
                nz = len(y_chunks(l)) // 2
                per_group = 4 + nz
                after = [1, 2, 4, per_group]

                def group_parts(s, q, g):
                    half = slot(s, KT, P)
                    full = slot(s, KT, 256)
                    if q < 2:
                        return [(half, wi[:, :, bass.ds(g * GW + (C_X + q * P), P)])]
                    if q == 2:
                        return [(full[:, :, 0:P], wi[:, :, bass.ds(g * P + C_B, P)]),
                                (full[:, :, P:2 * P], wi[:, :, bass.ds(g * P + C_C, P)])]
                    return [(full, wi[:, :, bass.ds(g * GW + C_Z, GW)])]

                s0 = len(done)
                for q in range(4):
                    load(lambda s: group_parts(s, q, 0), after[q])
                with sp.Fori(1, GROUPS) as g:
                    for q in range(4):
                        s = (s0 + q) % SLOTS
                        sp.wait_ge(tile_ready, g * per_group + (total[0] + after[q] - per_group))
                        for dst, src in group_parts(s, q, g):
                            sp.dma_start(dst, src).then_inc(slot_loaded[s], 16)
                for g in range(1, GROUPS):
                    done.extend((tile_ready, total[0] + per_group * g + n) for n in after)
                total[0] += per_group * GROUPS
                wide(wi, C_GA, 4)
                wide(of_layer("w_attn_o_2", l), 0, 4)
                wide(wi, C_GS, 4)
                wo = of_layer("w_ssd_o_2", l)
                slabs(KT, YT, P, lambda j: wo[:, :, bass.ds(j * P, P)], lambda j: j)
                wide(of_layer("w_out_2", l), 0, 4)
                w1, w2 = of_layer("w_mlp1_2", l), of_layer("w_mlp2_2", l)
                if l + 1 < LAYERS:
                    ada = of_layer("ada_w_2", l + 1)
                    slabs_and_mods(HIDT // 2, lambda s, j: [(slot(s, KT, 256), w1[:, :, bass.ds(j * 256, 256)])], ada)
                else:
                    wide(w1, 0, HIDT // 2)
                for n in range(KT):
                    for half in range(2):
                        load(lambda s: [(slot(s, YT, P), w2[:, YT * half:YT * (half + 1), n * P:(n + 1) * P])], 1)
                        if half == 0 and l + 1 < LAYERS:
                            load_mods(ada)
                    total[0] += 1

            sp.wait_ge(out_ready, 4)
            sp.dma_start(out[0].rearrange("(t p) d -> p t d", p=P), view(big2, 0, LT, D)).then_inc(stored, 16)
            sp.wait_ge(stored, 16)

        @block.tensor
        def _(pe):
            c = Counts(pe)
            slab, tile, bank4, fences = [0], [0], [0], [0]

            def stage():
                pe.drain().then_inc(*c.made(fence))
                fences[0] += 1
                pe.wait_ge(fence, 4 * fences[0])

            def ring_wait(sem):
                _, v = c.need(sem)
                if c.i is not None or v > 0:
                    pe.wait_ge(sem, v)

            def ring_begin(sem):
                c.skip(sem, -4)

            def ring_end(sem):
                pe.wait_ge(*c.need(sem, 4))

            def bodies(n, body, work, per):
                turns = n // body
                if turns >= 2:
                    with c.loop(turns, per) as i:
                        for j in range(body):
                            work(j, i)
                    for j in range(n % body):
                        work(j, turns)
                else:
                    for j in range(n):
                        work(j, 0)

            def weights(k=16):
                s = slab[0] % SLOTS
                slab[0] += 1
                pe.wait_ge(*c.need(slot_loaded[s], k))
                return s

            mods = [0]

            def mod_slab():
                w = slot(weights(), KT, 256)
                b = 5 + mods[0] % 2
                if mods[0] >= 2:
                    pe.wait_ge(*c.need(mod_read))
                for m in range(2):
                    for k in range(KT):
                        mm = pe.matmul(PS[:, b, 2 * m:2 * m + 2], w[:, k, m * P:(m + 1) * P], cact[:, k, :],
                                       start=(k == 0), stop=(k == KT - 1))
                mm.then_inc(*c.made(mod_ready))
                mods[0] += 1

            def to_features(n, rhs, cols, freed, kt=KT, width=256, halves=1, loads=1, body=None, with_mods=False):
                ring_begin(freed)
                per_slab = width // P
                body = body or SLOTS * halves
                n_mods = body // halves if with_mods else 0

                def work(j, i):
                    s = weights(16 * loads)
                    w = slot(s, kt, width)
                    half = j % halves
                    for m in range(per_slab):
                        b = tile[0] % 4
                        if half == 0:
                            ring_wait(freed)
                        for k in range(kt):
                            mm = pe.matmul(PS[:, b, 0:cols], w[:, k, m * P:(m + 1) * P], rhs(half * kt + k),
                                           start=(half == 0 and k == 0), stop=(half == halves - 1 and k == kt - 1))
                        if half == halves - 1:
                            mm.then_inc(*c.made(tile_ready))
                            tile[0] += 1
                    if with_mods and half == 0:
                        mod_slab()

                moved = body * per_slab // halves
                s0, kinds = slab[0], [q for j in range(body) for q in ([loads, 1] if with_mods and j % halves == 0 else [loads])]
                assert len(kinds) % SLOTS == 0 or n // body < 2
                per = [(slot_loaded[(s0 + q) % SLOTS], 16 * sum(kinds[q::SLOTS])) for q in range(SLOTS)]
                bodies(n, body, work, [(tile_ready, moved), (freed, moved), (mod_ready, n_mods), (mod_read, n_mods)] + per)
                if n // body >= 2:
                    mods[0] += n_mods * (n // body - 1)
                ring_end(freed)

            def to_tokens(n, width, n_tok, freed, pairs=False):
                ring_begin(freed)

                def work(j, i):
                    w = slot(weights(), KT, width)
                    for t in range(n_tok):
                        b = tile[0] % 4
                        ring_wait(freed)
                        for k in range(KT):
                            mm = pe.matmul(PS[:, b, 0:width], hT[:, k, t * P:(t + 1) * P], w[:, k, :],
                                           start=(k == 0), stop=(k == KT - 1))
                        mm.then_inc(*c.made(tile_ready))
                        tile[0] += 1

                bodies(n, SLOTS, work, [(tile_ready, SLOTS * n_tok), (freed, SLOTS * n_tok)]
                       + [(q, 16) for q in slot_loaded])
                ring_end(freed)

            def norm(cols):
                for k in range(KT):
                    pe.wait_ge(*c.need(squares))
                    mm = pe.matmul(PS[:, 4, 0:cols], ones, hT[:, k, 0:cols], start=(k == 0), stop=(k == KT - 1))
                mm.then_inc(*c.made(mean_sq))

            def turn_begin():
                c.skip(turned_freed, -4)

            def turn_end():
                pe.wait_ge(*c.need(turned_freed, 4))

            def turn(parts):
                b = 4 + bank4[0] % 4
                bank4[0] += 1
                ring_wait(turned_freed)
                for n, src in enumerate(parts):
                    mm = pe.transpose(PS[0:src.shape[1], b, n * P:n * P + src.shape[0]], src,
                                      ident[0:src.shape[0], 0:src.shape[0]])
                mm.then_inc(*c.made(turned))

            pe.wait_ge(const_loaded, 16)
            pe.wait_ge(x_loaded, 32)
            turn_begin()
            for k in range(KT):
                turn([xin[:, t, k * P:(k + 1) * P] for t in range(TT)])
            pe.wait_ge(vec_loaded, 16 * (len(pieces) + 8))
            n_left = [min(P, n_rows - n * P) for n in range(n_stage)]
            for b in range(-(-n_stage // 4)):
                turn([vstage[0:n_left[n], n, :] for n in range(4 * b, min(4 * b + 4, n_stage))])
            turn_end()
            stage()

            norm(SEQ)
            pe.wait_ge(*c.need(scaled, KT))
            lat = lambda k: hT[:, k, 0:SEQ]
            to_features(2, lat, SEQ, act_freed)
            to_features(1, lat, SEQ, act_freed, loads=4)
            to_tokens(1, 128, LT, act_freed)
            to_features(4, lat, SEQ, act_freed)
            to_tokens(2, 256, LT, act_freed)
            for n in range(7):
                pe.wait_ge(*c.need(head_sq, 2))
                pe.matmul(PS[:, n, :], heads, sq1[:, 2 * n:2 * n + 2, :], start=True, stop=True).then_inc(*c.made(head_ms))
            pe.wait_ge(*c.need(head_normed, 14))
            for n in range(3):
                pe.matmul(PS[:, n, :], turn1, raw1[:, 2 * n:2 * n + 2, :], start=True, stop=True).then_inc(*c.made(rot_ready))
            pe.wait_ge(*c.need(rot_done, 3))

            def scores1(u):
                kind, hp, q = UNITS1[u]
                if u >= 3:
                    pe.wait_ge(*c.need(p_ready))
                for e in range(2):
                    r = slice(e * HD, (e + 1) * HD)
                    tq = hp if kind == "A" else 6 + hp
                    tk = 4 + hp // 2 if kind == "A" else 10 + hp
                    mm = pe.matmul(PS[:, 2 * (u % 3) + e, 0:SEQ], raw1[r, tq, q * P:(q + 1) * P], raw1[r, tk, :],
                                   start=True, stop=True)
                mm.then_inc(*c.made(s_ready))

            def turn_weights(u, n):
                pe.wait_ge(*c.need(a_ready))
                if u >= 1:
                    pe.wait_ge(*c.need(at_ready))
                for m in range(n):
                    mm = pe.transpose(PS[:, 6, m * P:(m + 1) * P], amat[:, u % 2, m * P:(m + 1) * P], ident)
                mm.then_inc(*c.made(t_ready))

            def outputs1(u):
                kind, hp, q = UNITS1[u]
                if u == n_u - 1:
                    pe.wait_ge(*c.need(at_ready))
                if u >= 1:
                    pe.wait_ge(*c.need(o_done))
                for e in range(2):
                    h = 2 * hp + e
                    v0 = HD * (h // 4) if kind == "A" else P + HD * h
                    for t in range(LT):
                        mm = pe.matmul(PS[:, 7, e * HD:(e + 1) * HD],
                                       amatT[:, u % 2, (e * LT + t) * P:(e * LT + t + 1) * P],
                                       v1[:, t, v0:v0 + HD], start=(t == 0), stop=(t == LT - 1))
                mm.then_inc(*c.made(o_ready))

            n_u = len(UNITS1)
            scores1(0)
            scores1(1)
            for u in range(n_u + 1):
                if u + 2 < n_u:
                    scores1(u + 2)
                if u < n_u:
                    turn_weights(u, 4)
                if u >= 1:
                    outputs1(u - 1)
            c.skip(p_ready, 3)
            pe.wait_ge(*c.need(o_done))
            pe.wait_ge(*c.need(tok_scaled, 2 * LT))
            turn_begin()
            for f in range(KT):
                turn([o1[:, t, f * P:(f + 1) * P] for t in range(LT)])
            turn_end()
            to_features(4, lambda k: mix1[:, k, :], SEQ, dve_freed)
            stage()
            norm(SEQ)
            pe.wait_ge(*c.need(scaled, KT))
            pe.wait_ge(*c.need(cond_ready))
            for _ in range(2):
                mod_slab()
            to_features(FFT, lat, SEQ, dve_freed, loads=2, body=2, with_mods=True)
            pe.wait_ge(*c.need(conv_done, FFT))
            to_features(2 * KT, lambda k: gate1[:, k, :], SEQ, dve_freed, kt=FFT // 2, width=P, halves=2)
            stage()

            for l in range(LAYERS):
                norm(T)
                pe.wait_ge(*c.need(shifted, 2 * KT))
                c.skip(scaled, 2 * KT)
                both = lambda k: hT[:, k, :]
                q_cols = T if l == 0 else SEQ
                some = lambda k: hT[:, k, 0:q_cols]

                to_features(4, some, q_cols, act_freed)
                to_features(4, both, T, act_freed)
                for n in range(2 * KT):
                    src = qT if n < KT else kT
                    if n >= 4:
                        pe.wait_ge(*c.need(rot_done))
                    pe.matmul(PS[:, 4 + n % 4, 0:SEQ], turn2, src[:, n % KT, 0:SEQ], start=True, stop=True)\
                        .then_inc(*c.made(rot_ready))
                to_tokens(4, 256, TT, act_freed)
                pe.wait_ge(*c.need(rot_done, 4))

                units = units2(l)

                def scores2(u):
                    h, q = units[u]
                    k0, nk = (0, T) if q < LT else (SEQ, SEQ)
                    if u >= 3:
                        pe.wait_ge(*c.need(p_ready, 2))
                    for e in range(2):
                        r = slice(e * HD, (e + 1) * HD)
                        mm = pe.matmul(PS[:, 2 * (u % 3) + e, 0:nk], qT[r, h, q * P:(q + 1) * P], kT[r, h, k0:k0 + nk],
                                       start=True, stop=True)
                    mm.then_inc(*c.made(s_ready))

                def outputs2(u):
                    h, q = units[u]
                    k0, nt = (0, TT) if q < LT else (LT, LT)
                    if u == n_u - 1:
                        pe.wait_ge(*c.need(at_ready))
                    if u >= 1:
                        pe.wait_ge(*c.need(o_done))
                    for n in range(nt):
                        mm = pe.matmul(PS[:, 7, 0:P], amatT[:, u % 2, n * P:(n + 1) * P],
                                       v2[:, k0 + n, h * P:(h + 1) * P], start=(n == 0), stop=(n == nt - 1))
                    mm.then_inc(*c.made(o_ready))

                n_u = len(units)
                scores2(0)
                scores2(1)
                for u in range(n_u + 1):
                    if u + 2 < n_u:
                        scores2(u + 2)
                    if u < n_u:
                        turn_weights(u, TT if units[u][1] < LT else LT)
                    if u >= 1:
                        outputs2(u - 1)
                c.skip(p_ready, 6)
                pe.wait_ge(*c.need(o_done))
                n_tok = len(y_chunks(l))
                pe.wait_ge(*c.need(tok_scaled, n_tok))
                turn_begin()
                for f in range(KT):
                    turn([o2[:, t, f * P:(f + 1) * P] for t in range(n_tok)])
                turn_end()
                stage()

                to_tokens(1, 64, TT, dve_freed)
                pe.wait_ge(*c.need(dta_ready))
                for t in range(TT):
                    bank, o = t, 0
                    for m, lhs, r0, n in ((0, t_gt, 0, 32), (32, t_le, 0, 32), (64, t_lt, 32, 32), (96, t_ge, 32, 32),
                                          (128, ones, 0, 64)):
                        mm = pe.matmul(PS[:, bank, o + m:o + m + n], lhs, dta[:, t, r0:r0 + n], start=True, stop=True)
                    mm.then_inc(*c.made(dec_ready))
                stage()

                ny = len(y_chunks(l))
                nz = ny // 2
                s0 = slab[0]

                freed_before = [1] * 6 if l == 0 else [2, 1, 0, 1, 1]
                c.skip(dve_freed, -3)

                def product(n, w=None):
                    if n != 3:
                        q = min(n, 3)
                        s = (s0 + q) % SLOTS
                        if n <= 4:
                            pe.wait_ge(*c.need(slot_loaded[s], 32 if q == 2 else 16))
                    else:
                        s = (s0 + 2) % SLOTS
                    b = n % 3
                    if freed_before[n]:
                        pe.wait_ge(*c.need(dve_freed, freed_before[n]))
                    if n < 4:
                        w = slot(s, KT, P if n < 2 else 256)
                        m = P if n == 3 else 0
                        for k in range(KT):
                            mm = pe.matmul(PS[:, b, :], w[:, k, m:m + P], hT[:, k, :], start=(k == 0), stop=(k == KT - 1))
                    else:
                        w = slot(s, KT, 256)
                        for t in range(2):
                            t0 = (2 * (n - 4) + t) * P
                            for k in range(KT):
                                mm = pe.matmul(PS[:, b, t * GW:(t + 1) * GW], hT[:, k, t0:t0 + P], w[:, k, :],
                                               start=(k == 0), stop=(k == KT - 1))
                    mm.then_inc(*c.made(tile_ready))

                def turn_group(p, first):
                    pe.wait_ge(*c.need(chan_ready, 4))
                    if not first:
                        pe.wait_ge(*c.need(y_done))
                        pe.wait_ge(*c.need(e_ready, 2))
                    ch = chan[p]
                    for n in range(2):
                        for t in range(4):
                            mm = pe.transpose(PS[:, 3 + n, t * P:(t + 1) * P],
                                              ch[:, t % 2, (2 * n + t // 2) * P:(2 * n + t // 2 + 1) * P], ident)
                        mm.then_inc(*c.made(tok_turned))
                    for t in range(TT):
                        mm = pe.transpose(PS[:, 5, t * P:(t + 1) * P], ch[:, 2, t * P:(t + 1) * P], ident)
                    mm.then_inc(*c.made(tok_turned))
                    for t in range(ny):
                        mm = pe.matmul(PS[:, 6, t * P:(t + 1) * P], ch[:, 2, t * P:(t + 1) * P], ch[:, 3, t * P:(t + 1) * P],
                                       start=True, stop=True)
                    mm.then_inc(*c.made(cb_ready))

                def seg(t):
                    pe.wait_ge(*c.need(seg_in, 2))
                    if t == 1:
                        pe.wait_ge(*c.need(cb_masked))
                    if t >= 2:
                        pe.wait_ge(*c.need(e_ready))
                    for lhs, rhs in ((t_gt, seg_f), (t_lt, seg_b)):
                        mm = pe.matmul(PS[:, 7 - t % 2, :], lhs, rhs[:, t % 2, :, :].rearrange("p r l -> p (r l)"),
                                       start=lhs is t_gt, stop=lhs is t_lt)
                    mm.then_inc(*c.made(seg_ready))

                def states():
                    pe.wait_ge(*c.need(tok_ready, 3))
                    pe.wait_ge(*c.need(xw_ready, 6))
                    for n, t in enumerate(F_STATES + B_STATES):
                        mm = pe.matmul(PS[:, 3 + n // 2, (n % 2) * GW:(n % 2 + 1) * GW], btok[:, t, :], xw[:, n, :],
                                       start=True, stop=True)
                    mm.then_inc(*c.made(st_ready))

                def chunk(t, p):
                    pe.wait_ge(*c.need(m_ready))
                    if t == 0:
                        pe.wait_ge(*c.need(hin_ready))
                    else:
                        pe.wait_ge(*c.need(y_done))
                    for r in range(GH):
                        pe.matmul(PS[:, 3 + t % 2, r * HD:(r + 1) * HD], ex[:, t % 2, r * P:(r + 1) * P],
                                  xtok[:, t, r * HD:(r + 1) * HD], start=True, stop=True)
                    for d, hs in enumerate((HF, HB)):
                        if t in hs:
                            mm = pe.matmul(PS[:, 5, d * GW:(d + 1) * GW], chan[p][:, 3, t * P:(t + 1) * P],
                                           hin[:, hs[t], :], start=True, stop=True)
                    mm.then_inc(*c.made(y_ready))

                def turn_of(p, products=True, first=False):
                    turn_group(p, first)
                    if products:
                        product(0)
                    seg(0)
                    seg(1)
                    if products:
                        product(1)
                    states()
                    if products:
                        product(2)
                    for t in range(max(ny, 2)):
                        chunk(t, p)
                        if t + 2 < ny:
                            seg(t + 2)
                        if products and 3 + t < 4 + nz:
                            product(3 + t)

                for n in range(4 + nz):
                    product(n)
                turn_of(0, first=True)
                counted = [(tile_ready, 4 + nz), (dve_freed, 4 + nz), (chan_ready, 4), (tok_turned, 3),
                           (cb_ready, 1), (seg_in, 2 * ny), (cb_masked, 1), (seg_ready, ny), (tok_ready, 3),
                           (xw_ready, 6), (st_ready, 1), (m_ready, ny), (hin_ready, 1), (y_done, ny),
                           (y_ready, ny), (e_ready, ny)] + [(slot_loaded[(s0 + q) % SLOTS], 32 if q == 2 else 16) for q in range(4)]
                with c.loop(GROUPS // 2 - 1, [(q, 2 * k) for q, k in counted]):
                    turn_of(1)
                    turn_of(0)
                turn_of(1, products=False)
                pe.wait_ge(*c.need(dve_freed, 3))
                pe.wait_ge(*c.need(e_ready, 2))
                pe.wait_ge(*c.need(y_done))
                slab[0] += 4 * GROUPS
                tile[0] += (4 + nz) * GROUPS
                stage()
                pe.wait_ge(*c.need(tok_scaled, ny))
                turn_begin()
                for f in range(YT):
                    turn([yg[:, t, f * P:(f + 1) * P] for t in range(ny)])
                turn_end()
                stage()
                to_features(4, some, q_cols, act_freed)
                to_features(4, lambda k: attT[:, k, 0:q_cols], q_cols, dve_freed)
                to_features(4, some, q_cols, act_freed)
                to_features(KT, lambda k: yT[:, k, 0:q_cols], q_cols, dve_freed, kt=YT, width=P)
                pe.wait_ge(*c.need(gated, KT))
                to_features(4, lambda k: merged[:, k, 0:q_cols], q_cols, dve_freed)
                stage()
                norm(q_cols)
                pe.wait_ge(*c.need(shifted, 2 * KT if l == 0 else KT))
                c.skip(scaled, 2 * KT if l == 0 else KT)
                more = l + 1 < LAYERS
                to_features(HIDT // 2, some, q_cols, dve_freed, body=2, with_mods=True) if more else \
                    to_features(HIDT // 2, some, q_cols, dve_freed)
                pe.wait_ge(*c.need(hid_mid, HIDT))
                to_features(2 * KT, lambda k: hidden(k)[:, 0:q_cols], q_cols, dve_freed, kt=YT, width=P, halves=2, with_mods=more)
                stage()

            norm(SEQ)
            pe.wait_ge(*c.need(scaled, KT))
            turn_begin()
            for t in range(LT):
                for b in range(2):
                    turn([hT[:, 4 * b + k, t * P:(t + 1) * P] for k in range(4)])

        @block.scalar
        def _(act):
            c = Counts(act)
            tile, bank4, fences = [0], [0], [0]

            for n, p0, m, src in pieces:
                act.dma_start(vstage[p0:p0 + m, n, :], src).then_inc(vec_loaded, 16)
            for name in ("qa_norm_g", "qb_norm_g", "ka_norm_g", "kb_norm_g"):
                r = rows[name]
                for e in range(2):
                    act.dma_start(vstage[r % P:r % P + 1, r // P, e * HD:(e + 1) * HD],
                                  a[name].rearrange("(a b) -> a b", a=1)).then_inc(vec_loaded, 16)
            n_small = 0
            for l in range(LAYERS):
                for n, name in enumerate(("lambda_q1_2", "lambda_k1_2", "lambda_q2_2", "lambda_k2_2")):
                    act.dma_start(lam_in[:, l, n, :], a[name][l:l + 1, :].broadcast_to([P, HD])).then_inc(small_loaded, 16)
                for n, name in enumerate(("dt_bias_f_2", "dt_bias_b_2", "a_log_f_2", "a_log_b_2", "ssd_d_2")):
                    act.dma_start(head_in[:, l, n * 32:(n + 1) * 32], a[name][l:l + 1, :].broadcast_to([P, 32]))\
                        .then_inc(small_loaded, 16)
                n_small += 9

            def stage():
                act.drain().then_inc(*c.made(fence))
                fences[0] += 1
                act.wait_ge(fence, 4 * fences[0])

            def norm(cols):
                for k in range(KT):
                    act.activation(hT[:, k, 0:cols], xT[:, k, 0:cols], ACT.Square).then_inc(*c.made(squares))
                act.wait_ge(*c.need(mean_sq))
                act.activation(rms[:, 0:cols], PS[:, 4, 0:cols], ACT.Sqrt, scale=1.0 / D, bias=eps[:, 0:1])\
                    .then_inc(*c.made(rms_ready))

            def shift(l, m0, halves):
                for k in range(KT):
                    for e in range(halves):
                        act.wait_ge(*c.need(scaled))
                        h = hT[:, k, e * SEQ:(e + 1) * SEQ]
                        act.activation(h, h, ACT.Identity, bias=mod[:, m0 + k, e:e + 1]).then_inc(*c.made(shifted))

            def unload(dst, cols, func=ACT.Copy, scale=1.0):
                b = tile[0] % 4
                tile[0] += 1
                act.wait_ge(*c.need(tile_ready))
                act.activation(dst, PS[:, b:b + 1, 0:cols], func, scale=scale).then_inc(*c.made(act_freed))

            def unloads(n, dst, cols, func=ACT.Copy, scale=1.0):
                with c.loop(n // 4, [(tile_ready, 4), (act_freed, 4)]) as i:
                    for j in range(4):
                        unload(dst(i * 4 + j), cols, func, scale)

            def passed(n):
                c.skip(tile_ready, n)
                tile[0] += n

            def turned_to(dst, n, gain=None):
                b = 4 + bank4[0] % 4
                bank4[0] += 1
                act.wait_ge(*c.need(turned))
                if gain is None:
                    act.activation(dst, PS[:, b, 0:n], ACT.Copy).then_inc(*c.made(turned_freed))
                else:
                    act.activation(dst, PS[:, b, 0:n], ACT.Copy, scale=gain).then_inc(*c.made(turned_freed))

            act.wait_ge(*c.need(vec_ready))
            for k in range(KT):
                turned_to(xT[:, k, :], T)
            for b in range(-(-n_stage // 4)):
                turned_to(V[:, 512 * b:min(512 * (b + 1), n_rows)], min(512, n_rows - 512 * b))
            act.wait_ge(*c.sofar(turned_freed))
            act.wait_ge(*c.need(lam_sum))
            act.activation(lam_s[:, 4:8], lam_s[:, 0:4], ACT.Exp).then_inc(*c.made(lam_exp))
            act.wait_ge(small_loaded, 16 * n_small)
            act.activation(neg_a[:, :, :], head_in[:, :, 64:128], ACT.Exp).then_inc(*c.made(lam_exp))
            for e, name in enumerate(("c_2", "c_ctx_2")):
                act.activation(craw[:, :, e], V[:, rows[name]:rows[name] + KT], ACT.Copy).then_inc(*c.made(act_step))
            act.wait_ge(*c.sofar(act_step))
            act.activation(ctan[:, :, :], craw[:, :, :], ACT.Tanh, scale=0.5).then_inc(*c.made(cond_tanh))
            stage()

            norm(SEQ)
            c.skip(scaled, KT)
            for j in range(4):
                unload(raw1[:, j:j + 1, :], SEQ)
            for j in range(4, 6):
                unload(raw1[:, j:j + 1, :], SEQ)
            for t in range(LT):
                unload(v1[:, t:t + 1, 0:P], P)
            for j in range(6, 14):
                unload(raw1[:, j:j + 1, :], SEQ)
            for n in range(2):
                for t in range(LT):
                    unload(v1[:, t:t + 1, P + n * 256:P + (n + 1) * 256], 256)
            act.wait_ge(*c.sofar(act_freed))
            for j in range(14):
                act.activation(sq1[:, j, :], raw1[:, j, :], ACT.Square).then_inc(*c.made(head_sq))
            for n in range(7):
                act.wait_ge(*c.need(head_ms))
                act.activation(sq1[:, 2 * n:2 * n + 2, :], PS[:, n, :].rearrange("p (a b) -> p a b", a=2), ACT.Sqrt,
                               scale=1.0 / HD, bias=eps[:, 0:1]).then_inc(*c.made(head_rms))

            def exp1(u):
                act.wait_ge(*c.need(max_ready))
                if u >= 2:
                    act.wait_ge(*c.need(a_ready))
                for e in range(2):
                    src = PS[:, 2 * (u % 3) + e, 0:SEQ] if UNITS1[u][0] == "A" else atmp[:, u % 2, e * SEQ:(e + 1) * SEQ]
                    ins = act.activation(prob[:, u % 2, e * SEQ:(e + 1) * SEQ], src, ACT.Exp,
                                         bias=stat[:, 2 * u + e:2 * u + e + 1], accum_out=stat[:, 64 + 2 * u + e:65 + 2 * u + e])
                    if e:
                        ins.then_inc(*c.made(p_ready))

            def weightsT(u, n):
                act.wait_ge(*c.need(t_ready))
                if u >= 2:
                    act.wait_ge(*c.need(o_ready))
                act.activation(amatT[:, u % 2, 0:n], PS[:, 6, 0:n], ACT.Copy).then_inc(*c.made(at_ready))

            n_u = len(UNITS1)
            for u in range(n_u + 1):
                if u < n_u:
                    exp1(u)
                if u >= 1:
                    weightsT(u - 1, 512)
            c.skip(a_ready, 2)
            c.skip(o_ready, 2)
            act.wait_ge(*c.need(o_done, n_u))
            for t in range(LT):
                for e in range(2):
                    act.activation(junk[:, 0:512], o1[:, t, e * 512:(e + 1) * 512], ACT.Square,
                                   accum_out=stat[:, 128 + 2 * t + e:129 + 2 * t + e]).then_inc(*c.made(act_step))
                    act.wait_ge(*c.sofar(act_step))
            act.activation(stat[:, 136:140], stat[:, 128:132], ACT.Sqrt, scale=1.0 / 512, bias=eps[:, 0:1])\
                .then_inc(*c.made(tok_rms))
            c.skip(tok_scaled, 2 * LT)
            for f in range(KT):
                turned_to(mix1[:, f, :], SEQ, col("outa_norm_g", f) if f < 4 else col("outb_norm_g", f - 4))
            passed(KT)
            stage()
            norm(SEQ)
            c.skip(scaled, KT)

            def ffn(j):
                for e in range(2):
                    b = (tile0 + 2 * (j % 2) + e) % 4
                    act.wait_ge(*c.need(tile_ready))
                    if e == 0:
                        act.wait_ge(*c.need(conv_done))
                    jj = j if c.i is None else c.i * 2 + j
                    act.activation(cv1[:, j % 2, e, :], PS[:, b, 0:SEQ], ACT.Identity, scale=dcol("conv_w", 44 + 22 * e, jj),
                                   bias=dcol("conv_b", 22 * e, jj)).then_inc(*c.made(conv_mid))
                act.wait_ge(*c.need(dve_freed, 2))
                act.activation(cv1[:, 2 + j % 2, 0, :], cv1[:, j % 2, 0, :], ACT.Gelu_apprx_tanh).then_inc(*c.made(gate_act))

            c.skip(dve_freed, KT)
            tile0 = tile[0]
            c.skip(conv_done, -2)
            for j in range(2):
                jj = j
                for e in range(2):
                    b = (tile0 + 2 * (j % 2) + e) % 4
                    act.wait_ge(*c.need(tile_ready))
                    act.activation(cv1[:, j % 2, e, :], PS[:, b, 0:SEQ], ACT.Identity, scale=col("conv_w", 44 + 22 * e + j),
                                   bias=col("conv_b", 22 * e + j)).then_inc(*c.made(conv_mid))
                c.skip(conv_done)
                act.wait_ge(*c.need(dve_freed, 2))
                act.activation(cv1[:, 2 + j % 2, 0, :], cv1[:, j % 2, 0, :], ACT.Gelu_apprx_tanh).then_inc(*c.made(gate_act))
            with c.loop(FFT // 2 - 1, [(tile_ready, 4), (conv_mid, 4), (dve_freed, 4), (gate_act, 2), (conv_done, 2)]) as i:
                c.i = i
                for j in range(2):
                    for e in range(2):
                        b = (tile0 + 2 * j + e) % 4
                        act.wait_ge(*c.need(tile_ready))
                        if e == 0:
                            act.wait_ge(*c.need(conv_done))
                        act.activation(cv1[:, j, e, :], PS[:, b, 0:SEQ], ACT.Identity,
                                       scale=dcol("conv_w", 44 + 22 * e + 2 + j, i * 2),
                                       bias=dcol("conv_b", 22 * e + 2 + j, i * 2)).then_inc(*c.made(conv_mid))
                    act.wait_ge(*c.need(dve_freed, 2))
                    act.activation(cv1[:, 2 + j, 0, :], cv1[:, j, 0, :], ACT.Gelu_apprx_tanh).then_inc(*c.made(gate_act))
            c.skip(conv_done, 2)
            tile[0] += 2 * FFT
            passed(KT)
            c.skip(dve_freed, KT)
            stage()

            for l in range(LAYERS):
                halves = 2 if l == 0 else 1
                q_cols = halves * SEQ
                ny = len(y_chunks(l))
                norm(T)
                act.wait_ge(*c.need(mods_ready))
                shift(l, 0, 2)
                unloads(KT, lambda j: qT[:, bass.ds(j, 1), 0:q_cols], q_cols, scale=HD ** -0.5)
                unloads(KT, lambda j: kT[:, bass.ds(j, 1), :], T)
                with c.loop(4, [(tile_ready, 4), (act_freed, 4)]) as i:
                    for t in range(TT):
                        unload(v2[:, t:t + 1, bass.ds(i * 256, 256)], 256)

                units = units2(l)

                def exp2(u):
                    h, q = units[u]
                    nk = T if q < LT else SEQ
                    act.wait_ge(*c.need(max_ready))
                    if u >= 2:
                        act.wait_ge(*c.need(a_ready))
                    for e in range(2):
                        act.activation(prob[:, u % 2, e * T:e * T + nk], PS[:, 2 * (u % 3) + e, 0:nk], ACT.Exp,
                                       bias=stat[:, 2 * u + e:2 * u + e + 1],
                                       accum_out=stat[:, 64 + 2 * u + e:65 + 2 * u + e]).then_inc(*c.made(p_ready))

                n_u = len(units)
                for u in range(n_u + 1):
                    if u < n_u:
                        exp2(u)
                    if u >= 1:
                        weightsT(u - 1, T if units[u - 1][1] < LT else SEQ)
                c.skip(a_ready, 2)
                c.skip(o_ready, 2)
                act.wait_ge(*c.need(o_done, n_u))
                for h in range(HEADS):
                    for t in range(ny):
                        act.activation(junk[:, 0:P], o2[:, t, h * P:(h + 1) * P], ACT.Square,
                                       accum_out=stat[:, 128 + t * HEADS + h:129 + t * HEADS + h]).then_inc(*c.made(act_step))
                        act.wait_ge(*c.sofar(act_step))
                act.activation(stat[:, 160:160 + ny * HEADS], stat[:, 128:128 + ny * HEADS], ACT.Sqrt, scale=1.0 / P,
                               bias=eps[:, 0:1]).then_inc(*c.made(tok_rms))
                c.skip(tok_scaled, ny)
                for f in range(KT):
                    turned_to(attT[:, f, 0:ny * P], ny * P, col("attn_subln_g_2", l))
                stage()

                passed(TT)
                c.skip(dve_freed, TT)
                act.wait_ge(*c.need(dt_abs))
                act.activation(dtx[1][:, :, :], dtx[0][:, :, :], ACT.Abs).then_inc(*c.made(act_step))
                act.wait_ge(*c.sofar(act_step))
                act.activation(dtx[2][:, :, :], dtx[1][:, :, :], ACT.Exp, scale=-1.0).then_inc(*c.made(dt_exp))
                act.wait_ge(*c.need(dt_one))
                act.activation(dtx[4][:, :, :], dtx[3][:, :, :], ACT.Ln).then_inc(*c.made(dt_ln))
                for t in range(TT):
                    act.wait_ge(*c.need(dec_ready))
                    act.activation(edec[:, t, :], PS[:, t, 0:192], ACT.Exp)\
                        .then_inc(*c.made(dec_exp))
                stage()

                nz = ny // 2
                cw = rows["conv_w_2"] + l * 160
                cb = rows["conv_b_2"] + l * 32

                c.skip(chan_ready, -2)

                def conv(g, p, j):
                    act.wait_ge(*c.need(tile_ready))
                    st, off = (2, j) if j < 2 else (1, 16 + 8 * (j - 2))
                    act.activation(chan[p][:, j, :], PS[:, j % 3, :], ACT.Identity, scale=V[:, bass.ds(g * st + (cw + 64 + off), 1)],
                                   bias=V[:, bass.ds(g * st + (cb + off), 1)]).then_inc(*c.made(conv_mid))
                    act.wait_ge(*c.need(dve_freed))
                    _, used = c.need(chan_ready)
                    if c.i is not None or used > 0:
                        act.wait_ge(chan_ready, used)
                    act.activation(ctanh[j % 2], chan[p][:, j, :], ACT.Tanh).then_inc(*c.made(conv_tanh))

                def gate_of_z(p, b):
                    act.wait_ge(*c.need(tile_ready))
                    act.activation(sz[p][:, 2 * b:2 * b + 2, :], PS[:, (4 + b) % 3, :].rearrange("p (t n) -> p t n", t=2), ACT.Tanh,
                                   scale=0.5).then_inc(*c.made(z_tanh))

                def to_tok(first):
                    if not first:
                        act.wait_ge(*c.need(xd_ready, ny))
                    for n in range(2):
                        act.wait_ge(*c.need(tok_turned))
                        act.activation(xtok[:, 2 * n:2 * n + 2, :], PS[:, 3 + n, :].rearrange("p (t n) -> p t n", t=2), ACT.Copy)\
                            .then_inc(*c.made(tok_ready))
                    act.wait_ge(*c.need(tok_turned))
                    act.activation(btok[:, :, :], PS[:, 5, :].rearrange("p (t n) -> p t n", t=TT), ACT.Copy)\
                        .then_inc(*c.made(tok_ready))

                def decays(t):
                    act.wait_ge(*c.need(seg_ready))
                    if t >= 2:
                        act.wait_ge(*c.need(y_ready))
                    act.activation(ex[:, t % 2, :], PS[:, 7 - t % 2, :], ACT.Exp).then_inc(*c.made(e_ready))

                def turn_of(g, p, products=True, first=False):
                    to_tok(first)
                    if products:
                        conv(g, 1 - p, 0)
                    decays(0)
                    decays(1)
                    for j in range(1, 4):
                        if products:
                            conv(g, 1 - p, j)
                        if 2 <= j < ny:
                            decays(j)
                    c.skip(y_ready, 2)
                    if products:
                        for b in range(nz):
                            gate_of_z(1 - p, b)
                        c.skip(dve_freed, nz)

                for j in range(4):
                    conv(0, 0, j)
                for b in range(nz):
                    gate_of_z(0, b)
                c.skip(dve_freed, nz)
                turn_of(1, 0, first=True)
                counted = [(tile_ready, 4 + nz), (conv_mid, 4), (dve_freed, 4 + nz), (chan_ready, 4), (conv_tanh, 4),
                           (z_tanh, nz), (tok_turned, 3), (tok_ready, 3), (seg_ready, ny), (y_ready, ny), (xd_ready, ny), (e_ready, ny)]
                with c.loop(GROUPS // 2 - 1, [(q, 2 * k) for q, k in counted]) as i:
                    turn_of(i * 2 + 2, 1)
                    turn_of(i * 2 + 3, 0)
                turn_of(None, 1, products=False)
                c.skip(chan_ready, 2)
                c.skip(xd_ready, ny)
                tile[0] += (4 + nz) * GROUPS
                stage()
                for t in range(ny):
                    act.activation(junk, yg[:, t, :], ACT.Square, accum_out=stat[:, 128 + t:129 + t]).then_inc(*c.made(act_step))
                    act.wait_ge(*c.sofar(act_step))
                act.activation(stat[:, 160:160 + ny], stat[:, 128:128 + ny], ACT.Sqrt, scale=1.0 / SSD_IN, bias=eps[:, 0:1])\
                    .then_inc(*c.made(tok_rms))
                c.skip(tok_scaled, ny)
                for f in range(YT):
                    turned_to(yT[:, f, 0:ny * P], ny * P, col("ssd_norm_g_2", l * YT + f))
                stage()
                unloads(KT, lambda j: merged[:, bass.ds(j, 1), 0:q_cols], q_cols, ACT.Tanh, 0.5)
                passed(KT)
                unloads(KT, lambda j: gs[:, bass.ds(j, 1), 0:q_cols], q_cols, ACT.Tanh, 0.5)
                passed(2 * KT)
                c.skip(gated, KT)
                stage()
                norm(q_cols)
                shift(l, 24, halves)
                c.skip(dve_freed, 3 * KT)
                for n in range(HIDT):
                    act.wait_ge(*c.need(dve_freed))
                    h = hidden(n)[:, 0:q_cols]
                    act.activation(h, h, ACT.Square).then_inc(*c.made(hid_mid))
                passed(HIDT + KT)
                c.skip(dve_freed, KT)
                stage()

            norm(SEQ)
            c.skip(scaled, KT)
            res = view(big2, 0, LT, D)
            for t in range(LT):
                for b in range(2):
                    bk = 4 + bank4[0] % 4
                    bank4[0] += 1
                    act.wait_ge(*c.need(turned))
                    act.activation(res[:, t, 512 * b:512 * (b + 1)], PS[:, bk, :], ACT.Copy).then_inc(*c.made(out_ready))

        def act_total(l, n):
            return 20 + l * (8 + 8 + 16 + 16) + 32 + 8 * n

        @block.vector
        def _(dve):
            c = Counts(dve)
            tile, fences = [0], [0]

            def stage():
                dve.drain().then_inc(*c.made(fence))
                fences[0] += 1
                dve.wait_ge(fence, 4 * fences[0])

            def settle(sem=None):
                dve.wait_ge(*c.sofar(sem or dve_step))

            def step(ins):
                return ins.then_inc(*c.made(dve_step))

            def bc(ap, n, axis=2):
                return ap.unsqueeze(2).broadcast_to([P, ap.shape[1], n])

            def bc_mid(ap, n):
                return ap.unsqueeze(1).broadcast_to([P, n, ap.shape[1]])

            def norm(gain, cols):
                dve.wait_ge(*c.need(rms_ready))
                step(dve.reciprocal(rstd[:, 0:cols], rms[:, 0:cols]))
                settle()
                for k in range(KT):
                    for e in range(-(-cols // SEQ)):
                        r = slice(e * SEQ, (e + 1) * SEQ)
                        dve.scalar_tensor_tensor(out=hT[:, k, r], in0=xT[:, k, r], scalar=gain(k, e), in1=rstd[:, r],
                                                 op0=ALU.mult, op1=ALU.mult).then_inc(*c.made(scaled))

            def passed(n):
                c.skip(tile_ready, n)
                tile[0] += n

            def next_tile():
                b = tile[0] % 4
                tile[0] += 1
                dve.wait_ge(*c.need(tile_ready))
                return b

            mods = [0]

            def copy_mods(j):
                b = 5 + mods[0] % 2
                mods[0] += 1
                dve.wait_ge(*c.need(mod_ready))
                dve.tensor_copy(mod_in[:, bass.ds(j * 2, 2), :], PS[:, b, 0:4].rearrange("p (m e) -> p m e", e=2))\
                    .then_inc(*c.made(mod_read))

            dve.memset(eps[:, :], EPS).then_inc(*c.made(vec_ready))
            dve.wait_ge(small_loaded, 16 * 9 * LAYERS)
            for l in range(LAYERS):
                for n in range(2):
                    pr = view(big1, (2 * l + n) * HD, HD)
                    step(dve.tensor_tensor(pr, lam_in[:, l, 2 * n, :], lam_in[:, l, 2 * n + 1, :], ALU.mult))
                    settle()
                    ins = dve.reduce_sum(lam_s[:, 2 * l + n:2 * l + n + 1], pr, AX.X)
                    if l == LAYERS - 1 and n == 1:
                        ins.then_inc(*c.made(lam_sum))
                    else:
                        step(ins)
            dve.wait_ge(*c.need(lam_exp))
            step(dve.tensor_tensor(lam_s[:, 8:10], lam_s[:, 5:8:2], lam_s[:, 4:8:2], ALU.subtract))
            settle()
            for l in range(LAYERS):
                lam_init = 0.8 - 0.6 * float(np.exp(-0.3 * l))
                step(dve.tensor_scalar(neg_lam[:, l:l + 1], lam_s[:, 8 + l:9 + l], -lam_init, None, ALU.add))
            dve.wait_ge(*c.need(lam_exp))
            step(dve.tensor_scalar(neg_a[:, :, :], neg_a[:, :, :], -1.0, None, ALU.mult))
            dve.wait_ge(*c.need(cond_tanh))
            step(dve.scalar_tensor_tensor(out=craw[:, :, :], in0=ctan[:, :, :], scalar=1.0, in1=craw[:, :, :],
                                          op0=ALU.add, op1=ALU.mult))
            settle()
            dve.tensor_scalar(cact[:, :, :], craw[:, :, :], 0.5, None, ALU.mult).then_inc(*c.made(cond_ready))
            n_c2 = LAYERS * 6 * 32
            half_conv = V[:, rows["conv_w_2"]:rows["conv_w_2"] + n_c2]
            step(dve.tensor_scalar(half_conv, half_conv, 0.5, None, ALU.mult))
            q_gain = V[:, rows["qa_norm_g"]:rows["qa_norm_g"] + 2]
            step(dve.tensor_scalar(q_gain, q_gain, HD ** -0.5, None, ALU.mult))
            stage()

            norm(lambda k, e: col("norm1_g", k), SEQ)
            passed(20)
            gains = ["qa_norm_g"] * 4 + ["ka_norm_g"] * 2 + ["qb_norm_g"] * 4 + ["kb_norm_g"] * 4
            for n in range(7):
                dve.wait_ge(*c.need(head_rms))
                step(dve.reciprocal(sq1[:, 2 * n:2 * n + 2, :], sq1[:, 2 * n:2 * n + 2, :]))
                settle()
                for j in (2 * n, 2 * n + 1):
                    dve.scalar_tensor_tensor(out=raw1[:, j, :], in0=raw1[:, j, :], scalar=col(gains[j]), in1=sq1[:, j, :],
                                             op0=ALU.mult, op1=ALU.mult).then_inc(*c.made(head_normed))
            settle(head_normed)
            for n in range(3):
                dve.wait_ge(*c.need(rot_ready))
                t2 = rot1[:, n, :].rearrange("p (a b) -> p a b", a=2)
                src = raw1[:, 2 * n:2 * n + 2, :]
                step(dve.tensor_tensor(t2, PS[:, n, :].rearrange("p (a b) -> p a b", a=2), bc_mid(sin1, 2), ALU.mult))
                step(dve.tensor_tensor(src, src, bc_mid(cos1, 2), ALU.mult))
                settle()
                dve.tensor_tensor(src, src, t2, ALU.add).then_inc(*c.made(rot_done))

            n_u = len(UNITS1)

            def max1(u):
                kind, hp, q = UNITS1[u]
                dve.wait_ge(*c.need(s_ready))
                if kind == "A":
                    src = PS[:, 2 * (u % 3):2 * (u % 3) + 2, 0:SEQ]
                else:
                    for e in range(2):
                        slope = 2.0 ** -(2 * hp + e + 1)
                        if u - 2 >= 8 and e == 0:
                            dve.wait_ge(p_ready, u - 1)
                        step(dve.scalar_tensor_tensor(out=atmp[:, u % 2, e * SEQ:(e + 1) * SEQ], in0=far[q], scalar=slope,
                                                      in1=PS[:, 2 * (u % 3) + e, 0:SEQ], op0=ALU.mult, op1=ALU.add))
                    settle()
                    src = atmp[:, u % 2, :].rearrange("p (a b) -> p a b", a=2)
                dve.tensor_reduce(stat[:, 2 * u:2 * u + 2], src, AX.X, ALU.max, negate=True).then_inc(*c.made(max_ready))

            def weights1(u):
                kind, hp, q = UNITS1[u]
                dve.wait_ge(*c.need(p_ready))
                if u >= 2:
                    dve.wait_ge(*c.need(t_ready))
                src = prob[:, u % 2, 0:T]
                dst = amat[:, u % 2, :]
                rs = stat[:, 64 + 2 * u:66 + 2 * u]
                if kind == "A":
                    step(dve.reciprocal(stat[:, 160 + 2 * u:162 + 2 * u], rs))
                    dve.tensor_copy(dst, src).then_inc(*c.made(a_ready))
                else:
                    for e in range(2):
                        r = slice(e * SEQ, (e + 1) * SEQ)
                        ins = dve.scalar_tensor_tensor(out=dst[:, r], in0=src[:, r], scalar=1.0, in1=times_seen[q],
                                                       op0=ALU.mult, op1=ALU.mult, accum_out=rs[:, e:e + 1])
                        if e:
                            ins.then_inc(*c.made(a_ready))
                    settle(a_ready)
                    step(dve.reciprocal(stat[:, 160 + 2 * u:162 + 2 * u], rs))

            def out1(u):
                kind, hp, q = UNITS1[u]
                dve.wait_ge(*c.need(o_ready))
                c0 = (0 if kind == "A" else 512) + 2 * hp * HD
                dve.tensor_tensor(o1[:, q, c0:c0 + 2 * HD].rearrange("p (a b) -> p a b", a=2),
                                  PS[:, 7, 0:2 * HD].rearrange("p (a b) -> p a b", a=2),
                                  bc(stat[:, 160 + 2 * u:162 + 2 * u], HD), ALU.mult).then_inc(*c.made(o_done))

            for u in range(n_u + 2):
                if u < n_u:
                    max1(u)
                if 1 <= u <= n_u:
                    weights1(u - 1)
                if u >= 2:
                    settle()
                    out1(u - 2)
            c.skip(t_ready, 2)
            dve.wait_ge(*c.need(tok_rms))
            step(dve.reciprocal(stat[:, 144:148], stat[:, 136:140]))
            settle()
            settle(o_done)
            for t in range(LT):
                for e in range(2):
                    h = o1[:, t, e * 512:(e + 1) * 512]
                    dve.tensor_scalar(h, h, stat[:, 144 + 2 * t + e:145 + 2 * t + e], None, ALU.mult).then_inc(*c.made(tok_scaled))
            for k in range(KT):
                b = next_tile()
                dve.tensor_tensor(xT[:, k, 0:SEQ], xT[:, k, 0:SEQ], PS[:, b, 0:SEQ], ALU.add).then_inc(*c.made(dve_freed))
            stage()
            norm(lambda k, e: col("norm2_g", k), SEQ)

            for j in range(2):
                copy_mods(j)
            tile0 = tile[0]
            with c.loop(FFT // 2, [(tile_ready, 4), (conv_mid, 4), (dve_step, 4), (dve_freed, 4), (gate_act, 2), (conv_done, 2),
                                   (mod_ready, 2), (mod_read, 2)]) as i:
                for j in range(2):
                    for e in range(2):
                        b = (tile0 + 2 * j + e) % 4
                        dve.wait_ge(*c.need(conv_mid))
                        c.skip(tile_ready)
                        cv = cv1[:, j, e, :]
                        step(dve.scalar_tensor_tensor(out=cv[:, 1:SEQ], in0=PS[:, b, 0:SEQ - 1],
                                                      scalar=dcol("conv_w", 22 * e + j, i * 2), in1=cv[:, 1:SEQ],
                                                      op0=ALU.mult, op1=ALU.add))
                        settle()
                        dve.scalar_tensor_tensor(out=cv[:, 0:SEQ - 1], in0=PS[:, b, 1:SEQ],
                                                 scalar=dcol("conv_w", 88 + 22 * e + j, i * 2), in1=cv[:, 0:SEQ - 1],
                                                 op0=ALU.mult, op1=ALU.add).then_inc(*c.made(dve_freed))
                    dve.wait_ge(*c.need(gate_act))
                    settle(dve_freed)
                    dve.tensor_tensor(gate1[:, bass.ds(i * 2 + j, 1), :], cv1[:, 2 + j, 0:1, :], cv1[:, j, 1:2, :], ALU.mult)\
                        .then_inc(*c.made(conv_done))
                    copy_mods(i * 2 + (2 + j))
            mods[0] = N_MOD // 2
            tile[0] += 2 * FFT
            for k in range(KT):
                b = next_tile()
                dve.tensor_tensor(xT[:, k, 0:SEQ], xT[:, k, 0:SEQ], PS[:, b, 0:SEQ], ALU.add).then_inc(*c.made(dve_freed))
            stage()

            for l in range(LAYERS):
                halves = 2 if l == 0 else 1
                q_cols = halves * SEQ
                ny = len(y_chunks(l))
                settle(mod_read)
                ab = V[:, rows["ada_b_2"] + l * N_MOD:rows["ada_b_2"] + (l + 1) * N_MOD]
                step(dve.tensor_tensor(mod[:, :, :], mod_in[:, :, :], bc(ab, 2), ALU.add))
                settle()
                for dst, m0, name in ((amix, 8, "norm_mix_g_2"), (amlp, 32, "norm_mlp_g_2")):
                    g0 = rows[name] + l * KT
                    step(dve.scalar_tensor_tensor(out=dst[:, :, :], in0=mod[:, m0:m0 + KT, :], scalar=1.0, in1=bc(V[:, g0:g0 + KT], 2),
                                                  op0=ALU.add, op1=ALU.mult))
                dve.tensor_scalar(hgate[:, :, :], mod[:, 16:24, :], 0.5, None, ALU.mult).then_inc(*c.made(mods_ready))
                settle(mods_ready)
                norm(lambda k, e: amix[:, k, e:e + 1], T)

                passed(8 + 8)
                for n in range(2 * KT):
                    h = (qT if n < KT else kT)[:, n % KT, 0:SEQ]
                    dve.wait_ge(*c.need(rot_ready))
                    if n >= 2:
                        settle(rot_done)
                    step(dve.tensor_tensor(rot2[:, n % 2, :], PS[:, 4 + n % 4, 0:SEQ], sin2, ALU.mult))
                    step(dve.tensor_tensor(h, h, cos2, ALU.mult))
                    settle()
                    dve.tensor_tensor(h, h, rot2[:, n % 2, :], ALU.add).then_inc(*c.made(rot_done))
                passed(16)

                units = units2(l)
                n_u = len(units)

                def max2(u):
                    nk = T if units[u][1] < LT else SEQ
                    b = 2 * (u % 3)
                    dve.wait_ge(*c.need(s_ready))
                    dve.tensor_reduce(stat[:, 2 * u:2 * u + 2], PS[:, b:b + 2, 0:nk], AX.X, ALU.max, negate=True)\
                        .then_inc(*c.made(max_ready))

                def weights2(u):
                    nk = T if units[u][1] < LT else SEQ
                    dve.wait_ge(*c.need(p_ready, 2))
                    s0, s1 = (stat[:, 64 + 2 * u + e:65 + 2 * u + e] for e in range(2))
                    r0, r1 = (stat[:, 128 + 2 * u + e:129 + 2 * u + e] for e in range(2))
                    step(dve.reciprocal(stat[:, 128 + 2 * u:130 + 2 * u], stat[:, 64 + 2 * u:66 + 2 * u]))
                    settle()
                    step(dve.scalar_tensor_tensor(out=r1, in0=r1, scalar=neg_lam[:, l:l + 1], in1=s0, op0=ALU.mult, op1=ALU.mult))
                    settle()
                    if u >= 2:
                        dve.wait_ge(*c.need(t_ready))
                    dve.scalar_tensor_tensor(out=amat[:, u % 2, 0:nk], in0=prob[:, u % 2, T:T + nk], scalar=r1,
                                             in1=prob[:, u % 2, 0:nk], op0=ALU.mult, op1=ALU.add).then_inc(*c.made(a_ready))

                def out2(u):
                    h, q = units[u]
                    dve.wait_ge(*c.need(o_ready))
                    dve.tensor_scalar(o2[:, q, h * P:(h + 1) * P], PS[:, 7, 0:P], stat[:, 128 + 2 * u:129 + 2 * u], None,
                                      ALU.mult).then_inc(*c.made(o_done))

                for u in range(n_u + 2):
                    if u < n_u:
                        max2(u)
                    if 1 <= u <= n_u:
                        weights2(u - 1)
                    if u >= 2:
                        out2(u - 2)
                c.skip(t_ready, 2)
                dve.wait_ge(*c.need(tok_rms))
                lam_init = 0.8 - 0.6 * float(np.exp(-0.3 * l))
                n_st = ny * HEADS
                step(dve.reciprocal(stat[:, 192:192 + n_st], stat[:, 160:160 + n_st]))
                settle()
                step(dve.tensor_scalar(stat[:, 192:192 + n_st], stat[:, 192:192 + n_st], 1.0 - lam_init, None, ALU.mult))
                settle()
                settle(o_done)
                for t in range(ny):
                    h = o2[:, t, :].rearrange("p (h e) -> p h e", h=HEADS)
                    dve.tensor_tensor(h, h, bc(stat[:, 192 + t * HEADS:192 + (t + 1) * HEADS], P), ALU.mult)\
                        .then_inc(*c.made(tok_scaled))
                stage()

                for t in range(TT):
                    b = next_tile()
                    dve.tensor_tensor(dtx[0][:, t, :], PS[:, b, 0:64], head_in[:, l, 0:64], ALU.add).then_inc(*c.made(dve_freed))
                settle(dve_freed)
                step(dve.tensor_scalar(dt[:, :, :], dtx[0][:, :, :], 0.0, None, ALU.max).then_inc(*c.made(dt_abs))) if False else \
                    dve.tensor_scalar(dt[:, :, :], dtx[0][:, :, :], 0.0, None, ALU.max).then_inc(*c.made(dt_abs))
                dve.wait_ge(*c.need(dt_exp))
                dve.tensor_scalar(dtx[3][:, :, :], dtx[2][:, :, :], 1.0, None, ALU.add).then_inc(*c.made(dt_one))
                settle(dt_one)
                step(dve.scalar_tensor_tensor(out=dtx[5][:, :, :], in0=dtx[3][:, :, :], scalar=-1.0, in1=dtx[2][:, :, :],
                                              op0=ALU.add, op1=ALU.subtract))
                step(dve.reciprocal(dtx[1][:, :, :], dtx[3][:, :, :]))
                settle()
                step(dve.tensor_tensor(dtx[5][:, :, :], dtx[5][:, :, :], dtx[1][:, :, :], ALU.mult))
                dve.wait_ge(*c.need(dt_ln))
                settle()
                step(dve.tensor_tensor(dtx[4][:, :, :], dtx[4][:, :, :], dtx[5][:, :, :], ALU.subtract))
                settle()
                step(dve.tensor_tensor(dt[:, :, :], dt[:, :, :], dtx[4][:, :, :], ALU.add))
                settle()
                dve.tensor_tensor(dta[:, :, :], dt[:, :, :], bc_mid(neg_a[:, l, :], TT), ALU.mult).then_inc(*c.made(dta_ready))
                for t in range(TT):
                    step(dve.tensor_copy(by_head[:, t, 192:224], head_in[:, l, 128:160]))
                dve.wait_ge(*c.need(dec_exp, TT))
                for e in range(2):
                    step(dve.tensor_tensor(wst[:, :, 32 * e:32 * e + 32], dt[:, :, 32 * e:32 * e + 32],
                                           edec[:, :, 64 * e:64 * e + 32], ALU.mult))
                stage()

                nz = ny // 2
                cw = rows["conv_w_2"] + l * 160

                def heads_of(buf, t, c0, g, n=HD):
                    return buf[:, t, bass.ds(g * GH + c0, GH)].unsqueeze(2).broadcast_to([P, GH, n])

                def per_head(ap):
                    return ap.rearrange("p (r n) -> p r n", r=GH)

                def taps(g, p, j):
                    st, off = (2, j) if j < 2 else (1, 16 + 8 * (j - 2))
                    u = PS[:, j % 3, :].rearrange("p (s t) -> p s t", s=2)
                    cv = chan[p][:, j, :].rearrange("p (s t) -> p s t", s=2)
                    dve.wait_ge(*c.need(conv_mid))
                    c.skip(tile_ready)
                    for n, d in enumerate((-2, -1, 1, 2)):
                        to, fr = slice(max(0, -d), SEQ - max(0, d)), slice(max(0, d), SEQ - max(0, -d))
                        ins = dve.scalar_tensor_tensor(out=cv[:, :, to], in0=u[:, :, fr],
                                                       scalar=V[:, bass.ds(g * st + (cw + 32 * (d + 2) + off), 1)],
                                                       in1=cv[:, :, to], op0=ALU.mult, op1=ALU.add)
                        if n < 3:
                            step(ins)
                            settle()
                        else:
                            ins.then_inc(*c.made(dve_freed))

                def silu(p, j):
                    dve.wait_ge(*c.need(conv_tanh))
                    dve.scalar_tensor_tensor(out=chan[p][:, j, :], in0=ctanh[j % 2], scalar=1.0, in1=chan[p][:, j, :],
                                             op0=ALU.add, op1=ALU.mult).then_inc(*c.made(chan_ready))

                def gate_of_z(p, b):
                    dve.wait_ge(*c.need(z_tanh))
                    c.skip(tile_ready)
                    h = sz[p][:, 2 * b:2 * b + 2, :]
                    dve.scalar_tensor_tensor(out=h, in0=h, scalar=1.0, in1=PS[:, (4 + b) % 3, :].rearrange("p (t n) -> p t n", t=2),
                                             op0=ALU.add, op1=ALU.mult).then_inc(*c.made(dve_freed))

                def masks():
                    dve.wait_ge(*c.need(cb_ready))
                    cbp = PS[:, 6, 0:ny * P].rearrange("p (t l) -> p t l", t=ny)
                    step(dve.tensor_tensor(cb_lo[:, 0:ny, :], cbp, bc_mid(t_le, ny), ALU.mult))
                    dve.tensor_tensor(cb_up[:, 0:ny, :], cbp, bc_mid(t_ge, ny), ALU.mult).then_inc(*c.made(cb_masked))
                    settle(cb_masked)

                def weights(g, t):
                    lo = dt_lo[:, :, :]
                    step(dve.tensor_tensor(lo, bc_mid(cb_lo[:, t, :], GH), heads_of(dt, t, 0, g, P), ALU.mult))
                    dve.wait_ge(*c.need(dtu_ready))
                    settle()
                    step(dve.tensor_tensor(per_head(dt_up[:, t % 2, :]), lo, per_head(dt_up[:, t % 2, :]), ALU.add))
                    dve.wait_ge(*c.need(e_ready))
                    settle()
                    dve.tensor_tensor(ex[:, t % 2, :], dt_up[:, t % 2, :], ex[:, t % 2, :], ALU.mult).then_inc(*c.made(m_ready))

                def starts(g):
                    dve.wait_ge(*c.need(st_ready))
                    st = [PS[:, 3 + n // 2, (n % 2) * GW:(n % 2 + 1) * GW] for n in range(6)]
                    for d in range(2):
                        step(dve.tensor_copy(hin[:, 3 * d, :], st[3 * d]))
                    for n in range(1, 3):
                        settle()
                        for d, order in enumerate((F_STATES, B_STATES)):
                            step(dve.tensor_tensor(per_head(hin[:, 3 * d + n, :]), per_head(hin[:, 3 * d + n - 1, :]),
                                                   heads_of(edec, order[n], 128 + 32 * d, g), ALU.mult))
                        settle()
                        for d in range(2):
                            h = hin[:, 3 * d + n, :]
                            ins = dve.tensor_tensor(h, h, st[3 * d + n], ALU.add)
                            if n == 2 and d == 1:
                                ins.then_inc(*c.made(hin_ready))
                            else:
                                step(ins)

                def outputs(g, p, t):
                    dve.wait_ge(*c.need(y_ready))
                    dve.wait_ge(*c.need(xd_ready))
                    step(dve.tensor_tensor(ys, PS[:, 3 + t % 2, 0:GW], xd[:, t % 2, :], ALU.add))
                    for d, hs in enumerate((HF, HB)):
                        if t in hs:
                            step(dve.tensor_tensor(per_head(yi), per_head(PS[:, 5, d * GW:(d + 1) * GW]),
                                                   heads_of(edec, t, 32 + 64 * d, g), ALU.mult))
                            settle()
                            step(dve.tensor_tensor(ys, ys, yi, ALU.add))
                            settle()
                    dve.scalar_tensor_tensor(out=yg[:, t, bass.ds(g * GW, GW)], in0=ys, scalar=0.5, in1=sz[p][:, t, :],
                                             op0=ALU.mult, op1=ALU.mult).then_inc(*c.made(y_done))
                    settle(y_done)

                def turn_of(g, p, products=True):
                    nxt = g + 1
                    masks()
                    if products:
                        taps(nxt, 1 - p, 0)
                    weights(g, 0)
                    if products:
                        silu(1 - p, 0)
                    weights(g, 1)
                    if products:
                        taps(nxt, 1 - p, 1)
                    starts(g)
                    if products:
                        silu(1 - p, 1)
                        taps(nxt, 1 - p, 2)
                    for t in range(max(2, ny)):
                        outputs(g, p, t)
                        if products and t < 2:
                            silu(1 - p, 2 + t)
                        if t + 2 < ny:
                            weights(g, t + 2)
                        if products and t == 0:
                            taps(nxt, 1 - p, 3)
                        if products and 1 <= t <= nz:
                            gate_of_z(1 - p, t - 1)

                for j in range(4):
                    taps(0, 0, j)
                    silu(0, j)
                for b in range(nz):
                    gate_of_z(0, b)
                turn_of(0, 0)
                n_steps = 4 * 3 + 1 + 2 * ny + 2 + 7 + sum(1 + 2 * ((t in HF) + (t in HB)) for t in range(ny))
                counted = [(tile_ready, 4 + nz), (conv_mid, 4), (dve_step, n_steps), (dve_freed, 4 + nz),
                           (conv_tanh, 4), (chan_ready, 4), (z_tanh, nz), (cb_ready, 1), (cb_masked, 1),
                           (dtu_ready, ny), (e_ready, ny), (m_ready, ny), (st_ready, 1), (hin_ready, 1),
                           (y_ready, ny), (xd_ready, ny), (y_done, ny)]
                with c.loop(GROUPS // 2 - 1, [(q, 2 * k) for q, k in counted]) as i:
                    turn_of(i * 2 + 1, 1)
                    turn_of(i * 2 + 2, 0)
                turn_of(GROUPS - 1, 1, products=False)
                tile[0] += (4 + nz) * GROUPS
                stage()
                dve.wait_ge(*c.need(tok_rms))
                step(dve.reciprocal(stat[:, 192:192 + ny], stat[:, 160:160 + ny]))
                settle()
                for t in range(ny):
                    dve.tensor_scalar(yg[:, t, :], yg[:, t, :], stat[:, 192 + t:193 + t], None, ALU.mult).then_inc(*c.made(tok_scaled))
                stage()

                def gate(dst):
                    with c.loop(2, [(tile_ready, 4), (dve_freed, 4)]) as i:
                        for j in range(4):
                            b = next_tile()
                            h = dst[:, bass.ds(i * 4 + j, 1), 0:q_cols]
                            dve.scalar_tensor_tensor(out=h, in0=h, scalar=1.0, in1=PS[:, b:b + 1, 0:q_cols], op0=ALU.add,
                                                     op1=ALU.mult).then_inc(*c.made(dve_freed))

                passed(KT)
                dve.wait_ge(act_freed, act_total(l, 1))
                gate(merged)
                passed(KT)
                dve.wait_ge(act_freed, act_total(l, 2))
                gate(gs)
                settle(dve_freed)
                for k in range(KT):
                    dve.tensor_tensor(merged[:, k, 0:q_cols], merged[:, k, 0:q_cols], gs[:, k, 0:q_cols], ALU.add)\
                        .then_inc(*c.made(gated))

                more = l + 1 < LAYERS

                def add_gated(gate_of, mods_from=None):
                    for k in range(KT):
                        if mods_from is not None:
                            copy_mods(mods_from + k)
                        b = next_tile()
                        for e in range(halves):
                            r = slice(e * SEQ, (e + 1) * SEQ)
                            ins = dve.scalar_tensor_tensor(out=xT[:, k, r], in0=PS[:, b, r], scalar=gate_of(k, e), in1=xT[:, k, r],
                                                           op0=ALU.mult, op1=ALU.add)
                            if e == halves - 1:
                                ins.then_inc(*c.made(dve_freed))

                add_gated(lambda k, e: hgate[:, k, e:e + 1])
                stage()
                norm(lambda k, e: amlp[:, k, e:e + 1], q_cols)
                for n in range(HIDT):
                    b = next_tile()
                    dve.tensor_scalar(hidden(n)[:, 0:q_cols], PS[:, b, 0:q_cols], 0.0, None, ALU.max).then_inc(*c.made(dve_freed))
                    if more and n % 2:
                        copy_mods(n // 2)
                add_gated(lambda k, e: mod[:, 40 + k, e:e + 1], HIDT // 2 if more else None)
                stage()

            norm(lambda k, e: col("final_norm_g_2", k), SEQ)

        @block.gpsimd
        def _(pool):
            c = Counts(pool)
            fences = [0]

            def stage():
                pool.drain().then_inc(*c.made(fence))
                fences[0] += 1
                pool.wait_ge(fence, 4 * fences[0])

            def bc_mid(ap, n):
                return ap.unsqueeze(1).broadcast_to([P, n, ap.shape[1]])

            def heads_of(t, kind, n):
                return of_group[:, t, kind, :].unsqueeze(2).broadcast_to([P, GH, n])

            def per_head(ap):
                return ap.rearrange("p (r n) -> p r n", r=GH)

            stage()
            stage()
            stage()
            for l in range(LAYERS):
                ny = len(y_chunks(l))
                stage()
                stage()

                def group(g, first=False):
                    pool.tensor_copy(of_group[:, :, :, :].rearrange("p t k r -> p (t k) r"),
                                     by_head[:, :, :].rearrange("p t (k n) -> p (t k) n", k=7)[:, :, bass.ds(g * GH, GH)])\
                        .then_inc(*c.made(pool_step))
                    pool.wait_ge(*c.sofar(pool_step))

                    def seg(t):
                        if t >= 2 or not first:
                            pool.wait_ge(*c.need(seg_ready))
                        pool.tensor_tensor(seg_f[:, t % 2, :, :], bc_mid(t_le, GH), heads_of(t, 2, P), ALU.mult)\
                            .then_inc(*c.made(seg_in))
                        pool.tensor_tensor(seg_b[:, t % 2, :, :], bc_mid(t_ge, GH), heads_of(t, 3, P), ALU.mult)\
                            .then_inc(*c.made(seg_in))

                    def dtu(t):
                        if t >= 2:
                            pool.wait_ge(*c.need(m_ready))
                        pool.tensor_tensor(per_head(dt_up[:, t % 2, :]), bc_mid(cb_up[:, t, :], GH), heads_of(t, 1, P),
                                           ALU.mult).then_inc(*c.made(dtu_ready))

                    def skip_of(t):
                        if t >= 2:
                            pool.wait_ge(*c.need(y_done))
                        pool.tensor_tensor(per_head(xd[:, t % 2, :]), per_head(xtok[:, t, :]),
                                           heads_of(t, 6, HD),
                                           ALU.mult).then_inc(*c.made(xd_ready))

                    seg(0)
                    seg(1)
                    pool.wait_ge(*c.need(tok_ready, 3))
                    for n, t in enumerate(F_STATES + B_STATES):
                        pool.tensor_tensor(per_head(xw[:, n, :]), per_head(xtok[:, t, :]), heads_of(t, 4 + n // 3, HD),
                                           ALU.mult).then_inc(*c.made(xw_ready))
                    pool.wait_ge(*c.need(cb_masked))
                    for t in range(2):
                        dtu(t)
                        skip_of(t)
                    for t in range(2, ny):
                        seg(t)
                        dtu(t)
                        skip_of(t)
                    c.skip(m_ready, 2)
                    c.skip(y_done, 2)
                    pool.wait_ge(*c.sofar(xd_ready))

                group(0, first=True)
                with c.loop(GROUPS - 1, [(pool_step, 1), (seg_in, 2 * ny), (tok_ready, 3), (xw_ready, 6), (cb_masked, 1),
                                         (dtu_ready, ny), (xd_ready, ny), (seg_ready, ny), (m_ready, ny), (y_done, ny)]) as i:
                    group(i + 1)
                c.skip(seg_ready, 2)
                for _ in range(4):
                    stage()


_INS = [
    "x", "norm1_g", "w_in", "qa_norm_g", "ka_norm_g", "qb_norm_g", "kb_norm_g", "outa_norm_g", "outb_norm_g",
    "w_out", "norm2_g", "w_up", "conv_w", "conv_b", "w_down", "c_2", "ctx_2", "c_ctx_2", "ada_w_2", "ada_b_2",
    "norm_mix_g_2", "w_in_2", "conv_w_2", "conv_b_2", "dt_bias_f_2", "dt_bias_b_2", "a_log_f_2", "a_log_b_2",
    "ssd_d_2", "ssd_norm_g_2", "lambda_q1_2", "lambda_k1_2", "lambda_q2_2", "lambda_k2_2", "attn_subln_g_2",
    "w_attn_o_2", "w_ssd_o_2", "w_out_2", "norm_mlp_g_2", "w_mlp1_2", "w_mlp2_2", "final_norm_g_2",
]
_OUT = (1, SEQ, D)


def kernel(**inputs):
    import concourse.bacc as _bacc
    from concourse.bass_utils import run_bass_kernel_spmd as _run

    nc = _bacc.Bacc("TRN2", target_bir_lowering=False, num_devices=1)
    arrays, aps = {}, {}
    for name in _INS:
        arr = np.ascontiguousarray(inputs[name])
        arrays[f"in_{name}_dram"] = arr
        aps[name] = nc.dram_tensor(f"in_{name}_dram", arr.shape, mybir.dt.from_np(arr.dtype), kind="ExternalInput").ap()
    table = shape_constants()
    arrays["in_shape_constants_dram"] = table
    const = nc.dram_tensor("in_shape_constants_dram", table.shape, F32, kind="ExternalInput").ap()
    out = nc.dram_tensor("out_0_dram", _OUT, F32, kind="ExternalOutput").ap()
    two_blocks(nc, aps, const, out)
    r = _run(nc, [arrays], core_ids=[0])
    return r.results[0]["out_0_dram"]
```

```python
from contextlib import ExitStack, contextmanager

import numpy as np

import concourse.bass as bass
from concourse import mybir

F32 = mybir.dt.float32
F32R = mybir.dt.float32r
ALU = mybir.AluOpType
ACT = mybir.ActivationFunctionType
AX = mybir.AxisListType

P = 128
SEQ = 256
T = 2 * SEQ
D = 1024
KT = D // P
LT = SEQ // P
TT = T // P
HD = 64
HEADS = 8
D_FF = 2816
FFT = D_FF // P
EPS = 1e-6
LAYERS = 2
SSD_IN = 2048
GROUPS = 8
GH = 4
GW = GH * HD
SSD_HEADS = 32
HID = 4096
HIDT = HID // P
YT = SSD_IN // P
N_MOD = 48
SLOTS = 4
SLAB = 2048
C_Z, C_X, C_B, C_C, C_DT, C_GA, C_GS = 3072, 5120, 7168, 8192, 9216, 9280, 10304


def shape_constants():
    i, j = np.arange(P)[:, None], np.arange(P)[None, :]
    ident = (i == j).astype(np.float32)
    heads = (i // HD == j // HD).astype(np.float32)
    ones = np.ones((P, P), np.float32)

    def turn(half):
        m = np.zeros((P, P), np.float32)
        for p in range(P):
            if p % (2 * half) < half:
                m[p + half, p] = -1.0
            else:
                m[p - half, p] = 1.0
        return m

    row = np.repeat(np.arange(4, dtype=np.float32), 64)
    col = np.tile(np.arange(64, dtype=np.float32), 4)
    inv = np.float32(10000.0) ** (-np.arange(16, dtype=np.float32) / np.float32(16))
    ang1 = np.zeros((P, SEQ), np.float32)
    ang2 = np.zeros((P, SEQ), np.float32)
    for p in range(P):
        d = p % HD
        ang1[p] = (row if d < 32 else col) * inv[d % 16]
        e = p % 32
        ang2[p] = (row if e < 16 else col) * inv[e % 16]
    cols = [ident, heads, ones, turn(16), turn(32),
            (i > j), (i < j), (i <= j), (i >= j),
            np.cos(ang1), np.sin(ang1), np.cos(ang2), np.sin(ang2)]
    for q in range(LT):
        dist = np.abs(np.arange(SEQ)[None, :] - (q * P + np.arange(P))[:, None])
        count = (dist <= 64).astype(np.float32) + (dist % 4 == 0) + (dist % 16 == 0)
        cols += [np.where(count > 0, -dist, -1e30), count]
    cols += [np.arange(P)[:, None] % 32 == np.arange(2)[None, :]]
    return np.ascontiguousarray(np.concatenate([np.asarray(c, np.float32) for c in cols], axis=1))


class Counts:

    def __init__(self, eng):
        self.eng, self.n, self.i, self.per = eng, {}, None, {}

    def skip(self, sem, k=1):
        self.n[sem.name] = self.n.get(sem.name, 0) + k

    def value(self, sem):
        n = self.n.get(sem.name, 0)
        if self.i is not None and self.per.get(sem.name):
            return self.i * self.per[sem.name] + n
        return n

    def made(self, sem, k=1):
        self.skip(sem, k)
        return sem, k

    def need(self, sem, k=1):
        self.skip(sem, k)
        return sem, self.value(sem)

    def sofar(self, sem):
        return sem, self.value(sem)

    @contextmanager
    def loop(self, times, per):
        with self.eng.Fori(0, times) as i:
            start = dict(self.n)
            self.i, self.per = i, {s.name: k for s, k in per}
            yield i
            for name, n in self.n.items():
                moved = n - start.get(name, 0)
                assert moved == self.per.get(name, 0), (name, moved)
            for name, k in self.per.items():
                self.n[name] = start.get(name, 0) + k * times
            self.i, self.per = None, {}


def two_blocks(nc, a, const, out):
    with ExitStack() as ctx:
        def sb(name, shape):
            return ctx.enter_context(nc.sbuf_tensor(name, shape, F32))

        def sem(name):
            return ctx.enter_context(nc.semaphore(name))

        PS = ctx.enter_context(nc.psum_tensor("PS", [P, 8, 512], F32))
        n_const = const.shape[1]
        K = sb("constants", [P, n_const])
        AT, n_work = {}, 0
        with ExitStack() as plain:
            def work(name, *shape):
                nonlocal n_work
                AT[name] = n_work
                n_work += int(np.prod(shape))
                return plain.enter_context(nc.sbuf_tensor(name, [P, *shape], F32))

            xT = work("xT", KT, T)
            hT = work("hT", KT, T)
            ring = work("ring", SLOTS, SLAB)
            big1 = work("big1", 8192)
            big2 = work("big2", 8192)
            mid_v = work("mid_v", 4096)
            mid_o = work("mid_o", 4096)
            mid_a = work("mid_a", 4096)
        R = ctx.enter_context(nc.sbuf_tensor("rounded", [P, n_work], F32R))

        def view(buf, at, *dims):
            n = int(np.prod(dims))
            flat = buf[:, at:at + n]
            if len(dims) == 1:
                return flat
            if len(dims) == 2:
                return flat.rearrange("p (a b) -> p a b", a=dims[0])
            return flat.rearrange("p (a b c) -> p a b c", a=dims[0], b=dims[1])

        ident, heads, ones, turn1, turn2, t_gt, t_lt, t_le, t_ge = (
            K[:, n * P:(n + 1) * P] for n in range(9))
        at = 9 * P
        cos1, sin1, cos2, sin2 = (K[:, at + n * SEQ:at + (n + 1) * SEQ] for n in range(4))
        at += 4 * SEQ
        far = [K[:, at + 2 * q * SEQ:at + (2 * q + 1) * SEQ] for q in range(LT)]
        times_seen = [K[:, at + (2 * q + 1) * SEQ:at + (2 * q + 2) * SEQ] for q in range(LT)]

        by_cond = K[:, at + 2 * LT * SEQ:at + 2 * LT * SEQ + 2]

        rows, pieces = {}, []
        n_rows = 0

        def vector(name, src):
            nonlocal n_rows
            rows[name] = n_rows
            n, k = src.shape[0], 0
            while k < n:
                m = min(n - k, P - n_rows % P)
                pieces.append((n_rows // P, n_rows % P, m, src[k:k + m, :]))
                n_rows += m
                k += m

        flat1 = "(a b) -> a b"
        flat2 = "l (a b) -> (l a) b"
        for name in ("norm1_g", "norm2_g", "conv_b", "c_ctx_2", "final_norm_g_2", "outa_norm_g", "outb_norm_g"):
            vector(name, a[name].rearrange(flat1, b=P))
        vector("conv_w", a["conv_w"].rearrange(flat2, b=P))
        for name in ("c_2", "ada_b_2", "norm_mix_g_2", "norm_mlp_g_2", "ssd_norm_g_2", "attn_subln_g_2"):
            vector(name, a[name].rearrange(flat2, b=P))
        vector("conv_w_2", a["conv_w_2"].rearrange("l t (a b) -> (l t a) b", b=P))
        vector("conv_b_2", a["conv_b_2"].rearrange(flat2, b=P))
        for name in ("qa_norm_g", "qb_norm_g", "ka_norm_g", "kb_norm_g"):
            rows[name] = n_rows
            n_rows += 1
        n_stage = -(-n_rows // P)
        vstage = view(big2, 0, n_stage, P)
        V = sb("V", [P, n_rows])

        def col(name, j=0):
            return V[:, rows[name] + j:rows[name] + j + 1]

        def dcol(name, j, i):
            return V[:, bass.ds(i + (rows[name] + j), 1)]

        lam_in = sb("lam_in", [P, LAYERS, 4, HD])
        lam_s = sb("lam_s", [P, 3 * LAYERS * 2])
        neg_lam = sb("neg_lam", [P, LAYERS])
        head_in = sb("head_in", [P, LAYERS, 5 * SSD_HEADS])
        neg_a = sb("neg_a", [P, LAYERS, 2 * SSD_HEADS])
        cact = sb("cact", [P, KT, 32])
        ctan = sb("ctan", [P, KT, 2])
        craw = sb("craw", [P, KT, 2])
        mod = sb("mod", [P, N_MOD, 2])
        mod_in = sb("mod_in", [P, N_MOD, 2])
        ctanh_b = sb("ctanh_b", [P, T])
        amix = sb("amix", [P, KT, 2])
        amlp = sb("amlp", [P, KT, 2])
        hgate = sb("hgate", [P, KT, 2])
        eps = sb("eps", [P, 1])
        stat = sb("stat", [P, 256])
        by_head = sb("by_head", [P, TT, 7 * SSD_HEADS])
        dt, dta, wst = (by_head[:, :, n * 64:(n + 1) * 64] for n in range(3))
        of_group = sb("of_group", [P, TT, 7, GH])
        edec = sb("edec", [P, TT, 192])

        rms = ctanh_b[:, :]
        rstd = by_head[:, :, :].rearrange("p t n -> p (t n)")[:, 0:T]
        xin = view(mid_o, 0, TT, D)

        const_loaded, tables_loaded, x_loaded, vec_loaded, small_loaded = map(
            sem, ("const_loaded", "tables_loaded", "x_loaded", "vec_loaded", "small_loaded"))
        slot_loaded = [sem(f"slot_loaded{s}") for s in range(SLOTS)]
        mod_ready = sem("mod_ready")
        mod_copied = sem("mod_copied")
        mod_turned = sem("mod_turned")
        mod_read = sem("mod_read")
        tile_ready = sem("tile_ready")
        act_freed = sem("act_freed")
        dve_freed = sem("dve_freed")
        turned = sem("turned")
        turned_freed = sem("turned_freed")
        fence = sem("fence")
        act_step = sem("act_step")
        dve_step = sem("dve_step")
        pool_step = sem("pool_step")
        squares, mean_sq, rms_ready, scaled, shifted = map(
            sem, ("squares", "mean_sq", "rms_ready", "scaled", "shifted"))
        vec_ready, lam_sum, lam_exp, cond_tanh, cond_ready, mods_ready = map(
            sem, ("vec_ready", "lam_sum", "lam_exp", "cond_tanh", "cond_ready", "mods_ready"))
        head_sq, head_ms, head_rms, head_normed, rot_ready, rot_done = map(
            sem, ("head_sq", "head_ms", "head_rms", "head_normed", "rot_ready", "rot_done"))
        s_ready, max_ready, p_ready, a_ready, t_ready, at_ready, o_ready, o_done = map(
            sem, ("s_ready", "max_ready", "p_ready", "a_ready", "t_ready", "at_ready", "o_ready", "o_done"))
        y_summed, tok_rms, tok_scaled = map(sem, ("y_summed", "tok_rms", "tok_scaled"))
        conv_mid, conv_done, gate_act = map(sem, ("conv_mid", "conv_done", "gate_act"))
        dt_abs, dt_exp, dt_one, dt_ln, dta_ready, dec_ready, dec_exp = map(
            sem, ("dt_abs", "dt_exp", "dt_one", "dt_ln", "dta_ready", "dec_ready", "dec_exp"))
        conv_tanh, chan_ready, z_tanh = map(sem, ("conv_tanh", "chan_ready", "z_tanh"))
        tok_turned, tok_ready, cb_ready, cb_masked, seg_in, seg_ready, e_ready, dtu_ready, m_ready = map(
            sem, ("tok_turned", "tok_ready", "cb_ready", "cb_masked", "seg_in", "seg_ready", "e_ready",
                  "dtu_ready", "m_ready"))
        xw_ready, xd_ready, st_ready, hin_ready, y_ready, y_done = map(
            sem, ("xw_ready", "xd_ready", "st_ready", "hin_ready", "y_ready", "y_done"))
        split_ready = sem("split_ready")
        round_ready = sem("round_ready")
        hi_ready = sem("hi_ready")
        lo_ready = sem("lo_ready")
        put_aside = sem("put_aside")
        taken_back = sem("taken_back")
        squared = sem("squared")
        gated, out_ready, stored = map(sem, ("gated", "out_ready", "stored"))

        slab_loaded, slab_freed, slab_used, first_slab = [], [], [], {}

        mods_after = [(0, 2, 4, 6), (0, 2)]

        def part_of_slab(at, n, kt, width):
            return view(R, at[n % len(at)], kt, width)

        def lo_slab(s, kt, width):
            return view(R, AT["ring"] + s * SLAB, kt, width)

        x_aside, merged_aside = (nc.dram_tensor(name, (P, KT * T), F32, kind="Internal").ap()
                                 for name in ("x_aside", "merged_aside"))

        def aside(buf, cols):
            return buf[:, 0:KT * cols].rearrange("p (k n) -> p k n", k=KT)

        block = ctx.enter_context(nc.Block())

        def tiles(w):
            return w.rearrange("(k p) n -> p k n", p=P)

        w_in, w_out, w_up, w_down = (tiles(a[n]) for n in ("w_in", "w_out", "w_up", "w_down"))

        def of_layer(name, l):
            return tiles(a[name][l])

        def slot(s, kt, width):
            return ring[:, s, 0:kt * width].rearrange("p (k n) -> p k n", k=kt)

        raw1 = view(big1, 0, 14, SEQ)
        sq1 = view(big2, 0, 14, SEQ)
        v1 = view(mid_v, 0, LT, 640)
        rot1 = view(big1, 14 * SEQ, 3, 2 * SEQ)
        o1 = view(mid_o, 0, LT, D)
        mix1 = view(mid_a, 0, KT, SEQ)
        cv1 = view(big2, 0, 4, 2, SEQ)
        qT = [view(big1, 0, KT, T), view(big1, 0, KT, SEQ)]
        kT = view(big1, KT * T, KT, T)
        v2 = view(mid_v, 0, TT, D)
        rot2 = edec[:, :, :].rearrange("p t n -> p (t n)")[:, 0:2 * SEQ].rearrange("p (a b) -> p a b", a=2)
        mod_rows = rot2
        o2 = view(mid_o, 0, TT, D)
        prob = view(big2, 0, 2, 2 * T)
        amat = view(big2, 4 * T, 2, T)
        amatT = view(big2, 6 * T, 2, T)
        atmp = view(big2, 8 * T, 2, T)
        yg = view(big2, 0, TT, SSD_IN)
        junk = view(mid_v, 0, SSD_IN)
        squares_out = lam_in[:, 0, :, :].rearrange("p a b -> p (a b)")
        merged = [view(mid_a, 0, KT, T), view(mid_a, 0, KT, SEQ)]
        gs = view(big2, KT * T, KT, T)
        def slabs_at(*names):
            return [AT[name] + n * SLAB for name in names for n in range(2)]

        mix_at = [slabs_at("big2"), slabs_at("big2") + [AT["mid_a"] + SLAB, AT["big1"] + SLAB]]
        gate_at = [slabs_at("big2"), slabs_at("big2") + [AT["big1"] + 2 * SLAB, AT["big1"] + 3 * SLAB]]
        mlp_at = [slabs_at("mid_o"), slabs_at("mid_o", "mid_a")]
        h_hi, h_lo = view(R, AT["mid_o"], KT, T), view(R, AT["big2"] + KT * T, KT, T)

        def by_layer(name, tiles_n, at=0):
            return [view(R, AT[name] + at, tiles_n, T), view(R, AT[name] + at, tiles_n, SEQ)]

        att_hi, att_lo = by_layer("big1", KT), by_layer("big1", KT, KT * T)
        y_hi, y_lo = by_layer("big1", YT), by_layer("mid_v", YT)
        hs_hi, hs_lo = view(R, AT["mid_a"], KT, T), view(R, AT["hT"], KT, T)

        def group_hi(s, q):
            return AT["ring"] + s * SLAB + SLAB // 2 if q < 2 else AT["xT"] + (q - 2) * SLAB

        merged_hi, merged_lo = by_layer("hT", KT), by_layer("mid_a", KT)
        hm_hi = [view(R, AT["mid_v"], KT, T), view(R, AT["mid_v"], KT, SEQ)]
        hm_lo = view(R, AT["hT"], KT, T)
        ffn_hi, ffn_lo = view(R, AT["big1"], FFT, SEQ), view(R, AT["big2"] + 8 * SEQ, FFT, SEQ)
        up_at, up_rest_at, down_at = slabs_at("mid_o"), slabs_at("mid_a"), slabs_at("mid_a", "mid_o")
        hid_hi, hid_lo = ([view(R, AT[big], YT, T), view(R, AT[big], HIDT, SEQ)] for big in ("big1", "big2"))
        relu = [view(mid_a, 0, 2, T), view(mid_v, KT * SEQ, 2, SEQ)]
        relu2 = [view(mid_a, 2 * T, 2, T), view(mid_v, (KT + 2) * SEQ, 2, SEQ)]

        chan = [view(mid_o, 4 * T * n, 4, T) for n in range(2)]
        at = 9 * P
        ctanh = [K[:, at:at + T], ctanh_b[:, :]]
        sz = [view(big1, 7168, TT, GW), view(K, at + 4 * SEQ, TT, GW)]
        xtok = view(big1, 0, TT, GW)
        btok = view(big1, 1024, TT, P)
        cb_lo = view(big1, 1536, TT, P)
        cb_up = view(big1, 2048, TT, P)
        seg_f = view(big1, 2560, 2, GH, P)
        seg_b = view(big1, 3584, 2, GH, P)
        ex = view(big1, 4608, 2, GH * P)
        dt_lo = view(big1, 5632, GH, P)
        dt_up = view(big1, 6144, 2, GH * P)
        xw = view(mid_v, 0, 6, GW)
        hin = view(mid_v, 1536, 6, GW)
        ys = view(mid_v, 3072, GW)
        yi = view(mid_v, 3328, GW)
        xd = view(mid_v, 3584, 2, GW)
        dtx = [view(big1, n * 256, TT, 2 * SSD_HEADS) for n in range(6)]

        def y_chunks(l):
            return range(TT) if l == 0 else range(LT)

        F_STATES = [2, 3, 0]
        B_STATES = [3, 2, 1]
        HF = {3: 0, 0: 1, 1: 2}
        HB = {2: 3, 1: 4, 0: 5}

        def units2(l):
            return [(h, q) for h in range(HEADS) for q in range(TT if l == 0 else LT)]

        UNITS1 = [(kind, hp, q) for kind in "AB" for hp in range(4) for q in range(LT)]

        @block.sync
        def _(sp):
            c = Counts(sp)
            done = slab_freed
            loaded = [0] * SLOTS
            total = [0]

            def booked(freed_at, n=1, used_at=None):
                s = len(done) % SLOTS
                loaded[s] += 16 * n
                slab_loaded.append((slot_loaded[s], loaded[s]))
                done.append(freed_at)
                slab_used.append(used_at or freed_at)

            sp.dma_start(K[:, 0:3 * P], const[:, 0:3 * P]).then_inc(const_loaded, 16)
            sp.dma_start(xin[:, 0:LT, :], a["x"][0].rearrange("(t p) d -> p t d", p=P)).then_inc(x_loaded, 16)
            sp.dma_start(xin[:, LT:TT, :], a["ctx_2"][0].rearrange("(t p) d -> p t d", p=P)).then_inc(x_loaded, 16)

            sp.wait_ge(vec_loaded, 16 * (len(pieces) + 8))
            sp.dma_start(K[:, 3 * P:], const[:, 3 * P:]).then_inc(tables_loaded, 16)

            mods = [0]

            def freed(slab):
                if slab >= SLOTS:
                    sp.wait_ge(*done[slab - SLOTS])

            def load(parts, tiles_after):
                s = len(done) % SLOTS
                freed(len(done))
                for dst, src in parts(s):
                    sp.dma_start(dst, src).then_inc(slot_loaded[s], 16)
                booked((tile_ready, total[0] + tiles_after), len(parts(s)))

            def load_mods(ada):
                s = len(done) % SLOTS
                freed(len(done))
                j = mods[0] % (N_MOD // 2)
                sp.dma_start(slot(s, KT, 256), ada[:, :, j * 256:(j + 1) * 256]).then_inc(slot_loaded[s], 16)
                mods[0] += 1
                booked((mod_ready, mods[0]))

            def slabs(n, kt, width, src, tiles_done, body=SLOTS, parts=None):
                parts = parts or (lambda s, j: [(slot(s, kt, width), src(j))])
                turns = n // body
                first = body if turns >= 3 else n
                for j in range(first):
                    load(lambda s: parts(s, j), tiles_done(j + 1))
                if turns >= 3:
                    slope = tiles_done(2 * body) - tiles_done(body)
                    s0 = len(done) - body
                    with sp.Fori(1, turns) as i:
                        for q in range(body):
                            s = (s0 + q) % SLOTS
                            sp.wait_ge(tile_ready, i * slope + (total[0] + tiles_done(body + q - SLOTS + 1) - slope))
                            for dst, part in parts(s, i * body + q):
                                sp.dma_start(dst, part).then_inc(slot_loaded[s], 16)
                    for j in range(body, body * turns):
                        booked((tile_ready, total[0] + tiles_done(j + 1)), len(parts(0, 0)))
                    for j in range(body * turns, n):
                        load(lambda s: parts(s, j), tiles_done(j + 1))
                total[0] += tiles_done(n)

            def slabs_and_mods(n, parts, ada, copied=False):
                def turn(j, i, wait):
                    for q in range(2):
                        for m in range(2):
                            s = (s0 + 2 * q + m) % SLOTS
                            wait(q, m)
                            if m == 0:
                                for dst, src in parts(s, j + q):
                                    sp.dma_start(dst, src).then_inc(slot_loaded[s], 16)
                            else:
                                sp.dma_start(slot(s, KT, 256), ada[:, :, bass.ds(j * 256 + (m0 + q) * 256, 256)])\
                                    .then_inc(slot_loaded[s], 16)

                s0, m0 = len(done), mods[0] % (N_MOD // 2)
                turn(0, 0, lambda q, m: freed(s0 + 2 * q + m))
                with sp.Fori(1, n // 2) as i:
                    turn(i * 2, i, lambda q, m:
                         sp.wait_ge(split_ready, i * 2 + (q - 1)) if m == 0 and copied else
                         sp.wait_ge(tile_ready, i * 4 + (total[0] + 2 * q - 2)) if m == 0 else
                         sp.wait_ge(mod_ready, i * 2 + (mods[0] + q - 1)))
                for j in range(n):
                    used = (tile_ready, total[0] + 2 * (j + 1))
                    booked((split_ready, j + 1) if copied else used, len(parts(0, 0)), used)
                    mods[0] += 1
                    booked((mod_ready, mods[0]))
                total[0] += 2 * n

            def wide(w, c0, n, per=2):
                slabs(n, KT, 256, lambda j: w[:, :, bass.ds(j * 256 + c0, 256)], lambda j: per * j)

            wide(w_in, 0, 2)
            slabs(1, KT, 256, None, lambda j: 2 * j, parts=lambda s, j: [
                (slot(s, KT, 256)[:, :, n * HD:(n + 1) * HD], w_in[:, :, 512 + HD * (n // 2):576 + HD * (n // 2)])
                for n in range(4)])
            slabs(1, KT, 128, lambda j: w_in[:, :, 640:768], lambda j: 2 * j)
            wide(w_in, 768, 6)
            wide(w_out, 0, 4)
            ada = of_layer("ada_w_2", 0)
            for _ in range(2):
                load_mods(ada)
            first_slab["up"] = len(done)
            slabs_and_mods(FFT, lambda s, j: [
                (slot(s, KT, 256)[:, :, 0:P], w_up[:, :, bass.ds(j * P, P)]),
                (slot(s, KT, 256)[:, :, P:2 * P], w_up[:, :, bass.ds(j * P + D_FF, P)])], ada, copied=True)
            halves = FFT // 2
            first_slab["down"] = len(done)
            for n in range(KT):
                slabs(2, halves, P, lambda j: w_down[:, halves * j:halves * (j + 1), n * P:(n + 1) * P],
                      lambda j: (j + 1) // 2)

            for l in range(LAYERS):
                wi = of_layer("w_in_2", l)
                first_slab["q", l] = len(done)
                wide(wi, 0, 4)
                wide(wi, 1024, 4)
                wide(wi, 2048, 4, per=TT)
                wide(wi, C_GA, 4)
                wide(of_layer("w_attn_o_2", l), 0, 4)
                slabs(1, KT, 64, lambda j: wi[:, :, C_DT:C_DT + 64], lambda j: TT * j)
                nz = len(y_chunks(l)) // 2
                per_group = 4 + nz
                after = [1, 2, 4, per_group]

                def group_parts(s, q, g):
                    half = slot(s, KT, P)
                    full = slot(s, KT, 256)
                    if q < 2:
                        return [(half, wi[:, :, bass.ds(g * GW + (C_X + q * P), P)])]
                    if q == 2:
                        return [(full[:, :, 0:P], wi[:, :, bass.ds(g * P + C_B, P)]),
                                (full[:, :, P:2 * P], wi[:, :, bass.ds(g * P + C_C, P)])]
                    return [(full, wi[:, :, bass.ds(g * GW + C_Z, GW)])]

                s0 = len(done)
                first_slab["ssd", l] = s0
                for q in range(4):
                    load(lambda s: group_parts(s, q, 0), after[q])
                with sp.Fori(1, GROUPS) as g:
                    for q in range(4):
                        s = (s0 + q) % SLOTS
                        sp.wait_ge(tile_ready, g * per_group + (total[0] + after[q] - per_group))
                        for dst, src in group_parts(s, q, g):
                            sp.dma_start(dst, src).then_inc(slot_loaded[s], 16)
                for g in range(1, GROUPS):
                    for q, n in enumerate(after):
                        booked((tile_ready, total[0] + per_group * g + n), 2 if q == 2 else 1)
                total[0] += per_group * GROUPS
                first_slab["gs", l] = len(done)
                wide(wi, C_GS, 4)
                wo = of_layer("w_ssd_o_2", l)
                slabs(KT, YT, P, lambda j: wo[:, :, bass.ds(j * P, P)], lambda j: j)
                wide(of_layer("w_out_2", l), 0, 4)
                w1, w2 = of_layer("w_mlp1_2", l), of_layer("w_mlp2_2", l)
                first_slab["mlp", l] = len(done)
                if l == 0:
                    ada = of_layer("ada_w_2", l + 1)
                    for _ in range(2):
                        load_mods(ada)
                    for half in range(2):
                        slabs_and_mods(HIDT // 4, lambda s, j: [
                            (slot(s, KT, 256), w1[:, :, bass.ds(j * 256 + half * HID // 2, 256)])], ada)
                        for n in range(KT):
                            load(lambda s: [(slot(s, YT, P), w2[:, YT * half:YT * (half + 1), n * P:(n + 1) * P])], 1)
                            total[0] += 1
                            if n in mods_after[half]:
                                load_mods(ada)
                else:
                    wide(w1, 0, HIDT // 2)
                    for n in range(KT):
                        for half in range(2):
                            load(lambda s: [(slot(s, YT, P), w2[:, YT * half:YT * (half + 1), n * P:(n + 1) * P])], 1)
                        total[0] += 1

            sp.wait_ge(out_ready, 4)
            sp.dma_start(out[0].rearrange("(t p) d -> p t d", p=P), view(big2, 0, LT, D)).then_inc(stored, 16)
            sp.wait_ge(stored, 16)

        @block.tensor
        def _(pe):
            c = Counts(pe)
            slab, tile, bank4, fences = [0], [0], [0], [0]

            def stage():
                pe.drain().then_inc(*c.made(fence))
                fences[0] += 1
                pe.wait_ge(fence, 4 * fences[0])

            def ring_wait(sem):
                _, v = c.need(sem)
                if c.i is not None or v > 0:
                    pe.wait_ge(sem, v)

            def ring_begin(sem):
                c.skip(sem, -4)

            def ring_end(sem):
                pe.wait_ge(*c.need(sem, 4))

            def bodies(n, body, work, per):
                turns = n // body
                if turns >= 2:
                    with c.loop(turns, per) as i:
                        for j in range(body):
                            work(j, i)
                    for j in range(n % body):
                        work(j, turns)
                else:
                    for j in range(n):
                        work(j, 0)

            def weights(k=16):
                s = slab[0] % SLOTS
                slab[0] += 1
                pe.wait_ge(*c.need(slot_loaded[s], k))
                return s

            mods = [0]

            def mod_slab():
                w = slot(weights(), KT, 256)
                b = 5 + mods[0] % 2
                for k in range(KT):
                    g = slice(32 * (k % 4), 32 * (k % 4) + 32)
                    mm = pe.matmul(PS[g, b, 0:256], cact[:, k, :], w[:, k, :], start=(k < 4), stop=(k >= 4))
                mm.then_inc(*c.made(mod_ready))
                n = mods[0] % (N_MOD // 2)
                mods[0] += 1
                if n or c.i is not None:
                    mod_columns(n - 1)

            def mod_columns(n):
                pe.wait_ge(*c.need(mod_copied))
                if n > 0:
                    pe.wait_ge(*c.need(mod_read))
                for m in range(2):
                    mm = pe.matmul(PS[:, 7, 2 * m:2 * m + 2], mod_rows[:, n % 2, m * P:(m + 1) * P], by_cond,
                                   start=True, stop=True)
                mm.then_inc(*c.made(mod_turned))

            def mods_end():
                mod_columns(N_MOD // 2 - 1)
                c.skip(mod_read)

            splits = [0]

            def split_weights(hi_at, lo_at, kt, width, k):
                s, n = slab[0] % SLOTS, splits[0]
                slab[0] += 1
                splits[0] += 1
                c.skip(slot_loaded[s], k)
                pe.wait_ge(*c.need(split_ready))
                return part_of_slab(hi_at, n, kt, width), part_of_slab(lo_at, n, kt, width) if lo_at else lo_slab(s, kt, width)

            def to_features(n, rhs, cols, freed, kt=KT, width=256, halves=1, loads=1, body=None, with_mods=(),
                            rest=None, hi_at=None, lo_at=None):
                ring_begin(freed)
                per_slab = width // P
                body = body or SLOTS * halves

                def work(j, i):
                    if rest:
                        w_hi, w_lo = split_weights(hi_at, lo_at, kt, width, 16 * loads)
                        passes = [(w_hi, rhs), (w_hi, rest), (w_lo, rhs)]
                    else:
                        passes = [(slot(weights(16 * loads), kt, width), rhs)]
                    half = j % halves
                    for m in range(per_slab):
                        b = tile[0] % 4
                        if half == 0:
                            ring_wait(freed)
                        for k in range(kt):
                            for n_pass, (w, x) in enumerate(passes):
                                mm = pe.matmul(PS[:, b, 0:cols], w[:, k, m * P:(m + 1) * P], x(half * kt + k),
                                               start=(half == 0 and k == 0 and n_pass == 0),
                                               stop=(half == halves - 1 and k == kt - 1 and n_pass == len(passes) - 1))
                        if half == halves - 1:
                            mm.then_inc(*c.made(tile_ready))
                            tile[0] += 1
                    if j in with_mods:
                        mod_slab()

                moved = body * per_slab // halves
                s0, kinds = slab[0], []
                for j in range(body):
                    kinds += [loads] + [1] * (j in with_mods)
                n_mods = len(kinds) - body
                assert len(kinds) % SLOTS == 0 or n // body < 2
                per = [(slot_loaded[(s0 + q) % SLOTS], 16 * sum(kinds[q::SLOTS])) for q in range(SLOTS)]
                per += [(tile_ready, moved), (freed, moved), (mod_ready, n_mods)]
                per += [(q, n_mods) for q in (mod_copied, mod_turned, mod_read)]
                bodies(n, body, work, per + [(split_ready, body)] * (rest is not None))
                if n // body >= 2:
                    mods[0] += n_mods * (n // body - 1)
                ring_end(freed)

            def to_tokens(n, width, n_tok, freed, parts=None, hi_at=None):
                ring_begin(freed)

                def work(j, i):
                    if parts:
                        w_hi, w_lo = split_weights(hi_at, None, KT, width, 16)
                        passes = [(parts[0], w_hi), (parts[0], w_lo), (parts[1], w_hi)]
                    else:
                        passes = [(hT, slot(weights(), KT, width))]
                    for t in range(n_tok):
                        b = tile[0] % 4
                        ring_wait(freed)
                        for k in range(KT):
                            for n_pass, (x, w) in enumerate(passes):
                                mm = pe.matmul(PS[:, b, 0:width], x[:, k, t * P:(t + 1) * P], w[:, k, :],
                                               start=(k == 0 and n_pass == 0),
                                               stop=(k == KT - 1 and n_pass == len(passes) - 1))
                        mm.then_inc(*c.made(tile_ready))
                        tile[0] += 1

                bodies(n, SLOTS, work, [(tile_ready, SLOTS * n_tok), (freed, SLOTS * n_tok)]
                       + [(q, 16) for q in slot_loaded] + [(split_ready, SLOTS)] * (parts is not None))
                ring_end(freed)

            def norm(cols):
                for k in range(KT):
                    pe.wait_ge(*c.need(squares))
                    mm = pe.matmul(PS[:, 4, 0:cols], ones, hT[:, k, 0:cols], start=(k == 0), stop=(k == KT - 1))
                mm.then_inc(*c.made(mean_sq))

            def turn_begin():
                c.skip(turned_freed, -4)

            def turn_end():
                pe.wait_ge(*c.need(turned_freed, 4))

            def turn(parts):
                b = 4 + bank4[0] % 4
                bank4[0] += 1
                ring_wait(turned_freed)
                for n, src in enumerate(parts):
                    mm = pe.transpose(PS[0:src.shape[1], b, n * P:n * P + src.shape[0]], src,
                                      ident[0:src.shape[0], 0:src.shape[0]])
                mm.then_inc(*c.made(turned))

            pe.wait_ge(const_loaded, 16)
            pe.wait_ge(x_loaded, 32)
            turn_begin()
            for k in range(KT):
                turn([xin[:, t, k * P:(k + 1) * P] for t in range(TT)])
            pe.wait_ge(vec_loaded, 16 * (len(pieces) + 8))
            n_left = [min(P, n_rows - n * P) for n in range(n_stage)]
            for b in range(-(-n_stage // 4)):
                turn([vstage[0:n_left[n], n, :] for n in range(4 * b, min(4 * b + 4, n_stage))])
            turn_end()
            stage()

            norm(SEQ)
            pe.wait_ge(*c.need(scaled, KT))
            lat = lambda k: hT[:, k, 0:SEQ]
            def head_squares(n):
                pe.wait_ge(*c.need(head_sq, 2))
                if n >= 4:
                    pe.wait_ge(*c.need(head_rms))
                pe.matmul(PS[:, 4 + n % 4, :], heads, sq1[:, 2 * n:2 * n + 2, :], start=True, stop=True)\
                    .then_inc(*c.made(head_ms))

            to_features(2, lat, SEQ, act_freed)
            to_features(1, lat, SEQ, act_freed, loads=4)
            to_tokens(1, 128, LT, act_freed)
            for n in range(3):
                head_squares(n)
            to_features(4, lat, SEQ, act_freed)
            head_squares(3)
            pe.wait_ge(tables_loaded, 16)
            pe.wait_ge(*c.need(head_normed, 6))
            for n in range(3):
                pe.matmul(PS[:, 4 + n, :], turn1, raw1[:, 2 * n:2 * n + 2, :], start=True, stop=True).then_inc(*c.made(rot_ready))
            to_tokens(1, 256, LT, act_freed)
            pe.wait_ge(*c.need(rot_done, 3))
            for n in range(4, 7):
                head_squares(n)
            to_tokens(1, 256, LT, act_freed)
            c.skip(head_rms, 4)

            def scores1(u):
                kind, hp, q = UNITS1[u]
                if u == UNITS1.index(("B", 0, 0)):
                    pe.wait_ge(*c.need(head_normed, 8))
                if u >= 3:
                    pe.wait_ge(*c.need(p_ready))
                for e in range(2):
                    r = slice(e * HD, (e + 1) * HD)
                    tq = hp if kind == "A" else 6 + hp
                    tk = 4 + hp // 2 if kind == "A" else 10 + hp
                    mm = pe.matmul(PS[:, 2 * (u % 3) + e, 0:SEQ], raw1[r, tq, q * P:(q + 1) * P], raw1[r, tk, :],
                                   start=True, stop=True)
                mm.then_inc(*c.made(s_ready))

            def turn_weights(u, n):
                pe.wait_ge(*c.need(a_ready))
                if u >= 1:
                    pe.wait_ge(*c.need(at_ready))
                for m in range(n):
                    mm = pe.transpose(PS[:, 6, m * P:(m + 1) * P], amat[:, u % 2, m * P:(m + 1) * P], ident)
                mm.then_inc(*c.made(t_ready))

            def outputs1(u):
                kind, hp, q = UNITS1[u]
                if u == n_u - 1:
                    pe.wait_ge(*c.need(at_ready))
                if u >= 1:
                    pe.wait_ge(*c.need(o_done))
                for e in range(2):
                    h = 2 * hp + e
                    v0 = HD * (h // 4) if kind == "A" else P + HD * h
                    for t in range(LT):
                        mm = pe.matmul(PS[:, 7, e * HD:(e + 1) * HD],
                                       amatT[:, u % 2, (e * LT + t) * P:(e * LT + t + 1) * P],
                                       v1[:, t, v0:v0 + HD], start=(t == 0), stop=(t == LT - 1))
                mm.then_inc(*c.made(o_ready))

            n_u = len(UNITS1)
            scores1(0)
            scores1(1)
            for u in range(n_u + 1):
                if u + 2 < n_u:
                    scores1(u + 2)
                if u < n_u:
                    turn_weights(u, 4)
                if u >= 1:
                    outputs1(u - 1)
            c.skip(p_ready, 3)
            pe.wait_ge(*c.need(o_done))
            pe.wait_ge(*c.need(tok_scaled, 2 * LT))
            turn_begin()
            for f in range(KT):
                turn([o1[:, t, f * P:(f + 1) * P] for t in range(LT)])
            turn_end()
            to_features(4, lambda k: mix1[:, k, :], SEQ, dve_freed)
            stage()
            norm(SEQ)
            pe.wait_ge(*c.need(cond_ready))
            for _ in range(2):
                mod_slab()
            pe.wait_ge(*c.need(lo_ready, KT))
            c.skip(scaled, KT)
            to_features(FFT, lambda k: hm_hi[1][:, k, :], SEQ, dve_freed, loads=2, body=2, with_mods=(0, 1),
                        rest=lambda k: hm_lo[:, k, 0:SEQ], hi_at=up_at, lo_at=up_rest_at)
            mods_end()
            splits[0] = 0
            pe.wait_ge(*c.need(conv_done, FFT))
            to_features(2 * KT, lambda k: ffn_hi[:, k, :], SEQ, dve_freed, kt=FFT // 2, width=P, halves=2,
                        rest=lambda k: ffn_lo[:, k, :], hi_at=down_at)
            stage()

            for l in range(LAYERS):
                norm(T)
                pe.wait_ge(*c.need(shifted, 2 * KT))
                c.skip(scaled, 2 * KT)
                n_half = 2 if l == 0 else 1
                q_cols = n_half * SEQ
                pe.wait_ge(*c.need(lo_ready, KT))
                in_parts = dict(rest=lambda k: h_lo[:, k, 0:q_cols], hi_at=mix_at[l])
                hi = lambda k: h_hi[:, k, 0:q_cols]
                to_features(4, hi, q_cols, act_freed, **in_parts)
                to_features(4, lambda k: h_hi[:, k, :], T, act_freed, rest=lambda k: h_lo[:, k, :], hi_at=mix_at[l])
                for n in range(2 * KT):
                    src = qT[l] if n < KT else kT
                    if n >= 4:
                        pe.wait_ge(*c.need(rot_done))
                    pe.matmul(PS[:, 4 + n % 4, 0:SEQ], turn2, src[:, n % KT, 0:SEQ], start=True, stop=True)\
                        .then_inc(*c.made(rot_ready))
                to_tokens(4, 256, TT, act_freed, parts=(h_hi, h_lo), hi_at=mix_at[l])
                to_features(4, hi, q_cols, act_freed, **in_parts)
                pe.wait_ge(*c.need(rot_done, 4))

                units = units2(l)

                def scores2(u):
                    h, q = units[u]
                    k0, nk = (0, T) if q < LT else (SEQ, SEQ)
                    if u >= 3:
                        pe.wait_ge(*c.need(p_ready, 2))
                    for e in range(2):
                        r = slice(e * HD, (e + 1) * HD)
                        mm = pe.matmul(PS[:, 2 * (u % 3) + e, 0:nk], qT[l][r, h, q * P:(q + 1) * P], kT[r, h, k0:k0 + nk],
                                       start=True, stop=True)
                    mm.then_inc(*c.made(s_ready))

                def outputs2(u):
                    h, q = units[u]
                    k0, nt = (0, TT) if q < LT else (LT, LT)
                    if u == n_u - 1:
                        pe.wait_ge(*c.need(at_ready))
                    if u >= 1:
                        pe.wait_ge(*c.need(o_done))
                    for n in range(nt):
                        mm = pe.matmul(PS[:, 7, 0:P], amatT[:, u % 2, n * P:(n + 1) * P],
                                       v2[:, k0 + n, h * P:(h + 1) * P], start=(n == 0), stop=(n == nt - 1))
                    mm.then_inc(*c.made(o_ready))

                n_u = len(units)
                scores2(0)
                scores2(1)
                for u in range(n_u + 1):
                    if u + 2 < n_u:
                        scores2(u + 2)
                    if u < n_u:
                        turn_weights(u, TT if units[u][1] < LT else LT)
                    if u >= 1:
                        outputs2(u - 1)
                c.skip(p_ready, 6)
                pe.wait_ge(*c.need(o_done))
                n_tok = len(y_chunks(l))
                pe.wait_ge(*c.need(tok_scaled, n_tok))
                turn_begin()
                for f in range(KT):
                    turn([o2[:, t, f * P:(f + 1) * P] for t in range(n_tok)])
                turn_end()
                to_features(4, lambda k: att_hi[l][:, k, :], q_cols, dve_freed, rest=lambda k: att_lo[l][:, k, :],
                            hi_at=mix_at[l])
                stage()

                to_tokens(1, 64, TT, dve_freed)
                pe.wait_ge(*c.need(dta_ready))
                for t in range(TT):
                    for m, lhs, r0, n in ((0, t_gt, 0, 32), (32, t_le, 0, 32), (64, t_lt, 32, 32), (96, t_ge, 32, 32),
                                          (128, ones, 0, 64)):
                        mm = pe.matmul(PS[:, t, m:m + n], lhs, dta[:, t, r0:r0 + n], start=True, stop=True)
                    mm.then_inc(*c.made(dec_ready))
                stage()

                ny = len(y_chunks(l))
                nz = ny // 2
                s0 = slab[0]

                freed_before = [1] * 6 if l == 0 else [2, 1, 0, 1, 1]
                c.skip(dve_freed, -3)
                pe.wait_ge(*c.need(lo_ready, KT))

                def product(n):
                    q = [0, 1, 2, 2, 3, 3][n]
                    s = (s0 + q) % SLOTS
                    if n not in (3, 5):
                        c.skip(slot_loaded[s], 32 if q == 2 else 16)
                        pe.wait_ge(*c.need(split_ready))
                    b = n % 3
                    if freed_before[n]:
                        pe.wait_ge(*c.need(dve_freed, freed_before[n]))
                    width = P if q < 2 else 256
                    w_hi, w_lo = view(R, group_hi(s, q), KT, width), lo_slab(s, KT, width)
                    if n < 4:
                        m = P if n == 3 else 0
                        for k in range(KT):
                            for w, x in ((w_hi, hs_hi), (w_hi, hs_lo), (w_lo, hs_hi)):
                                mm = pe.matmul(PS[:, b, :], w[:, k, m:m + P], x[:, k, :], start=(k == 0 and x is hs_hi and w is w_hi),
                                               stop=(k == KT - 1 and w is w_lo))
                    else:
                        for t in range(2):
                            t0 = (2 * (n - 4) + t) * P
                            for k in range(KT):
                                for w, x in ((w_hi, hs_hi), (w_hi, hs_lo), (w_lo, hs_hi)):
                                    mm = pe.matmul(PS[:, b, t * GW:(t + 1) * GW], x[:, k, t0:t0 + P], w[:, k, :],
                                                   start=(k == 0 and x is hs_hi and w is w_hi),
                                                   stop=(k == KT - 1 and w is w_lo))
                    mm.then_inc(*c.made(tile_ready))

                def turn_group(p, first):
                    pe.wait_ge(*c.need(chan_ready, 4))
                    if not first:
                        pe.wait_ge(*c.need(y_done))
                        pe.wait_ge(*c.need(e_ready, 2))
                    ch = chan[p]
                    for n in range(2):
                        for t in range(4):
                            mm = pe.transpose(PS[:, 3 + n, t * P:(t + 1) * P],
                                              ch[:, t % 2, (2 * n + t // 2) * P:(2 * n + t // 2 + 1) * P], ident)
                        mm.then_inc(*c.made(tok_turned))
                    for t in range(TT):
                        mm = pe.transpose(PS[:, 5, t * P:(t + 1) * P], ch[:, 2, t * P:(t + 1) * P], ident)
                    mm.then_inc(*c.made(tok_turned))
                    for t in range(ny):
                        mm = pe.matmul(PS[:, 6, t * P:(t + 1) * P], ch[:, 2, t * P:(t + 1) * P], ch[:, 3, t * P:(t + 1) * P],
                                       start=True, stop=True)
                    mm.then_inc(*c.made(cb_ready))

                def seg(t):
                    pe.wait_ge(*c.need(seg_in, 2))
                    if t == 1:
                        pe.wait_ge(*c.need(cb_masked))
                    if t >= 2:
                        pe.wait_ge(*c.need(e_ready))
                    for lhs, rhs in ((t_gt, seg_f), (t_lt, seg_b)):
                        mm = pe.matmul(PS[:, 7 - t % 2, :], lhs, rhs[:, t % 2, :, :].rearrange("p r l -> p (r l)"),
                                       start=lhs is t_gt, stop=lhs is t_lt)
                    mm.then_inc(*c.made(seg_ready))

                def states():
                    pe.wait_ge(*c.need(tok_ready, 3))
                    pe.wait_ge(*c.need(xw_ready, 6))
                    for n, t in enumerate(F_STATES + B_STATES):
                        mm = pe.matmul(PS[:, 3 + n // 2, (n % 2) * GW:(n % 2 + 1) * GW], btok[:, t, :], xw[:, n, :],
                                       start=True, stop=True)
                    mm.then_inc(*c.made(st_ready))

                def chunk(t, p):
                    pe.wait_ge(*c.need(m_ready))
                    if t == 0:
                        pe.wait_ge(*c.need(hin_ready))
                    else:
                        pe.wait_ge(*c.need(y_done))
                    for r in range(GH):
                        pe.matmul(PS[:, 3 + t % 2, r * HD:(r + 1) * HD], ex[:, t % 2, r * P:(r + 1) * P],
                                  xtok[:, t, r * HD:(r + 1) * HD], start=True, stop=True)
                    for d, hs in enumerate((HF, HB)):
                        if t in hs:
                            mm = pe.matmul(PS[:, 5, d * GW:(d + 1) * GW], chan[p][:, 3, t * P:(t + 1) * P],
                                           hin[:, hs[t], :], start=True, stop=True)
                    mm.then_inc(*c.made(y_ready))

                def turn_of(p, products=True, first=False):
                    turn_group(p, first)
                    if products:
                        product(0)
                    seg(0)
                    seg(1)
                    if products:
                        product(1)
                    states()
                    if products:
                        product(2)
                    for t in range(max(ny, 2)):
                        chunk(t, p)
                        if t + 2 < ny:
                            seg(t + 2)
                        if products and 3 + t < 4 + nz:
                            product(3 + t)

                for n in range(4 + nz):
                    product(n)
                turn_of(0, first=True)
                counted = [(tile_ready, 4 + nz), (dve_freed, 4 + nz), (chan_ready, 4), (tok_turned, 3),
                           (cb_ready, 1), (seg_in, 2 * ny), (cb_masked, 1), (seg_ready, ny), (tok_ready, 3),
                           (xw_ready, 6), (st_ready, 1), (m_ready, ny), (hin_ready, 1), (y_done, ny),
                           (y_ready, ny), (e_ready, ny), (split_ready, 4)]
                counted += [(slot_loaded[(s0 + q) % SLOTS], 32 if q == 2 else 16) for q in range(4)]
                with c.loop(GROUPS // 2 - 1, [(q, 2 * k) for q, k in counted]):
                    turn_of(1)
                    turn_of(0)
                turn_of(1, products=False)
                pe.wait_ge(*c.need(dve_freed, 3))
                pe.wait_ge(*c.need(e_ready, 2))
                pe.wait_ge(*c.need(y_done))
                slab[0] += 4 * GROUPS
                tile[0] += (4 + nz) * GROUPS
                stage()
                pe.wait_ge(*c.need(tok_scaled, ny))
                turn_begin()
                for f in range(YT):
                    turn([yg[:, t, f * P:(f + 1) * P] for t in range(ny)])
                turn_end()
                stage()
                to_features(4, lambda k: hs_hi[:, k, 0:q_cols], q_cols, act_freed, rest=lambda k: hs_lo[:, k, 0:q_cols],
                            hi_at=gate_at[l])
                to_features(KT, lambda k: y_hi[l][:, k, :], q_cols, dve_freed, kt=YT, width=P,
                            rest=lambda k: y_lo[l][:, k, :], hi_at=gate_at[l])
                pe.wait_ge(*c.need(lo_ready, KT))
                c.skip(gated, KT)
                to_features(4, lambda k: merged_hi[l][:, k, :], q_cols, dve_freed, rest=lambda k: merged_lo[l][:, k, :],
                            hi_at=gate_at[l])
                stage()
                norm(q_cols)
                if l == 0:
                    for _ in range(2):
                        mod_slab()
                pe.wait_ge(*c.need(lo_ready, n_half * KT))
                c.skip(scaled, n_half * KT)
                h_parts = dict(rest=lambda k: hm_lo[:, k, 0:q_cols], hi_at=mlp_at[l])
                hid_parts = dict(rest=lambda k: hid_lo[l][:, k, :], hi_at=mlp_at[l])
                h_of, hid_of = lambda k: hm_hi[l][:, k, :], lambda k: hid_hi[l][:, k, :]
                if l == 0:
                    for half in range(2):
                        to_features(HIDT // 4, h_of, T, dve_freed, body=2, with_mods=(0, 1), **h_parts)
                        pe.wait_ge(*c.need(lo_ready, YT))
                        to_features(KT, hid_of, T, dve_freed, kt=YT, width=P, body=KT, with_mods=mods_after[half], **hid_parts)
                    mods_end()
                else:
                    to_features(HIDT // 2, h_of, SEQ, dve_freed, **h_parts)
                    pe.wait_ge(*c.need(lo_ready, HIDT))
                    to_features(2 * KT, hid_of, SEQ, dve_freed, kt=YT, width=P, halves=2, **hid_parts)
                stage()

            norm(SEQ)
            pe.wait_ge(*c.need(scaled, KT))
            turn_begin()
            for t in range(LT):
                for b in range(2):
                    turn([hT[:, 4 * b + k, t * P:(t + 1) * P] for k in range(4)])

        @block.scalar
        def _(act):
            c = Counts(act)
            tile, bank4, fences = [0], [0], [0]

            for n, p0, m, src in pieces:
                act.dma_start(vstage[p0:p0 + m, n, :], src).then_inc(vec_loaded, 16)
            for name in ("qa_norm_g", "qb_norm_g", "ka_norm_g", "kb_norm_g"):
                r = rows[name]
                for e in range(2):
                    act.dma_start(vstage[r % P:r % P + 1, r // P, e * HD:(e + 1) * HD],
                                  a[name].rearrange("(a b) -> a b", a=1)).then_inc(vec_loaded, 16)
            def stage():
                act.drain().then_inc(*c.made(fence))
                fences[0] += 1
                act.wait_ge(fence, 4 * fences[0])

            def norm(cols):
                for k in range(KT):
                    act.activation(hT[:, k, 0:cols], xT[:, k, 0:cols], ACT.Square).then_inc(*c.made(squares))
                act.wait_ge(*c.need(mean_sq))
                act.activation(rms[:, 0:cols], PS[:, 4, 0:cols], ACT.Sqrt, scale=1.0 / D, bias=eps[:, 0:1])\
                    .then_inc(*c.made(rms_ready))

            def unload(dst, cols, func=ACT.Copy, scale=1.0):
                b = tile[0] % 4
                tile[0] += 1
                act.wait_ge(*c.need(tile_ready))
                act.activation(dst, PS[:, b:b + 1, 0:cols], func, scale=scale).then_inc(*c.made(act_freed))

            def unloads(n, dst, cols, func=ACT.Copy, scale=1.0):
                with c.loop(n // 4, [(tile_ready, 4), (act_freed, 4)]) as i:
                    for j in range(4):
                        unload(dst(i * 4 + j), cols, func, scale)

            def round_part(n, at, slab, size=SLAB):
                act.activation(view(R, at[n % len(at)], size), ring[:, slab % SLOTS, 0:size], ACT.Copy)\
                    .then_inc(*c.made(round_ready))

            def round_slab(slabs, n, at, size=SLAB):
                if n >= len(slabs):
                    return
                act.wait_ge(*slab_loaded[slabs[n]])
                if n >= len(at):
                    act.wait_ge(*slab_used[slabs[n - len(at)]])
                round_part(n, at, slabs[n], size)

            def passed(n):
                c.skip(tile_ready, n)
                tile[0] += n

            def turned_to(dst, n, gain=None, freed=turned_freed):
                b = 4 + bank4[0] % 4
                bank4[0] += 1
                act.wait_ge(*c.need(turned))
                if gain is None:
                    act.activation(dst, PS[:, b, 0:n], ACT.Copy).then_inc(*c.made(freed))
                else:
                    act.activation(dst, PS[:, b, 0:n], ACT.Copy, scale=gain).then_inc(*c.made(freed))

            act.wait_ge(*c.need(vec_ready))
            for k in range(KT):
                turned_to(xT[:, k, :], T)
            for b in range(-(-n_stage // 4)):
                turned_to(V[:, 512 * b:min(512 * (b + 1), n_rows)], min(512, n_rows - 512 * b))
            act.wait_ge(*c.sofar(turned_freed))
            act.wait_ge(*c.need(lam_sum))
            act.activation(lam_s[:, 4:8], lam_s[:, 0:4], ACT.Exp).then_inc(*c.made(lam_exp))
            act.wait_ge(small_loaded, 16 * 9 * LAYERS)
            act.activation(neg_a[:, :, :], head_in[:, :, 64:128], ACT.Exp).then_inc(*c.made(lam_exp))
            for e, name in enumerate(("c_2", "c_ctx_2")):
                act.activation(craw[:, :, e], V[:, rows[name]:rows[name] + KT], ACT.Copy).then_inc(*c.made(act_step))
            act.wait_ge(*c.sofar(act_step))
            act.activation(ctan[:, :, :], craw[:, :, :], ACT.Tanh, scale=0.5).then_inc(*c.made(cond_tanh))
            stage()

            norm(SEQ)
            c.skip(scaled, KT)
            def unload_head(j):
                b = tile[0] % 4
                tile[0] += 1
                act.wait_ge(*c.need(tile_ready))
                act.activation(sq1[:, j, :], PS[:, b, 0:SEQ], ACT.Square).then_inc(*c.made(head_sq))
                act.activation(raw1[:, j, :], PS[:, b, 0:SEQ], ACT.Copy).then_inc(*c.made(act_freed))

            def head_roots(n):
                act.wait_ge(*c.need(head_ms))
                act.activation(sq1[:, 2 * n:2 * n + 2, :], PS[:, 4 + n % 4, :].rearrange("p (a b) -> p a b", a=2), ACT.Sqrt,
                               scale=1.0 / HD, bias=eps[:, 0:1]).then_inc(*c.made(head_rms))

            for j in range(6):
                unload_head(j)
            for t in range(LT):
                unload(v1[:, t:t + 1, 0:P], P)
            for n in range(3):
                head_roots(n)
            for j in range(6, 14):
                unload_head(j)
            head_roots(3)
            for t in range(LT):
                unload(v1[:, t:t + 1, P:P + 256], 256)
            for n in range(4, 7):
                head_roots(n)
            for t in range(LT):
                unload(v1[:, t:t + 1, P + 256:P + 512], 256)

            def exp1(u):
                act.wait_ge(*c.need(max_ready))
                if u >= 2:
                    act.wait_ge(*c.need(a_ready))
                for e in range(2):
                    src = PS[:, 2 * (u % 3) + e, 0:SEQ] if UNITS1[u][0] == "A" else atmp[:, u % 2, e * SEQ:(e + 1) * SEQ]
                    ins = act.activation(prob[:, u % 2, e * SEQ:(e + 1) * SEQ], src, ACT.Exp,
                                         bias=stat[:, 2 * u + e:2 * u + e + 1], accum_out=stat[:, 64 + 2 * u + e:65 + 2 * u + e])
                    if e:
                        ins.then_inc(*c.made(p_ready))

            def weightsT(u, n):
                act.wait_ge(*c.need(t_ready))
                if u >= 2:
                    act.wait_ge(*c.need(o_ready))
                act.activation(amatT[:, u % 2, 0:n], PS[:, 6, 0:n], ACT.Copy).then_inc(*c.made(at_ready))

            n_u = len(UNITS1)
            for u in range(n_u + 1):
                if u < n_u:
                    exp1(u)
                if u >= 1:
                    weightsT(u - 1, 512)
            c.skip(a_ready, 2)
            c.skip(o_ready, 2)
            act.wait_ge(*c.need(o_done, n_u))
            for t in range(LT):
                for e in range(2):
                    act.activation(junk[:, 0:512], o1[:, t, e * 512:(e + 1) * 512], ACT.Square,
                                   accum_out=stat[:, 128 + 2 * t + e:129 + 2 * t + e]).then_inc(*c.made(act_step))
                    act.wait_ge(*c.sofar(act_step))
            act.activation(stat[:, 136:140], stat[:, 128:132], ACT.Sqrt, scale=1.0 / 512, bias=eps[:, 0:1])\
                .then_inc(*c.made(tok_rms))
            c.skip(tok_scaled, 2 * LT)
            for f in range(KT):
                turned_to(mix1[:, f, :], SEQ, col("outa_norm_g", f) if f < 4 else col("outb_norm_g", f - 4))
            passed(KT)
            stage()
            norm(SEQ)
            ups = range(first_slab["up"], first_slab["up"] + 2 * FFT, 2)
            downs = range(first_slab["down"], first_slab["down"] + 2 * KT)
            round_slab(ups, 0, up_at)
            for k in range(KT):
                act.wait_ge(*c.need(scaled))
                act.activation(hm_hi[1][:, k, :], hT[:, k, 0:SEQ], ACT.Copy).then_inc(*c.made(hi_ready))
            round_slab(ups, 1, up_at)
            c.skip(lo_ready, KT)
            c.skip(dve_freed, KT)
            tile0 = tile[0]

            def taps(j, at, ahead=None, first=False):
                for e in range(2):
                    b = (tile0 + 2 * j + e) % 4
                    act.wait_ge(*c.need(tile_ready))
                    if e == 0 and not first:
                        act.wait_ge(*c.need(conv_done))
                    act.activation(cv1[:, j, e, :], PS[:, b, 0:SEQ], ACT.Identity, scale=dcol("conv_w", 44 + 22 * e + j, at),
                                   bias=dcol("conv_b", 22 * e + j, at)).then_inc(*c.made(conv_mid))
                if ahead:
                    ahead()
                act.wait_ge(*c.need(dve_freed, 2))
                act.activation(cv1[:, 2 + j, 0, :], cv1[:, j, 0, :], ACT.Gelu_apprx_tanh).then_inc(*c.made(gate_act))

            for j in range(2):
                taps(j, 0, lambda: round_slab(ups, 2 + j, up_at), first=True)
            turns = FFT // 2 - 2
            with c.loop(turns, [(tile_ready, 4), (conv_mid, 4), (dve_freed, 4), (gate_act, 2), (conv_done, 2),
                                (round_ready, 2)]) as i:
                def round_later(j):
                    (loaded, now), (_, later) = (slab_loaded[ups[4 + j + n]] for n in (0, 2))
                    act.wait_ge(loaded, i * (later - now) + now)
                    round_part(j, up_at, ups[4 + j])

                for j in range(2):
                    taps(j, i * 2 + 2, lambda: round_later(j))
            for j in range(2):
                taps(j, 2 * turns + 2)
            down_words = FFT // 2 * P
            for n in range(len(downs)):
                round_slab(downs, n, down_at, down_words)
            c.skip(conv_done, 2)
            tile[0] += 2 * FFT
            passed(KT)
            c.skip(dve_freed, KT)
            stage()

            for l in range(LAYERS):
                halves = 2 if l == 0 else 1
                q_cols = halves * SEQ
                ny = len(y_chunks(l))
                norm(T)
                act.wait_ge(*c.need(mods_ready))
                s0 = first_slab["q", l]
                slabs = range(s0, s0 + 20)
                if l:
                    for n in range(2):
                        round_slab(slabs, n, mix_at[l])
                for k in range(KT):
                    for e in range(2):
                        act.wait_ge(*c.need(scaled))
                        h = hT[:, k, e * SEQ:(e + 1) * SEQ]
                        act.activation(h, h, ACT.Identity, bias=mod[:, k, e:e + 1]).then_inc(*c.made(shifted))
                    act.wait_ge(*c.sofar(shifted))
                    act.activation(h_hi[:, k, :], hT[:, k, :], ACT.Copy).then_inc(*c.made(hi_ready))
                if l == 0:
                    unloads(KT, lambda j: qT[l][:, bass.ds(j, 1), :], T, scale=HD ** -0.5)
                    unloads(KT, lambda j: kT[:, bass.ds(j, 1), :], T)
                    with c.loop(4, [(tile_ready, 4), (act_freed, 4)]) as i:
                        for t in range(TT):
                            unload(v2[:, t:t + 1, bass.ds(i * 256, 256)], 256)
                    unloads(KT, lambda j: merged[l][:, bass.ds(j, 1), :], T, ACT.Tanh, 0.5)
                else:
                    round_slab(slabs, 2, mix_at[l])
                    for j in range(KT):
                        unload(qT[l][:, j:j + 1, :], SEQ, scale=HD ** -0.5)
                        if j % 2:
                            round_slab(slabs, 3 + j // 2, mix_at[l])
                    for j in range(KT):
                        unload(kT[:, j:j + 1, :], T)
                        if j % 2:
                            round_slab(slabs, 7 + j // 2, mix_at[l])
                    for n in range(4):
                        for t in range(TT):
                            unload(v2[:, t:t + 1, n * 256:(n + 1) * 256], 256)
                        round_slab(slabs, 11 + n, mix_at[l])
                    round_slab(slabs, 15, mix_at[l])
                    for j in range(KT):
                        unload(merged[l][:, j:j + 1, :], SEQ, ACT.Tanh, 0.5)

                units = units2(l)

                def exp2(u):
                    h, q = units[u]
                    nk = T if q < LT else SEQ
                    act.wait_ge(*c.need(max_ready))
                    if u >= 2:
                        act.wait_ge(*c.need(a_ready))
                    for e in range(2):
                        act.activation(prob[:, u % 2, e * T:e * T + nk], PS[:, 2 * (u % 3) + e, 0:nk], ACT.Exp,
                                       bias=stat[:, 2 * u + e:2 * u + e + 1],
                                       accum_out=stat[:, 64 + 2 * u + e:65 + 2 * u + e]).then_inc(*c.made(p_ready))

                def sum_squares(u):
                    h, t = units[u]
                    act.wait_ge(*c.need(o_done))
                    act.wait_ge(*c.sofar(act_step))
                    act.activation(rms[:, 0:P], o2[:, t, h * P:(h + 1) * P], ACT.Square,
                                   accum_out=stat[:, 192 + t * HEADS + h:193 + t * HEADS + h]).then_inc(*c.made(act_step))

                n_u = len(units)
                for u in range(n_u + 4):
                    if u < n_u:
                        exp2(u)
                    if 1 <= u <= n_u:
                        weightsT(u - 1, T if units[u - 1][1] < LT else SEQ)
                    if u >= 4:
                        sum_squares(u - 4)
                act.wait_ge(*c.sofar(act_step))
                c.skip(a_ready, 2)
                c.skip(o_ready, 2)
                act.activation(stat[:, 224:224 + ny * HEADS], stat[:, 192:192 + ny * HEADS], ACT.Sqrt, scale=1.0 / P,
                               bias=eps[:, 0:1]).then_inc(*c.made(tok_rms))
                if l:
                    for n in range(16, 20):
                        round_slab(slabs, n, mix_at[l])
                c.skip(tok_scaled, ny)
                for f in range(KT):
                    turned_to(att_hi[l][:, f, :], q_cols, col("attn_subln_g_2", l), hi_ready)
                passed(KT)
                c.skip(dve_freed, KT)
                stage()

                act.dma_start(aside(merged_aside, q_cols), merged[l]).then_inc(*c.made(put_aside, 16))
                act.dma_start(aside(x_aside, q_cols), xT[:, :, 0:q_cols]).then_inc(*c.made(put_aside, 16))
                passed(TT)
                c.skip(dve_freed, TT)
                act.wait_ge(*c.need(dt_abs))
                act.activation(dtx[1][:, :, :], dtx[0][:, :, :], ACT.Abs).then_inc(*c.made(act_step))
                act.wait_ge(*c.sofar(act_step))
                act.activation(dtx[2][:, :, :], dtx[1][:, :, :], ACT.Exp, scale=-1.0).then_inc(*c.made(dt_exp))
                act.wait_ge(*c.need(dt_one))
                act.activation(dtx[4][:, :, :], dtx[3][:, :, :], ACT.Ln).then_inc(*c.made(dt_ln))
                for t in range(TT):
                    act.wait_ge(*c.need(dec_ready))
                    act.activation(edec[:, t, :], PS[:, t, 0:192], ACT.Exp)\
                        .then_inc(*c.made(dec_exp))
                act.wait_ge(*c.sofar(put_aside))
                for k in range(KT):
                    act.activation(hs_hi[:, k, :], hT[:, k, :], ACT.Copy).then_inc(*c.made(hi_ready))
                stage()

                nz = ny // 2
                cw = rows["conv_w_2"] + l * 160
                cb = rows["conv_b_2"] + l * 32

                c.skip(chan_ready, -2)

                def conv(g, p, j):
                    act.wait_ge(*c.need(tile_ready))
                    st, off = (2, j) if j < 2 else (1, 16 + 8 * (j - 2))
                    act.activation(chan[p][:, j, :], PS[:, j % 3, :], ACT.Identity, scale=V[:, bass.ds(g * st + (cw + 64 + off), 1)],
                                   bias=V[:, bass.ds(g * st + (cb + off), 1)]).then_inc(*c.made(conv_mid))
                    act.wait_ge(*c.need(dve_freed))
                    _, used = c.need(chan_ready)
                    if c.i is not None or used > 0:
                        act.wait_ge(chan_ready, used)
                    act.activation(ctanh[j % 2], chan[p][:, j, :], ACT.Tanh).then_inc(*c.made(conv_tanh))

                s0 = first_slab["ssd", l]

                def round_of_group(g, q):
                    s, words = (s0 + q) % SLOTS, SLAB // 2 if q < 2 else SLAB
                    loaded, at = slab_loaded[s0 + q]
                    act.wait_ge(loaded, g * (32 if q == 2 else 16) + at)
                    act.activation(view(R, group_hi(s, q), words), ring[:, s, 0:words], ACT.Copy).then_inc(*c.made(round_ready))

                def gate_of_z(p, b):
                    act.wait_ge(*c.need(tile_ready))
                    act.activation(sz[p][:, 2 * b:2 * b + 2, :], PS[:, (4 + b) % 3, :].rearrange("p (t n) -> p t n", t=2), ACT.Tanh,
                                   scale=0.5).then_inc(*c.made(z_tanh))

                def to_tok(first):
                    if not first:
                        act.wait_ge(*c.need(xd_ready, ny))
                    for n in range(2):
                        act.wait_ge(*c.need(tok_turned))
                        act.activation(xtok[:, 2 * n:2 * n + 2, :], PS[:, 3 + n, :].rearrange("p (t n) -> p t n", t=2), ACT.Copy)\
                            .then_inc(*c.made(tok_ready))
                    act.wait_ge(*c.need(tok_turned))
                    act.activation(btok[:, :, :], PS[:, 5, :].rearrange("p (t n) -> p t n", t=TT), ACT.Copy)\
                        .then_inc(*c.made(tok_ready))

                def decays(t):
                    act.wait_ge(*c.need(seg_ready))
                    if t >= 2:
                        act.wait_ge(*c.need(y_ready))
                    act.activation(ex[:, t % 2, :], PS[:, 7 - t % 2, :], ACT.Exp).then_inc(*c.made(e_ready))

                def squares_of(g):
                    for t in range(ny):
                        act.wait_ge(*c.need(y_done))
                        act.wait_ge(*c.sofar(act_step))
                        act.activation(squares_out, yg[:, t, bass.ds(g * GW, GW)], ACT.Square,
                                       accum_out=stat[:, bass.ds(g + (128 + t * GROUPS), 1)]).then_inc(*c.made(act_step))

                def turn_of(g, p, last=None, products=True, first=False):
                    if products:
                        round_of_group(g, 0)
                        round_of_group(g, 1)
                    for b in range(nz):
                        gate_of_z(p, b)
                    c.skip(dve_freed, nz)
                    to_tok(first)
                    if products:
                        round_of_group(g, 2)
                        conv(g, 1 - p, 0)
                    decays(0)
                    decays(1)
                    if not first:
                        squares_of(last)
                    for j in range(1, 4):
                        if products:
                            conv(g, 1 - p, j)
                            if j == 1:
                                round_of_group(g, 3)
                        if 2 <= j < ny:
                            decays(j)
                    c.skip(y_ready, 2)

                for q in range(4):
                    round_of_group(0, q)
                for j in range(4):
                    conv(0, 0, j)
                turn_of(1, 0, first=True)
                counted = [(y_done, ny), (act_step, ny), (round_ready, 4), (tile_ready, 4 + nz), (conv_mid, 4),
                           (dve_freed, 4 + nz), (chan_ready, 4), (conv_tanh, 4),
                           (z_tanh, nz), (tok_turned, 3), (tok_ready, 3),
                           (seg_ready, ny), (y_ready, ny), (xd_ready, ny), (e_ready, ny)]
                with c.loop(GROUPS // 2 - 1, [(q, 2 * k) for q, k in counted]) as i:
                    turn_of(i * 2 + 2, 1, i * 2)
                    turn_of(i * 2 + 3, 0, i * 2 + 1)
                turn_of(None, 1, GROUPS - 2, products=False)
                squares_of(GROUPS - 1)
                c.skip(chan_ready, 2)
                c.skip(xd_ready, ny)
                tile[0] += (4 + nz) * GROUPS
                stage()
                act.dma_start(xT[:, :, 0:q_cols], aside(x_aside, q_cols)).then_inc(*c.made(taken_back, 16))
                act.wait_ge(*c.need(y_summed))
                act.activation(stat[:, 160:160 + ny], stat[:, 168:168 + ny], ACT.Sqrt, scale=1.0 / SSD_IN, bias=eps[:, 0:1])\
                    .then_inc(*c.made(tok_rms))
                c.skip(tok_scaled, ny)
                for f in range(YT):
                    turned_to(y_hi[l][:, f, :], q_cols, col("ssd_norm_g_2", l * YT + f), hi_ready)
                stage()
                s0 = first_slab["gs", l]
                slabs = range(s0, s0 + 16)
                if l == 0:
                    unloads(KT, lambda j: gs[:, bass.ds(j, 1), :], T, ACT.Tanh, 0.5)
                else:
                    for n in range(3):
                        round_slab(slabs, n, gate_at[l])
                    for j in range(KT):
                        unload(gs[:, j:j + 1, 0:SEQ], SEQ, ACT.Tanh, 0.5)
                        if j % 2:
                            round_slab(slabs, 3 + j // 2, gate_at[l])
                act.dma_start(merged[l], aside(merged_aside, q_cols)).then_inc(*c.made(taken_back, 16))
                passed(KT)
                for k in range(KT):
                    if l:
                        round_slab(slabs, 7 + k, gate_at[l])
                    act.wait_ge(*c.need(gated))
                    act.activation(merged_hi[l][:, k, :], merged[l][:, k, :], ACT.Copy).then_inc(*c.made(hi_ready))
                if l:
                    round_slab(slabs, 15, gate_at[l])
                passed(KT)
                c.skip(dve_freed, 2 * KT)
                stage()
                norm(q_cols)
                s0 = first_slab["mlp", l]
                slabs = range(s0, s0 + HIDT)
                if l:
                    for n in range(2):
                        round_slab(slabs, n, mlp_at[l])
                for k in range(KT):
                    for e in range(halves):
                        r = slice(e * SEQ, (e + 1) * SEQ)
                        act.wait_ge(*c.need(scaled))
                        act.activation(hm_hi[l][:, k, r], hT[:, k, r], ACT.Identity, bias=mod[:, 24 + k, e:e + 1])\
                            .then_inc(*c.made(hi_ready))
                c.skip(lo_ready, 3 * KT + halves * KT)

                def square(n, i, first):
                    act.wait_ge(*c.need(dve_freed))
                    if not first:
                        act.wait_ge(*c.need(lo_ready))
                    act.activation(relu2[l][:, n % 2, :], relu[l][:, n % 2, :], ACT.Square).then_inc(*c.made(squared))
                    act.wait_ge(*c.sofar(squared))
                    act.activation(hid_hi[l][:, i, :], relu2[l][:, n % 2, :], ACT.Copy).then_inc(*c.made(hi_ready))

                if l == 0:
                    for half in range(2):
                        for n in range(YT):
                            square(n, n, n < 2)
                        c.skip(lo_ready, 2)
                        passed(YT + KT)
                        c.skip(dve_freed, KT)
                else:
                    round_slab(slabs, 2, mlp_at[l])
                    for n in range(HIDT):
                        square(n, n, n < 2)
                        if n % 2:
                            round_slab(slabs, 3 + n // 2, mlp_at[l])
                    for n in range(3 + HIDT // 2, HIDT):
                        round_slab(slabs, n, mlp_at[l])
                    c.skip(lo_ready, 2)
                    passed(HIDT + KT)
                    c.skip(dve_freed, KT)
                stage()

            norm(SEQ)
            c.skip(scaled, KT)
            res = view(big2, 0, LT, D)
            for t in range(LT):
                for b in range(2):
                    bk = 4 + bank4[0] % 4
                    bank4[0] += 1
                    act.wait_ge(*c.need(turned))
                    act.activation(res[:, t, 512 * b:512 * (b + 1)], PS[:, bk, :], ACT.Copy).then_inc(*c.made(out_ready))

        def act_total(l, n):
            return 20 + l * (8 + 8 + 16 + 16) + 32 + 8 * n

        @block.vector
        def _(dve):
            c = Counts(dve)
            tile, fences = [0], [0]

            def stage():
                dve.drain().then_inc(*c.made(fence))
                fences[0] += 1
                dve.wait_ge(fence, 4 * fences[0])

            def settle(sem=None):
                dve.wait_ge(*c.sofar(sem or dve_step))

            def step(ins):
                return ins.then_inc(*c.made(dve_step))

            def bc(ap, n, axis=2):
                return ap.unsqueeze(2).broadcast_to([P, ap.shape[1], n])

            def bc_mid(ap, n):
                return ap.unsqueeze(1).broadcast_to([P, n, ap.shape[1]])

            def norm(gain, cols):
                dve.wait_ge(*c.need(rms_ready))
                step(dve.reciprocal(rstd[:, 0:cols], rms[:, 0:cols]))
                settle()
                for k in range(KT):
                    for e in range(-(-cols // SEQ)):
                        r = slice(e * SEQ, (e + 1) * SEQ)
                        dve.scalar_tensor_tensor(out=hT[:, k, r], in0=xT[:, k, r], scalar=gain(k, e), in1=rstd[:, r],
                                                 op0=ALU.mult, op1=ALU.mult).then_inc(*c.made(scaled))

            def passed(n):
                c.skip(tile_ready, n)
                tile[0] += n

            def next_tile():
                b = tile[0] % 4
                tile[0] += 1
                dve.wait_ge(*c.need(tile_ready))
                return b

            bank4 = [KT + -(-n_stage // 4) + KT]

            def rest_of_turned(lo, hi, gain, n):
                b = 4 + bank4[0] % 4
                bank4[0] += 1
                dve.wait_ge(*c.need(hi_ready))
                dve.scalar_tensor_tensor(out=lo, in0=PS[:, b, 0:n], scalar=gain, in1=hi, op0=ALU.mult, op1=ALU.subtract)\
                    .then_inc(*c.made(turned_freed))

            def rest_of(lo, x, hi):
                dve.wait_ge(*c.need(hi_ready))
                dve.tensor_tensor(lo, x, hi, ALU.subtract).then_inc(*c.made(lo_ready))

            mods = [0]

            def copy_mods(j):
                n = mods[0] % (N_MOD // 2)
                mods[0] += 1
                dve.wait_ge(*c.need(mod_ready))
                dve.tensor_copy(mod_rows[:, n % 2, :], PS[:, 5 + n % 2, 0:256]).then_inc(*c.made(mod_copied))
                if n or c.i is not None:
                    copy_columns(j - 1)

            def copy_columns(j):
                dve.wait_ge(*c.need(mod_turned))
                dve.tensor_copy(mod_in[:, bass.ds(j * 2, 2), :], PS[:, 7, 0:4].rearrange("p (m e) -> p m e", e=2))\
                    .then_inc(*c.made(mod_read))

            dve.memset(eps[:, :], EPS).then_inc(*c.made(vec_ready))
            dve.wait_ge(small_loaded, 16 * 9 * LAYERS)
            for l in range(LAYERS):
                for n in range(2):
                    pr = view(big1, (2 * l + n) * HD, HD)
                    step(dve.tensor_tensor(pr, lam_in[:, l, 2 * n, :], lam_in[:, l, 2 * n + 1, :], ALU.mult))
                    settle()
                    ins = dve.reduce_sum(lam_s[:, 2 * l + n:2 * l + n + 1], pr, AX.X)
                    if l == LAYERS - 1 and n == 1:
                        ins.then_inc(*c.made(lam_sum))
                    else:
                        step(ins)
            dve.wait_ge(*c.need(lam_exp))
            step(dve.tensor_tensor(lam_s[:, 8:10], lam_s[:, 5:8:2], lam_s[:, 4:8:2], ALU.subtract))
            settle()
            for l in range(LAYERS):
                lam_init = 0.8 - 0.6 * float(np.exp(-0.3 * l))
                step(dve.tensor_scalar(neg_lam[:, l:l + 1], lam_s[:, 8 + l:9 + l], -lam_init, None, ALU.add))
            dve.wait_ge(*c.need(lam_exp))
            step(dve.tensor_scalar(neg_a[:, :, :], neg_a[:, :, :], -1.0, None, ALU.mult))
            dve.wait_ge(*c.need(cond_tanh))
            step(dve.scalar_tensor_tensor(out=craw[:, :, :], in0=ctan[:, :, :], scalar=1.0, in1=craw[:, :, :],
                                          op0=ALU.add, op1=ALU.mult))
            settle()
            step(dve.memset(cact[:, :, :], 0.0))
            settle()
            dve.tensor_scalar(cact[:, :, 0:2], craw[:, :, :], 0.5, None, ALU.mult).then_inc(*c.made(cond_ready))
            n_c2 = LAYERS * 6 * 32
            half_conv = V[:, rows["conv_w_2"]:rows["conv_w_2"] + n_c2]
            step(dve.tensor_scalar(half_conv, half_conv, 0.5, None, ALU.mult))
            q_gain = V[:, rows["qa_norm_g"]:rows["qa_norm_g"] + 2]
            step(dve.tensor_scalar(q_gain, q_gain, HD ** -0.5, None, ALU.mult))
            stage()

            norm(lambda k, e: col("norm1_g", k), SEQ)
            passed(20)
            gains = ["qa_norm_g"] * 4 + ["ka_norm_g"] * 2 + ["qb_norm_g"] * 4 + ["kb_norm_g"] * 4
            def norm_heads(n):
                dve.wait_ge(*c.need(head_rms))
                step(dve.reciprocal(sq1[:, 2 * n:2 * n + 2, :], sq1[:, 2 * n:2 * n + 2, :]))
                settle()
                for j in (2 * n, 2 * n + 1):
                    dve.scalar_tensor_tensor(out=raw1[:, j, :], in0=raw1[:, j, :], scalar=col(gains[j]), in1=sq1[:, j, :],
                                             op0=ALU.mult, op1=ALU.mult).then_inc(*c.made(head_normed))

            for n in range(3):
                norm_heads(n)
            settle(head_normed)
            dve.wait_ge(tables_loaded, 16)
            for n in range(3):
                dve.wait_ge(*c.need(rot_ready))
                t2 = rot1[:, n, :].rearrange("p (a b) -> p a b", a=2)
                src = raw1[:, 2 * n:2 * n + 2, :]
                step(dve.tensor_tensor(t2, PS[:, 4 + n, :].rearrange("p (a b) -> p a b", a=2), bc_mid(sin1, 2), ALU.mult))
                step(dve.tensor_tensor(src, src, bc_mid(cos1, 2), ALU.mult))
                settle()
                dve.tensor_tensor(src, src, t2, ALU.add).then_inc(*c.made(rot_done))
            for n in range(3, 7):
                norm_heads(n)

            n_u = len(UNITS1)

            def max1(u):
                kind, hp, q = UNITS1[u]
                dve.wait_ge(*c.need(s_ready))
                if kind == "A":
                    src = PS[:, 2 * (u % 3):2 * (u % 3) + 2, 0:SEQ]
                else:
                    for e in range(2):
                        slope = 2.0 ** -(2 * hp + e + 1)
                        if u - 2 >= 8 and e == 0:
                            dve.wait_ge(p_ready, u - 1)
                        step(dve.scalar_tensor_tensor(out=atmp[:, u % 2, e * SEQ:(e + 1) * SEQ], in0=far[q], scalar=slope,
                                                      in1=PS[:, 2 * (u % 3) + e, 0:SEQ], op0=ALU.mult, op1=ALU.add))
                    settle()
                    src = atmp[:, u % 2, :].rearrange("p (a b) -> p a b", a=2)
                dve.tensor_reduce(stat[:, 2 * u:2 * u + 2], src, AX.X, ALU.max, negate=True).then_inc(*c.made(max_ready))

            def weights1(u):
                kind, hp, q = UNITS1[u]
                dve.wait_ge(*c.need(p_ready))
                if u >= 2:
                    dve.wait_ge(*c.need(t_ready))
                src = prob[:, u % 2, 0:T]
                dst = amat[:, u % 2, :]
                rs = stat[:, 64 + 2 * u:66 + 2 * u]
                if kind == "A":
                    step(dve.reciprocal(stat[:, 160 + 2 * u:162 + 2 * u], rs))
                    dve.tensor_copy(dst, src).then_inc(*c.made(a_ready))
                else:
                    for e in range(2):
                        r = slice(e * SEQ, (e + 1) * SEQ)
                        ins = dve.scalar_tensor_tensor(out=dst[:, r], in0=src[:, r], scalar=1.0, in1=times_seen[q],
                                                       op0=ALU.mult, op1=ALU.mult, accum_out=rs[:, e:e + 1])
                        if e:
                            ins.then_inc(*c.made(a_ready))
                    settle(a_ready)
                    step(dve.reciprocal(stat[:, 160 + 2 * u:162 + 2 * u], rs))

            def out1(u):
                kind, hp, q = UNITS1[u]
                dve.wait_ge(*c.need(o_ready))
                c0 = (0 if kind == "A" else 512) + 2 * hp * HD
                dve.tensor_tensor(o1[:, q, c0:c0 + 2 * HD].rearrange("p (a b) -> p a b", a=2),
                                  PS[:, 7, 0:2 * HD].rearrange("p (a b) -> p a b", a=2),
                                  bc(stat[:, 160 + 2 * u:162 + 2 * u], HD), ALU.mult).then_inc(*c.made(o_done))

            for u in range(n_u + 2):
                if 1 <= u <= n_u:
                    weights1(u - 1)
                if u < n_u:
                    max1(u)
                if u >= 2:
                    settle()
                    out1(u - 2)
            c.skip(t_ready, 2)
            dve.wait_ge(*c.need(tok_rms))
            step(dve.reciprocal(stat[:, 144:148], stat[:, 136:140]))
            settle()
            settle(o_done)
            for t in range(LT):
                for e in range(2):
                    h = o1[:, t, e * 512:(e + 1) * 512]
                    dve.tensor_scalar(h, h, stat[:, 144 + 2 * t + e:145 + 2 * t + e], None, ALU.mult).then_inc(*c.made(tok_scaled))
            for k in range(KT):
                b = next_tile()
                dve.tensor_tensor(xT[:, k, 0:SEQ], xT[:, k, 0:SEQ], PS[:, b, 0:SEQ], ALU.add).then_inc(*c.made(dve_freed))
            stage()
            norm(lambda k, e: col("norm2_g", k), SEQ)
            for j in range(2):
                copy_mods(j)
            for k in range(KT):
                rest_of(hm_lo[:, k, 0:SEQ], hT[:, k, 0:SEQ], hm_hi[1][:, k, :])

            tile0 = tile[0]
            with c.loop(FFT // 2, [(tile_ready, 4), (conv_mid, 4), (dve_step, 8), (dve_freed, 4), (gate_act, 2), (conv_done, 2),
                                   (mod_ready, 2), (mod_copied, 2), (mod_turned, 2), (mod_read, 2)]) as i:
                for j in range(2):
                    for e in range(2):
                        b = (tile0 + 2 * j + e) % 4
                        dve.wait_ge(*c.need(conv_mid))
                        c.skip(tile_ready)
                        cv = cv1[:, j, e, :]
                        step(dve.scalar_tensor_tensor(out=cv[:, 1:SEQ], in0=PS[:, b, 0:SEQ - 1],
                                                      scalar=dcol("conv_w", 22 * e + j, i * 2), in1=cv[:, 1:SEQ],
                                                      op0=ALU.mult, op1=ALU.add))
                        settle()
                        dve.scalar_tensor_tensor(out=cv[:, 0:SEQ - 1], in0=PS[:, b, 1:SEQ],
                                                 scalar=dcol("conv_w", 88 + 22 * e + j, i * 2), in1=cv[:, 0:SEQ - 1],
                                                 op0=ALU.mult, op1=ALU.add).then_inc(*c.made(dve_freed))
                    dve.wait_ge(*c.need(gate_act))
                    settle(dve_freed)
                    n = bass.ds(i * 2 + j, 1)
                    step(dve.tensor_tensor(ffn_hi[:, n, :], cv1[:, 2 + j, 0:1, :], cv1[:, j, 1:2, :], ALU.mult))
                    step(dve.tensor_tensor(cv1[:, j, 0, :], cv1[:, 2 + j, 0, :], cv1[:, j, 1, :], ALU.mult))
                    settle()
                    dve.tensor_tensor(ffn_lo[:, n, :], cv1[:, j, 0:1, :], ffn_hi[:, n, :], ALU.subtract)\
                        .then_inc(*c.made(conv_done))
                    copy_mods(i * 2 + (2 + j))
            mods[0] = N_MOD // 2
            copy_columns(N_MOD // 2 - 1)
            tile[0] += 2 * FFT
            for k in range(KT):
                b = next_tile()
                dve.tensor_tensor(xT[:, k, 0:SEQ], xT[:, k, 0:SEQ], PS[:, b, 0:SEQ], ALU.add).then_inc(*c.made(dve_freed))
            stage()

            for l in range(LAYERS):
                halves = 2 if l == 0 else 1
                q_cols = halves * SEQ
                ny = len(y_chunks(l))
                settle(mod_read)
                ab = V[:, rows["ada_b_2"] + l * N_MOD:rows["ada_b_2"] + (l + 1) * N_MOD]
                step(dve.tensor_tensor(mod[:, :, :], mod_in[:, :, :], bc(ab, 2), ALU.add))
                settle()
                for dst, m0, name in ((amix, 8, "norm_mix_g_2"), (amlp, 32, "norm_mlp_g_2")):
                    g0 = rows[name] + l * KT
                    step(dve.scalar_tensor_tensor(out=dst[:, :, :], in0=mod[:, m0:m0 + KT, :], scalar=1.0, in1=bc(V[:, g0:g0 + KT], 2),
                                                  op0=ALU.add, op1=ALU.mult))
                dve.tensor_scalar(hgate[:, :, :], mod[:, 16:24, :], 0.5, None, ALU.mult).then_inc(*c.made(mods_ready))
                settle(mods_ready)
                norm(lambda k, e: amix[:, k, e:e + 1], T)
                for k in range(KT):
                    rest_of(h_lo[:, k, :], hT[:, k, :], h_hi[:, k, :])

                passed(8 + 8)
                for n in range(2 * KT):
                    h = (qT[l] if n < KT else kT)[:, n % KT, 0:SEQ]
                    dve.wait_ge(*c.need(rot_ready))
                    if n >= 2:
                        settle(rot_done)
                    step(dve.tensor_tensor(rot2[:, n % 2, :], PS[:, 4 + n % 4, 0:SEQ], sin2, ALU.mult))
                    step(dve.tensor_tensor(h, h, cos2, ALU.mult))
                    settle()
                    dve.tensor_tensor(h, h, rot2[:, n % 2, :], ALU.add).then_inc(*c.made(rot_done))
                passed(16 + 8)

                units = units2(l)
                n_u = len(units)

                def max2(u):
                    nk = T if units[u][1] < LT else SEQ
                    b = 2 * (u % 3)
                    dve.wait_ge(*c.need(s_ready))
                    dve.tensor_reduce(stat[:, 2 * u:2 * u + 2], PS[:, b:b + 2, 0:nk], AX.X, ALU.max, negate=True)\
                        .then_inc(*c.made(max_ready))

                def weights2(u):
                    nk = T if units[u][1] < LT else SEQ
                    dve.wait_ge(*c.need(p_ready, 2))
                    s0, s1 = (stat[:, 64 + 2 * u + e:65 + 2 * u + e] for e in range(2))
                    r0, r1 = (stat[:, 128 + 2 * u + e:129 + 2 * u + e] for e in range(2))
                    step(dve.reciprocal(stat[:, 128 + 2 * u:130 + 2 * u], stat[:, 64 + 2 * u:66 + 2 * u]))
                    settle()
                    step(dve.scalar_tensor_tensor(out=r1, in0=r1, scalar=neg_lam[:, l:l + 1], in1=s0, op0=ALU.mult, op1=ALU.mult))
                    settle()
                    if u >= 2:
                        dve.wait_ge(*c.need(t_ready))
                    dve.scalar_tensor_tensor(out=amat[:, u % 2, 0:nk], in0=prob[:, u % 2, T:T + nk], scalar=r1,
                                             in1=prob[:, u % 2, 0:nk], op0=ALU.mult, op1=ALU.add).then_inc(*c.made(a_ready))

                def out2(u):
                    h, q = units[u]
                    dve.wait_ge(*c.need(o_ready))
                    dve.tensor_scalar(o2[:, q, h * P:(h + 1) * P], PS[:, 7, 0:P], stat[:, 128 + 2 * u:129 + 2 * u], None,
                                      ALU.mult).then_inc(*c.made(o_done))

                for u in range(n_u + 2):
                    if 1 <= u <= n_u:
                        weights2(u - 1)
                    if u < n_u:
                        max2(u)
                    if u >= 2:
                        out2(u - 2)
                c.skip(t_ready, 2)
                dve.wait_ge(*c.need(tok_rms))
                lam_init = 0.8 - 0.6 * float(np.exp(-0.3 * l))
                n_st = ny * HEADS
                step(dve.reciprocal(stat[:, 192:192 + n_st], stat[:, 224:224 + n_st]))
                settle()
                step(dve.tensor_scalar(stat[:, 192:192 + n_st], stat[:, 192:192 + n_st], 1.0 - lam_init, None, ALU.mult))
                settle()
                settle(o_done)
                for t in range(ny):
                    h = o2[:, t, :].rearrange("p (h e) -> p h e", h=HEADS)
                    dve.tensor_tensor(h, h, bc(stat[:, 192 + t * HEADS:192 + (t + 1) * HEADS], P), ALU.mult)\
                        .then_inc(*c.made(tok_scaled))
                for f in range(KT):
                    rest_of_turned(att_lo[l][:, f, :], att_hi[l][:, f, :], col("attn_subln_g_2", l), q_cols)
                dve.wait_ge(act_freed, act_total(l, 1))
                with c.loop(2, [(tile_ready, 4), (dve_freed, 4)]) as i:
                    for j in range(4):
                        b = next_tile()
                        h = merged[l][:, bass.ds(i * 4 + j, 1), :]
                        dve.scalar_tensor_tensor(out=h, in0=h, scalar=1.0, in1=PS[:, b:b + 1, 0:q_cols], op0=ALU.add,
                                                 op1=ALU.mult).then_inc(*c.made(dve_freed))
                stage()

                for t in range(TT):
                    b = next_tile()
                    dve.tensor_tensor(dtx[0][:, t, :], PS[:, b, 0:64], head_in[:, l, 0:64], ALU.add).then_inc(*c.made(dve_freed))
                settle(dve_freed)
                dve.tensor_scalar(dt[:, :, :], dtx[0][:, :, :], 0.0, None, ALU.max).then_inc(*c.made(dt_abs))
                dve.wait_ge(*c.need(dt_exp))
                dve.tensor_scalar(dtx[3][:, :, :], dtx[2][:, :, :], 1.0, None, ALU.add).then_inc(*c.made(dt_one))
                settle(dt_one)
                step(dve.scalar_tensor_tensor(out=dtx[5][:, :, :], in0=dtx[3][:, :, :], scalar=-1.0, in1=dtx[2][:, :, :],
                                              op0=ALU.add, op1=ALU.subtract))
                step(dve.reciprocal(dtx[1][:, :, :], dtx[3][:, :, :]))
                settle()
                step(dve.tensor_tensor(dtx[5][:, :, :], dtx[5][:, :, :], dtx[1][:, :, :], ALU.mult))
                dve.wait_ge(*c.need(dt_ln))
                settle()
                step(dve.tensor_tensor(dtx[4][:, :, :], dtx[4][:, :, :], dtx[5][:, :, :], ALU.subtract))
                settle()
                step(dve.tensor_tensor(dt[:, :, :], dt[:, :, :], dtx[4][:, :, :], ALU.add))
                settle()
                dve.tensor_tensor(dta[:, :, :], dt[:, :, :], bc_mid(neg_a[:, l, :], TT), ALU.mult).then_inc(*c.made(dta_ready))
                for t in range(TT):
                    step(dve.tensor_copy(by_head[:, t, 192:224], head_in[:, l, 128:160]))
                dve.wait_ge(*c.need(dec_exp, TT))
                for e in range(2):
                    step(dve.tensor_tensor(wst[:, :, 32 * e:32 * e + 32], dt[:, :, 32 * e:32 * e + 32],
                                           edec[:, :, 64 * e:64 * e + 32], ALU.mult))
                for k in range(KT):
                    rest_of(hs_lo[:, k, :], hT[:, k, :], hs_hi[:, k, :])
                stage()

                nz = ny // 2
                cw = rows["conv_w_2"] + l * 160

                def heads_of(buf, t, c0, g, n=HD):
                    return buf[:, t, bass.ds(g * GH + c0, GH)].unsqueeze(2).broadcast_to([P, GH, n])

                def per_head(ap):
                    return ap.rearrange("p (r n) -> p r n", r=GH)

                def taps(g, p, j):
                    st, off = (2, j) if j < 2 else (1, 16 + 8 * (j - 2))
                    u = PS[:, j % 3, :].rearrange("p (s t) -> p s t", s=2)
                    cv = chan[p][:, j, :].rearrange("p (s t) -> p s t", s=2)
                    dve.wait_ge(*c.need(conv_mid))
                    c.skip(tile_ready)
                    for n, d in enumerate((-2, -1, 1, 2)):
                        to, fr = slice(max(0, -d), SEQ - max(0, d)), slice(max(0, d), SEQ - max(0, -d))
                        ins = dve.scalar_tensor_tensor(out=cv[:, :, to], in0=u[:, :, fr],
                                                       scalar=V[:, bass.ds(g * st + (cw + 32 * (d + 2) + off), 1)],
                                                       in1=cv[:, :, to], op0=ALU.mult, op1=ALU.add)
                        if n < 3:
                            step(ins)
                            settle()
                        else:
                            ins.then_inc(*c.made(dve_freed))

                def silu(p, j):
                    dve.wait_ge(*c.need(conv_tanh))
                    dve.scalar_tensor_tensor(out=chan[p][:, j, :], in0=ctanh[j % 2], scalar=1.0, in1=chan[p][:, j, :],
                                             op0=ALU.add, op1=ALU.mult).then_inc(*c.made(chan_ready))

                def gate_of_z(p, b):
                    dve.wait_ge(*c.need(z_tanh))
                    c.skip(tile_ready)
                    h = sz[p][:, 2 * b:2 * b + 2, :]
                    dve.scalar_tensor_tensor(out=h, in0=h, scalar=1.0, in1=PS[:, (4 + b) % 3, :].rearrange("p (t n) -> p t n", t=2),
                                             op0=ALU.add, op1=ALU.mult).then_inc(*c.made(dve_freed))

                def masks():
                    dve.wait_ge(*c.need(cb_ready))
                    cbp = PS[:, 6, 0:ny * P].rearrange("p (t l) -> p t l", t=ny)
                    step(dve.tensor_tensor(cb_lo[:, 0:ny, :], cbp, bc_mid(t_le, ny), ALU.mult))
                    dve.tensor_tensor(cb_up[:, 0:ny, :], cbp, bc_mid(t_ge, ny), ALU.mult).then_inc(*c.made(cb_masked))
                    settle(cb_masked)

                def weights(g, t):
                    lo = dt_lo[:, :, :]
                    step(dve.tensor_tensor(lo, bc_mid(cb_lo[:, t, :], GH), heads_of(dt, t, 0, g, P), ALU.mult))
                    dve.wait_ge(*c.need(dtu_ready))
                    settle()
                    step(dve.tensor_tensor(per_head(dt_up[:, t % 2, :]), lo, per_head(dt_up[:, t % 2, :]), ALU.add))
                    dve.wait_ge(*c.need(e_ready))
                    settle()
                    dve.tensor_tensor(ex[:, t % 2, :], dt_up[:, t % 2, :], ex[:, t % 2, :], ALU.mult).then_inc(*c.made(m_ready))

                def starts(g):
                    dve.wait_ge(*c.need(st_ready))
                    st = [PS[:, 3 + n // 2, (n % 2) * GW:(n % 2 + 1) * GW] for n in range(6)]
                    for d in range(2):
                        step(dve.tensor_copy(hin[:, 3 * d, :], st[3 * d]))
                    for n in range(1, 3):
                        settle()
                        for d, order in enumerate((F_STATES, B_STATES)):
                            step(dve.tensor_tensor(per_head(hin[:, 3 * d + n, :]), per_head(hin[:, 3 * d + n - 1, :]),
                                                   heads_of(edec, order[n], 128 + 32 * d, g), ALU.mult))
                        settle()
                        for d in range(2):
                            h = hin[:, 3 * d + n, :]
                            ins = dve.tensor_tensor(h, h, st[3 * d + n], ALU.add)
                            if n == 2 and d == 1:
                                ins.then_inc(*c.made(hin_ready))
                            else:
                                step(ins)

                def outputs(g, p, t):
                    dve.wait_ge(*c.need(y_ready))
                    dve.wait_ge(*c.need(xd_ready))
                    step(dve.tensor_tensor(ys, PS[:, 3 + t % 2, 0:GW], xd[:, t % 2, :], ALU.add))
                    for d, hs in enumerate((HF, HB)):
                        if t in hs:
                            step(dve.tensor_tensor(per_head(yi), per_head(PS[:, 5, d * GW:(d + 1) * GW]),
                                                   heads_of(edec, t, 32 + 64 * d, g), ALU.mult))
                            settle()
                            step(dve.tensor_tensor(ys, ys, yi, ALU.add))
                            settle()
                    dve.scalar_tensor_tensor(out=yg[:, t, bass.ds(g * GW, GW)], in0=ys, scalar=0.5, in1=sz[p][:, t, :],
                                             op0=ALU.mult, op1=ALU.mult).then_inc(*c.made(y_done))
                    settle(y_done)

                def turn_of(g, p, products=True):
                    nxt = g + 1
                    masks()
                    if products:
                        taps(nxt, 1 - p, 0)
                    weights(g, 0)
                    if products:
                        silu(1 - p, 0)
                    weights(g, 1)
                    if products:
                        taps(nxt, 1 - p, 1)
                    starts(g)
                    if products:
                        silu(1 - p, 1)
                        taps(nxt, 1 - p, 2)
                    for t in range(max(2, ny)):
                        outputs(g, p, t)
                        if products and t < 2:
                            silu(1 - p, 2 + t)
                        if t + 2 < ny:
                            weights(g, t + 2)
                        if products and t == 0:
                            taps(nxt, 1 - p, 3)
                        if products and 1 <= t <= nz:
                            gate_of_z(1 - p, t - 1)

                for j in range(4):
                    taps(0, 0, j)
                    silu(0, j)
                for b in range(nz):
                    gate_of_z(0, b)
                turn_of(0, 0)
                n_steps = 4 * 3 + 1 + 2 * ny + 2 + 7 + sum(1 + 2 * ((t in HF) + (t in HB)) for t in range(ny))
                counted = [(tile_ready, 4 + nz), (conv_mid, 4), (dve_step, n_steps), (dve_freed, 4 + nz),
                           (conv_tanh, 4), (chan_ready, 4), (z_tanh, nz), (cb_ready, 1), (cb_masked, 1),
                           (dtu_ready, ny), (e_ready, ny), (m_ready, ny), (st_ready, 1), (hin_ready, 1),
                           (y_ready, ny), (xd_ready, ny), (y_done, ny)]
                with c.loop(GROUPS // 2 - 1, [(q, 2 * k) for q, k in counted]) as i:
                    turn_of(i * 2 + 1, 1)
                    turn_of(i * 2 + 2, 0)
                turn_of(GROUPS - 1, 1, products=False)
                tile[0] += (4 + nz) * GROUPS
                stage()
                dve.reduce_sum(stat[:, 168:168 + ny], stat[:, 128:128 + ny * GROUPS].rearrange("p (t g) -> p t g", t=ny), AX.X)\
                    .then_inc(*c.made(y_summed))
                dve.wait_ge(*c.need(tok_rms))
                step(dve.reciprocal(stat[:, 192:192 + ny], stat[:, 160:160 + ny]))
                settle()
                for t in range(ny):
                    dve.tensor_scalar(yg[:, t, :], yg[:, t, :], stat[:, 192 + t:193 + t], None, ALU.mult).then_inc(*c.made(tok_scaled))
                for f in range(YT):
                    rest_of_turned(y_lo[l][:, f, :], y_hi[l][:, f, :], col("ssd_norm_g_2", l * YT + f), q_cols)
                stage()

                passed(KT)
                dve.wait_ge(act_freed, act_total(l, 2))
                dve.wait_ge(*c.need(taken_back, 32))
                settle(dve_freed)
                for k in range(KT):
                    b = next_tile()
                    g = gs[:, k, 0:q_cols]
                    m = merged[l][:, k, :]
                    dve.scalar_tensor_tensor(out=g, in0=g, scalar=1.0, in1=PS[:, b, 0:q_cols], op0=ALU.add, op1=ALU.mult)\
                        .then_inc(*c.made(dve_freed))
                    settle(dve_freed)
                    dve.tensor_tensor(m, m, g, ALU.add).then_inc(*c.made(gated))
                    for done in range(k - 1, k if k < KT - 1 else KT):
                        if done >= 0:
                            rest_of(merged_lo[l][:, done, :], merged[l][:, done, :], merged_hi[l][:, done, :])

                next_mods = iter(range(N_MOD // 2))

                def add_gated(gate_of, with_mods=()):
                    for k in range(KT):
                        b = next_tile()
                        for e in range(halves):
                            r = slice(e * SEQ, (e + 1) * SEQ)
                            ins = dve.scalar_tensor_tensor(out=xT[:, k, r], in0=PS[:, b, r], scalar=gate_of(k, e), in1=xT[:, k, r],
                                                           op0=ALU.mult, op1=ALU.add)
                            if e == halves - 1:
                                ins.then_inc(*c.made(dve_freed))
                        if k in with_mods:
                            copy_mods(next(next_mods))

                add_gated(lambda k, e: hgate[:, k, e:e + 1])
                stage()
                norm(lambda k, e: amlp[:, k, e:e + 1], q_cols)
                if l == 0:
                    for _ in range(2):
                        copy_mods(next(next_mods))
                for k in range(KT):
                    for e in range(halves):
                        r = slice(e * SEQ, (e + 1) * SEQ)
                        dve.wait_ge(*c.need(hi_ready))
                        dve.scalar_tensor_tensor(out=hm_lo[:, k, r], in0=hT[:, k, r], scalar=mod[:, 24 + k, e:e + 1],
                                                 in1=hm_hi[l][:, k, r], op0=ALU.add, op1=ALU.subtract)\
                            .then_inc(*c.made(lo_ready))

                def hidden(n):
                    b = next_tile()
                    dve.tensor_scalar(relu[l][:, n % 2, :], PS[:, b, 0:q_cols], 0.0, None, ALU.max).then_inc(*c.made(dve_freed))
                    if l == 0 and n % 2:
                        copy_mods(next(next_mods))
                    rest_of(hid_lo[l][:, n, :], relu2[l][:, n % 2, :], hid_hi[l][:, n, :])

                if l == 0:
                    for half in range(2):
                        for n in range(YT):
                            hidden(n)
                        add_gated(lambda k, e: mod[:, 40 + k, e:e + 1], mods_after[half])
                        settle(dve_freed)
                    copy_columns(N_MOD // 2 - 1)
                else:
                    for n in range(HIDT):
                        hidden(n)
                    add_gated(lambda k, e: mod[:, 40 + k, e:e + 1])
                stage()

            norm(lambda k, e: col("final_norm_g_2", k), SEQ)

        @block.gpsimd
        def _(pool):
            c = Counts(pool)
            fences = [0]

            def stage():
                pool.drain().then_inc(*c.made(fence))
                fences[0] += 1
                pool.wait_ge(fence, 4 * fences[0])

            def bc_mid(ap, n):
                return ap.unsqueeze(1).broadcast_to([P, n, ap.shape[1]])

            def heads_of(t, kind, n):
                return of_group[:, t, kind, :].unsqueeze(2).broadcast_to([P, GH, n])

            def per_head(ap):
                return ap.rearrange("p (r n) -> p r n", r=GH)

            for l in range(LAYERS):
                for n, name in enumerate(("lambda_q1_2", "lambda_k1_2", "lambda_q2_2", "lambda_k2_2")):
                    pool.dma_start(lam_in[:, l, n, :], a[name][l:l + 1, :].broadcast_to([P, HD])).then_inc(small_loaded, 16)
                for n, name in enumerate(("dt_bias_f_2", "dt_bias_b_2", "a_log_f_2", "a_log_b_2", "ssd_d_2")):
                    pool.dma_start(head_in[:, l, n * 32:(n + 1) * 32], a[name][l:l + 1, :].broadcast_to([P, 32]))\
                        .then_inc(small_loaded, 16)

            split_slabs = []

            def rests(slabs, at, body=SLOTS, size=SLAB, lo_at=None):
                with c.loop(len(slabs) // body, [(round_ready, body), (split_ready, body)]):
                    for q in range(body):
                        s = slabs[q] % SLOTS
                        pool.wait_ge(*c.need(round_ready))
                        lo = lo_at[q] if lo_at else AT["ring"] + s * SLAB
                        pool.tensor_tensor(view(R, lo, size), ring[:, s, 0:size],
                                           view(R, at[q % len(at)], size), ALU.subtract).then_inc(*c.made(split_ready))

            def split(slabs, hi_at):
                def one(q, i, slope, free_slope):
                    s, n = slabs[q] % SLOTS, len(split_slabs)
                    loaded, at = slab_loaded[slabs[q]]
                    pool.wait_ge(loaded, i * slope + at)
                    if n >= 2:
                        freed, at = slab_used[split_slabs[n - 2]]
                        pool.wait_ge(freed, i * free_slope + at)
                    raw, hi, lo = ring[:, s, :], view(R, hi_at[n % 2], SLAB), view(R, AT["ring"] + s * SLAB, SLAB)
                    pool.tensor_tensor(hi, raw, ones[:, 0:1].broadcast_to([P, SLAB]), ALU.mult).then_inc(*c.made(pool_step))
                    pool.wait_ge(*c.sofar(pool_step))
                    pool.tensor_tensor(lo, raw, hi, ALU.subtract).then_inc(*c.made(split_ready))
                    split_slabs.append(slabs[q])

                body, turns = 4, len(slabs) // 4
                for q in range(body):
                    one(q, 0, 0, 0)
                if turns >= 2:
                    moved = [(slab_loaded[slabs[q + body]][1] - slab_loaded[slabs[q]][1],
                              slab_used[slabs[q + body]][1] - slab_used[slabs[q]][1]) for q in range(body)]
                    with c.loop(turns - 1, [(pool_step, body), (split_ready, body)]) as i:
                        for q in range(body):
                            one(body + q, i, *moved[q])
                    split_slabs.extend(slabs[2 * body:])

            stage()
            stage()
            rests(range(first_slab["up"], first_slab["up"] + 2 * FFT, 2), up_at, body=2, lo_at=up_rest_at)
            rests(range(first_slab["down"], first_slab["down"] + 2 * KT), down_at, size=FFT // 2 * P)
            stage()
            c.skip(o_done, len(UNITS1))
            for l in range(LAYERS):
                ny = len(y_chunks(l))
                if l == 0:
                    s0 = first_slab["q", l]
                    split(range(s0, s0 + 8), mix_at[l])
                    split(range(s0 + 8, s0 + 12), mix_at[l])
                    split(range(s0 + 12, s0 + 16), mix_at[l])
                    pool.wait_ge(*c.need(o_done, len(units2(l))))
                    split(range(s0 + 16, s0 + 20), mix_at[l])
                else:
                    s0 = first_slab["q", l]
                    rests(range(s0, s0 + 20), mix_at[l])
                stage()
                stage()

                s0 = first_slab["ssd", l]

                def rest_of_group(q):
                    s, words = (s0 + q) % SLOTS, SLAB // 2 if q < 2 else SLAB
                    pool.wait_ge(*c.need(round_ready))
                    pool.tensor_tensor(view(R, AT["ring"] + s * SLAB, words), ring[:, s, 0:words],
                                       view(R, group_hi(s, q), words), ALU.subtract).then_inc(*c.made(split_ready))

                def group(g, first=False, products=True):
                    if products:
                        rest_of_group(0)
                        rest_of_group(1)
                    pool.tensor_copy(of_group[:, :, :, :].rearrange("p t k r -> p (t k) r"),
                                     by_head[:, :, :].rearrange("p t (k n) -> p (t k) n", k=7)[:, :, bass.ds(g * GH, GH)])\
                        .then_inc(*c.made(pool_step))
                    pool.wait_ge(*c.sofar(pool_step))

                    def seg(t):
                        if t >= 2 or not first:
                            pool.wait_ge(*c.need(seg_ready))
                        pool.tensor_tensor(seg_f[:, t % 2, :, :], bc_mid(t_le, GH), heads_of(t, 2, P), ALU.mult)\
                            .then_inc(*c.made(seg_in))
                        pool.tensor_tensor(seg_b[:, t % 2, :, :], bc_mid(t_ge, GH), heads_of(t, 3, P), ALU.mult)\
                            .then_inc(*c.made(seg_in))

                    def dtu(t):
                        if t >= 2:
                            pool.wait_ge(*c.need(m_ready))
                        pool.tensor_tensor(per_head(dt_up[:, t % 2, :]), bc_mid(cb_up[:, t, :], GH), heads_of(t, 1, P),
                                           ALU.mult).then_inc(*c.made(dtu_ready))

                    def skip_of(t):
                        if t >= 2:
                            pool.wait_ge(*c.need(y_done))
                        pool.tensor_tensor(per_head(xd[:, t % 2, :]), per_head(xtok[:, t, :]),
                                           heads_of(t, 6, HD),
                                           ALU.mult).then_inc(*c.made(xd_ready))

                    seg(0)
                    seg(1)
                    pool.wait_ge(*c.need(tok_ready, 3))
                    for n, t in enumerate(F_STATES + B_STATES):
                        pool.tensor_tensor(per_head(xw[:, n, :]), per_head(xtok[:, t, :]), heads_of(t, 4 + n // 3, HD),
                                           ALU.mult).then_inc(*c.made(xw_ready))
                    pool.wait_ge(*c.need(cb_masked))
                    dtu(0)
                    dtu(1)
                    if products:
                        rest_of_group(2)
                    for t in range(2, ny):
                        seg(t)
                    skip_of(0)
                    skip_of(1)
                    if products:
                        rest_of_group(3)
                    for t in range(2, ny):
                        dtu(t)
                        skip_of(t)
                    c.skip(m_ready, 2)
                    c.skip(y_done, 2)
                    pool.wait_ge(*c.sofar(xd_ready))

                for q in range(4):
                    rest_of_group(q)
                group(0, first=True)
                with c.loop(GROUPS - 2, [(round_ready, 4), (split_ready, 4), (pool_step, 1), (seg_in, 2 * ny),
                                         (tok_ready, 3), (xw_ready, 6), (cb_masked, 1),
                                         (dtu_ready, ny), (xd_ready, ny), (seg_ready, ny), (m_ready, ny), (y_done, ny)]) as i:
                    group(i + 1)
                group(GROUPS - 1, products=False)
                c.skip(seg_ready, 2)
                stage()
                stage()
                if l == 0:
                    s0 = first_slab["gs", l]
                    split(range(s0, s0 + 4), gate_at[l])
                    split(range(s0 + 4, s0 + 4 + KT), gate_at[l])
                    split(range(s0 + 4 + KT, s0 + 8 + KT), gate_at[l])
                else:
                    s0 = first_slab["gs", l]
                    rests(range(s0, s0 + 8 + KT), gate_at[l])
                stage()
                if l == 0:
                    s0 = first_slab["mlp", l] + 2
                    for half in range(2):
                        split(range(s0, s0 + 16, 2), mlp_at[l])
                        s0 += 16
                        split([s0 + q + sum(n < q for n in mods_after[half]) for q in range(KT)], mlp_at[l])
                        s0 += 12
                else:
                    s0 = first_slab["mlp", l]
                    rests(range(s0, s0 + HIDT), mlp_at[l])
                stage()


_INS = [
    "x", "norm1_g", "w_in", "qa_norm_g", "ka_norm_g", "qb_norm_g", "kb_norm_g", "outa_norm_g", "outb_norm_g",
    "w_out", "norm2_g", "w_up", "conv_w", "conv_b", "w_down", "c_2", "ctx_2", "c_ctx_2", "ada_w_2", "ada_b_2",
    "norm_mix_g_2", "w_in_2", "conv_w_2", "conv_b_2", "dt_bias_f_2", "dt_bias_b_2", "a_log_f_2", "a_log_b_2",
    "ssd_d_2", "ssd_norm_g_2", "lambda_q1_2", "lambda_k1_2", "lambda_q2_2", "lambda_k2_2", "attn_subln_g_2",
    "w_attn_o_2", "w_ssd_o_2", "w_out_2", "norm_mlp_g_2", "w_mlp1_2", "w_mlp2_2", "final_norm_g_2",
]
_OUT = (1, SEQ, D)


def kernel(**inputs):
    import concourse.bacc as _bacc
    from concourse.bass_utils import run_bass_kernel_spmd as _run

    nc = _bacc.Bacc("TRN2", target_bir_lowering=False, num_devices=1)
    arrays, aps = {}, {}
    for name in _INS:
        arr = np.ascontiguousarray(inputs[name])
        arrays[f"in_{name}_dram"] = arr
        aps[name] = nc.dram_tensor(f"in_{name}_dram", arr.shape, mybir.dt.from_np(arr.dtype), kind="ExternalInput").ap()
    table = shape_constants()
    arrays["in_shape_constants_dram"] = table
    const = nc.dram_tensor("in_shape_constants_dram", table.shape, F32, kind="ExternalInput").ap()
    out = nc.dram_tensor("out_0_dram", _OUT, F32, kind="ExternalOutput").ap()
    two_blocks(nc, aps, const, out)
    r = _run(nc, [arrays], core_ids=[0])
    return r.results[0]["out_0_dram"]
```
